# Optimizing a Trainium2 kernel written in Bass

```python
import math
import jax, jax.numpy as jnp
from jax import lax
import numpy as np

D_MODEL = 1024
BATCH = 1
SEQ = 1024
DEPTH = 1

DA_HEADS = 4
DA_HALF = 64
DA_VDIM = 2 * DA_HALF
DA_WIDTH = DA_HEADS * DA_VDIM
ROPE_THETA = 500000.0
ROPE_DIM = DA_HALF // 4
QBLK = 128
RET_HEADS = 4
RET_KDIM = 128
RET_VDIM = 128
RET_WIDTH = RET_HEADS * RET_VDIM
RET_THETA = 10000.0
RCHUNK = 128
SPLIT_SIZES = [DA_WIDTH, DA_WIDTH, DA_WIDTH,
               RET_HEADS * RET_KDIM, RET_HEADS * RET_KDIM, RET_WIDTH, RET_WIDTH,
               D_MODEL, D_MODEL]
IN_COLS = sum(SPLIT_SIZES)
N_GROUPS = 4
EXPERTS_PER_GROUP = 8
N_EXPERTS = N_GROUPS * EXPERTS_PER_GROUP
TOP_K = 2
EXPERT_FF = 512
MOE_BLOCK = 128
EPS = 1e-6

kernel_name = "hybrid_diffattn_retention_hiermoe"

def rms_norm(x, g):
    xf = x.astype(jnp.float32)
    y = xf * lax.rsqrt(jnp.mean(xf * xf, axis=-1, keepdims=True) + EPS)
    return (y * g.astype(jnp.float32)).astype(x.dtype)

def apply_rope(x, positions, rot_dim, theta):
    half = rot_dim // 2
    freqs = jnp.power(jnp.float32(theta), -2.0 * jnp.arange(half, dtype=jnp.float32) / rot_dim)
    ang = positions.astype(jnp.float32)[..., None] * freqs
    ang = ang.reshape(ang.shape[:2] + (1,) * (x.ndim - 3) + (half,))
    cos, sin = jnp.cos(ang), jnp.sin(ang)
    xf = x.astype(jnp.float32)
    x1, x2, rest = xf[..., :half], xf[..., half:rot_dim], xf[..., rot_dim:]
    out = jnp.concatenate([x1 * cos - x2 * sin, x2 * cos + x1 * sin, rest], axis=-1)
    return out.astype(x.dtype)

def diff_attention(q, k, v, lam):
    B, S, H, _, d = q.shape
    nb = S // QBLK
    scale = 1.0 / math.sqrt(d)
    qb = q.reshape(B, nb, QBLK, H, 2, d).transpose(1, 0, 2, 3, 4, 5)
    kpos = jnp.arange(S)

    def one_block(args):
        qblk, i = args
        s = jnp.einsum('bqhcd,bkhcd->bhcqk', qblk, k).astype(jnp.float32) * scale
        qpos = i * QBLK + jnp.arange(QBLK)
        mask = kpos[None, :] <= qpos[:, None]
        p = jax.nn.softmax(jnp.where(mask, s, -jnp.inf), axis=-1)
        a = p[:, :, 0] - lam * p[:, :, 1]
        return jnp.einsum('bhqk,bkhe->bqhe', a.astype(v.dtype), v)

    o = lax.map(one_block, (qb, jnp.arange(nb)))
    return o.transpose(1, 0, 2, 3, 4).reshape(B, S, H, v.shape[-1])

def retention(q, k, v):
    B, S, H, dk = q.shape
    dv = v.shape[-1]
    C = RCHUNK
    nc = S // C
    log_g = jnp.log1p(-jnp.exp2(-5.0 - jnp.arange(H, dtype=jnp.float32)))
    idx = jnp.arange(C, dtype=jnp.float32)
    rel = idx[:, None] - idx[None, :]
    dmask = jnp.where(rel[None] >= 0, jnp.exp(jnp.maximum(rel, 0.0)[None] * log_g[:, None, None]), 0.0)
    zeta = jnp.exp((C - 1 - idx)[None, :] * log_g[:, None])
    xi = jnp.exp((idx + 1.0)[None, :] * log_g[:, None])
    g_chunk = jnp.exp(C * log_g)
    qc = q.reshape(B, nc, C, H, dk)
    kc = k.reshape(B, nc, C, H, dk)
    vc = v.reshape(B, nc, C, H, dv)
    s = jnp.einsum('bnihd,bnjhd->bnhij', qc, kc) * dmask
    o_intra = jnp.einsum('bnhij,bnjhe->bnihe', s, vc)
    kv = jnp.einsum('bnjhd,hj,bnjhe->nbhde', kc, zeta, vc)

    def step(r, kv_n):
        return g_chunk[None, :, None, None] * r + kv_n, r

    _, r_prev = lax.scan(step, jnp.zeros((B, H, dk, dv), jnp.float32), kv)
    o_cross = jnp.einsum('bnihd,hi,nbhde->bnihe', qc, xi, r_prev)
    return (o_intra + o_cross).reshape(B, S, H, dv)

def hier_moe(h, w_gr, b_gr, w_er, b_er, w_gate, w_up, w_down):
    B, S, D = h.shape
    N = B * S
    hf = h.reshape(N, D)
    gl = (hf @ w_gr + b_gr).astype(jnp.float32)
    g_idx = jnp.argmax(gl, axis=-1)
    p_g = jnp.take_along_axis(jax.nn.softmax(gl, axis=-1), g_idx[:, None], axis=1)[:, 0]
    el = (hf @ w_er + b_er).astype(jnp.float32).reshape(N, N_GROUPS, EXPERTS_PER_GROUP)
    el_sel = jnp.take_along_axis(el, g_idx[:, None, None], axis=1)[:, 0]
    top_v, top_i = lax.top_k(el_sel, TOP_K)
    w = jax.nn.softmax(top_v, axis=-1) * p_g[:, None]
    e_flat = (g_idx[:, None] * EXPERTS_PER_GROUP + top_i).reshape(-1).astype(jnp.int32)
    w_flat = w.reshape(-1)
    NK = N * TOP_K
    order = jnp.argsort(e_flat)
    e_s = e_flat[order]
    t_s = (order // TOP_K).astype(jnp.int32)
    w_s = w_flat[order]
    counts = jnp.zeros((N_EXPERTS,), jnp.int32).at[e_flat].add(1)
    padded = ((counts + MOE_BLOCK - 1) // MOE_BLOCK) * MOE_BLOCK
    pad_end = jnp.cumsum(padded)
    pad_start = pad_end - padded
    start = jnp.cumsum(counts) - counts
    dest = pad_start[e_s] + jnp.arange(NK, dtype=jnp.int32) - start[e_s]
    P = NK + N_EXPERTS * MOE_BLOCK
    nblk = P // MOE_BLOCK
    row_tok = jnp.zeros((P,), jnp.int32).at[dest].set(t_s)
    row_w = jnp.zeros((P,), jnp.float32).at[dest].set(w_s)
    blk_expert = jnp.clip(jnp.searchsorted(pad_end, jnp.arange(nblk, dtype=jnp.int32) * MOE_BLOCK, side='right'),
                          0, N_EXPERTS - 1)
    xs = hf[row_tok].reshape(nblk, MOE_BLOCK, D)

    def expert_block(args):
        xb, eid = args
        a = xb @ w_gate[eid]
        u = xb @ w_up[eid]
        return (jax.nn.silu(a) * u) @ w_down[eid]

    ys = lax.map(expert_block, (xs, blk_expert)).reshape(P, D)
    out = jnp.zeros((N, D), h.dtype).at[row_tok].add(ys * row_w[:, None].astype(h.dtype))
    return out.reshape(B, S, D)

def setup_inputs(seed: int = 0) -> dict:
    key = jax.random.key(seed)
    ks = jax.random.split(key, 24)
    nrm = lambda k, shape, fan: jax.random.normal(k, shape, jnp.float32) * fan ** -0.5
    gain = lambda k, shape: 1.0 + 0.02 * jax.random.normal(k, shape, jnp.float32)
    L = DEPTH
    x = jax.random.normal(ks[0], (BATCH, SEQ, D_MODEL), jnp.float32)
    offsets = jax.random.randint(ks[1], (BATCH, 1), 0, 1024, jnp.int32)
    positions = (offsets + jnp.arange(SEQ, dtype=jnp.int32)[None, :]).astype(jnp.int32)
    return {
        "x": x,
        "positions": positions,
        "norm1_g": gain(ks[2], (L, D_MODEL)),
        "w_in": nrm(ks[3], (L, D_MODEL, IN_COLS), D_MODEL),
        "q_norm_g": gain(ks[4], (L, DA_HALF)),
        "k_norm_g": gain(ks[5], (L, DA_HALF)),
        "lambda_q1": 0.1 * jax.random.normal(ks[6], (L, DA_HALF), jnp.float32),
        "lambda_k1": 0.1 * jax.random.normal(ks[7], (L, DA_HALF), jnp.float32),
        "lambda_q2": 0.1 * jax.random.normal(ks[8], (L, DA_HALF), jnp.float32),
        "lambda_k2": 0.1 * jax.random.normal(ks[9], (L, DA_HALF), jnp.float32),
        "diff_subln_g": gain(ks[10], (L, DA_VDIM)),
        "ret_gn_g": gain(ks[11], (L, RET_WIDTH)),
        "ret_gn_b": 0.02 * jax.random.normal(ks[12], (L, RET_WIDTH), jnp.float32),
        "w_branch_a": nrm(ks[13], (L, DA_WIDTH, D_MODEL), DA_WIDTH),
        "w_branch_b": nrm(ks[14], (L, RET_WIDTH, D_MODEL), RET_WIDTH),
        "w_out": nrm(ks[15], (L, D_MODEL, D_MODEL), D_MODEL),
        "norm2_g": gain(ks[16], (L, D_MODEL)),
        "w_group_router": nrm(ks[17], (L, D_MODEL, N_GROUPS), D_MODEL),
        "b_group_router": 0.01 * jax.random.normal(ks[18], (L, N_GROUPS), jnp.float32),
        "w_expert_router": nrm(ks[19], (L, D_MODEL, N_EXPERTS), D_MODEL),
        "b_expert_router": 0.01 * jax.random.normal(ks[20], (L, N_EXPERTS), jnp.float32),
        "w_gate": nrm(ks[21], (L, N_EXPERTS, D_MODEL, EXPERT_FF), D_MODEL),
        "w_up": nrm(ks[22], (L, N_EXPERTS, D_MODEL, EXPERT_FF), D_MODEL),
        "w_down": nrm(ks[23], (L, N_EXPERTS, EXPERT_FF, D_MODEL), EXPERT_FF),
    }

def reference(x, positions, norm1_g, w_in, q_norm_g, k_norm_g, lambda_q1, lambda_k1, lambda_q2, lambda_k2,
              diff_subln_g, ret_gn_g, ret_gn_b, w_branch_a, w_branch_b, w_out, norm2_g,
              w_group_router, b_group_router, w_expert_router, b_expert_router, w_gate, w_up, w_down):
    B, S, D = x.shape
    split_idx = np.cumsum(SPLIT_SIZES)[:-1].tolist()
    for l in range(DEPTH):
        lam_init = 0.8 - 0.6 * math.exp(-0.3 * l)
        h = rms_norm(x, norm1_g[l])
        qa, ka, va, qb, kb, vb, gb, gate_a, gate_b = jnp.split(h @ w_in[l], split_idx, axis=-1)
        qa = apply_rope(rms_norm(qa.reshape(B, S, DA_HEADS, 2, DA_HALF), q_norm_g[l]), positions, ROPE_DIM, ROPE_THETA)
        ka = apply_rope(rms_norm(ka.reshape(B, S, DA_HEADS, 2, DA_HALF), k_norm_g[l]), positions, ROPE_DIM, ROPE_THETA)
        va = va.reshape(B, S, DA_HEADS, DA_VDIM)
        lam = (jnp.exp(jnp.sum(lambda_q1[l].astype(jnp.float32) * lambda_k1[l].astype(jnp.float32)))
               - jnp.exp(jnp.sum(lambda_q2[l].astype(jnp.float32) * lambda_k2[l].astype(jnp.float32)))
               + lam_init)
        oa = rms_norm(diff_attention(qa, ka, va, lam), diff_subln_g[l]) * (1.0 - lam_init)
        ya = oa.reshape(B, S, DA_WIDTH) @ w_branch_a[l]
        qr = apply_rope(qb.reshape(B, S, RET_HEADS, RET_KDIM), positions, RET_KDIM, RET_THETA).astype(jnp.float32)
        kr = apply_rope(kb.reshape(B, S, RET_HEADS, RET_KDIM), positions, RET_KDIM, RET_THETA).astype(jnp.float32) * RET_KDIM ** -0.5
        vr = vb.reshape(B, S, RET_HEADS, RET_VDIM).astype(jnp.float32)
        ob = retention(qr, kr, vr)
        mu = jnp.mean(ob, axis=-1, keepdims=True)
        var = jnp.mean(jnp.square(ob - mu), axis=-1, keepdims=True)
        ob = ((ob - mu) * lax.rsqrt(var + EPS)).reshape(B, S, RET_WIDTH)
        ob = (ob * ret_gn_g[l].astype(jnp.float32) + ret_gn_b[l].astype(jnp.float32)).astype(x.dtype)
        yb = (jax.nn.silu(gb) * ob) @ w_branch_b[l]
        merged = jax.nn.sigmoid(gate_a) * ya + jax.nn.sigmoid(gate_b) * yb
        x = x + merged @ w_out[l]
        h2 = rms_norm(x, norm2_g[l])
        x = x + hier_moe(h2, w_group_router[l], b_group_router[l], w_expert_router[l], b_expert_router[l],
                         w_gate[l], w_up[l], w_down[l])
    return x


_drawn_inputs = setup_inputs


def setup_inputs(seed=0):
    import zlib

    import numpy as np

    out = dict(_drawn_inputs(seed))
    spreads = {}
    factors = {'q_norm_g': 3.25,
     'k_norm_g': 2.864,
     'lambda_q1': 2.716,
     'lambda_k2': 7.36,
     'diff_subln_g': 9.941,
     'ret_gn_g': 15.885,
     'ret_gn_b': 15.703,
     'b_group_router': 12.827,
     'b_expert_router': 14.238,
     'norm2_g': 4.525}
    for name, (base, spread) in spreads.items():
        noise = np.random.default_rng([zlib.crc32(name.encode()), seed]).standard_normal(out[name].shape)
        drawn = base * np.exp(spread * noise) if base else spread * noise
        out[name] = __import__('jax').numpy.asarray(drawn.astype(out[name].dtype))
    for name, factor in factors.items():
        out[name] = (out[name] * factor).astype(out[name].dtype)
    return out
```

```python
from contextlib import ExitStack
import math

import numpy as np

import concourse.bass as bass
from concourse import mybir

ALU = mybir.AluOpType
ACT = mybir.ActivationFunctionType
AX_X = mybir.AxisListType.X
F32 = mybir.dt.float32
F32R = mybir.dt.float32r
I32 = mybir.dt.int32
DS = bass.ds

P = 128
EPS = 1e-6
BIG_NEG = -1.0e30
QA, KA, VA, QB, KB, VB, GB, GATE_A, GATE_B = 0, 512, 1024, 1536, 2048, 2560, 3072, 3584, 4608
N_TILES = 8
N_KD = 8
N_HEADS = 4
N_EXP = 32
N_GRP = 4
EPG = 8
FF = 512
LAM_INIT = 0.8 - 0.6 * math.exp(-0.3 * 0)
BLOCK = 128
MAX_BLOCKS = 8
FREE = 1
DMA = 16

CONST_WIDTHS = [
    ("ident", 128), ("tri", 128), ("causal", 128), ("strict", 128), ("ones", 128), ("iota", 256),
    ("freq", 72), ("ret_q", 4), ("ret_k", 4), ("ret_g", 4), ("ret_ginv", 4),
    ("token1", 16), ("minus_half", 16), ("half_pi", 1), ("iota_grp", 4), ("iota_exp8", 8),
]
CONST_AT = {}
_at = 0
for _name, _width in CONST_WIDTHS:
    CONST_AT[_name] = (_at, _at + _width)
    _at += _width
N_CONST = _at


def constants():
    p = np.arange(P)
    c = {}
    c["ident"] = np.eye(P)
    c["tri"] = (p[:, None] <= p[None, :]).astype(np.float64)
    c["causal"] = np.where(p[None, :] <= p[:, None], 0.0, BIG_NEG)
    c["strict"] = (p[:, None] < p[None, :]).astype(np.float64)
    c["ones"] = np.ones((P, P))
    c["iota"] = np.tile(np.arange(256.0), (P, 1))
    fa = np.power(np.float32(500000.0), (-2.0 * np.arange(8, dtype=np.float32) / np.float32(16)).astype(np.float32))
    fr = np.power(np.float32(10000.0), (-2.0 * np.arange(64, dtype=np.float32) / np.float32(128)).astype(np.float32))
    c["freq"] = np.tile(np.concatenate([fa, fr]), (P, 1))
    gamma = 1.0 - 2.0 ** (-5.0 - np.arange(4.0))
    c["ret_q"] = gamma[None, :] ** (p[:, None] + 1.0 + P)
    c["ret_k"] = gamma[None, :] ** (-(p[:, None] + 1.0)) * P ** -0.5
    c["ret_g"] = np.tile(gamma ** P, (P, 1))
    c["ret_ginv"] = np.tile(gamma ** -P, (P, 1))
    c["token1"] = (p[:, None] + 1.0) + 128.0 * np.arange(16)[None, :]
    c["minus_half"] = np.full((P, 16), -0.5)
    c["half_pi"] = np.full((P, 1), np.pi / 2)
    c["iota_grp"] = np.tile(np.arange(4.0), (P, 1))
    c["iota_exp8"] = np.tile(np.arange(8.0), (P, 1))
    return np.concatenate([c[name] for name, _ in CONST_WIDTHS], axis=1).astype(np.float32)


def split3(pe, out, left, right, start, stop):
    (lh, ll), (rh, rl) = left, right
    pe.matmul(out, lh, rh, start=start, stop=False)
    pe.matmul(out, lh, rl, start=False, stop=False)
    return pe.matmul(out, ll, rh, start=False, stop=stop)




def decoder_layer(nc, T):
    with ExitStack() as ctx:
        limit = nc.sbuf_usable_end
        cursor = [(nc.sbuf_base + 63) // 64 * 64]

        def place(size):
            at = cursor[0]
            cursor[0] = (at + size + 31) // 32 * 32
            assert cursor[0] <= limit, (cursor[0], limit)
            return at

        def sb(name, shape, dt=F32, at=None):
            size = int(np.prod(shape[1:])) * 4
            return nc.alloc_sbuf_tensor_at(name, shape, dt, offset=place(size) if at is None else at)

        def psum(name, shape):
            return ctx.enter_context(nc.psum_tensor(name, shape, F32))

        def sem(name):
            return ctx.enter_context(nc.semaphore(name))

        KIB = 1024

        consts = sb("consts", [P, N_CONST])

        def const(name, a=0, b=None):
            lo, hi = CONST_AT[name]
            return consts[:, lo + a:(hi if b is None else lo + b)]

        ident = const("ident")
        small = sb("small", [P, 64])
        g1_cols = small[:, 0:8]
        subln_col = small[:, 8:9]
        subln_scaled = small[:, 9:10]
        lam = small[:, 10:11]
        lam_e = small[:, 12:14]
        lam_s = small[:, 14:16]
        x_ss = small[:, 16:24]
        x_rstd = small[:, 24:32]
        x_ms = small[:, 32:40]
        posf = small[:, 40:48]
        posi = sb("posi", [P, 8], I32)

        R_HT, R_A, R_B, R_OT = place(64 * KIB), place(24 * KIB), place(32 * KIB), place(32 * KIB)
        R_WORK = cursor[0]

        hTH = sb("hTH", [P, N_KD, 1024], F32R, at=R_HT)
        hTL = sb("hTL", [P, N_KD, 1024], F32R, at=R_HT + 32 * KIB)
        wA_in = sb("wA_in", [P, N_KD, 384], F32, at=R_A)
        wAL = sb("wAL", [P, N_KD, 384], F32R, at=R_A)
        wAH = sb("wAH", [P, N_KD, 384], F32R, at=R_A + 12 * KIB)
        wB_in = sb("wB_in", [P, N_KD, 512], F32, at=R_B)
        wBL = sb("wBL", [P, N_KD, 512], F32R, at=R_B)
        wBH = sb("wBH", [P, N_KD, 512], F32R, at=R_B + 16 * KIB)
        x_all = sb("x_all", [P, N_TILES, 1024], F32, at=R_B)
        oT = sb("oT", [P, 8, 1024], F32, at=R_OT)
        x_sq = sb("x_sq", [P, 1024], F32, at=R_OT)
        lam_rows = sb("lam_rows", [P, 4, 64], F32, at=R_OT + 4 * KIB)
        lam_prod = sb("lam_prod", [P, 2, 64], F32, at=R_OT + 6 * KIB)
        ang = sb("ang", [P, N_TILES, 72], F32, at=R_OT + 8 * KIB)
        turns = sb("turns", [P, N_TILES, 72], F32, at=R_OT + 12 * KIB)

        sin_t = sb("sin_t", [P, N_TILES, 72])
        cos_t = sb("cos_t", [P, N_TILES, 72])
        gains = sb("gains", [P, 2, 64])
        gn_rows = sb("gn_rows", [P, 2, 128])
        KH = sb("KH", [P, 1024], F32R)
        KL = sb("KL", [P, 1024], F32R)
        QH = sb("QH", [P, 128], F32R)
        QL = sb("QL", [P, 128], F32R)
        V = sb("V", [P, N_TILES, 128])
        probs = sb("probs", [P, 2, 1024])
        aT = sb("aT", [P, N_TILES, 128])
        sqA = sb("sqA", [P, 256])
        qkA = sb("qkA", [P, 256])
        rope_cos = sb("rope_cos", [P, 4, 2, 8])
        rope_sin = sb("rope_sin", [P, 4, 2, 8])
        oN = sb("oN", [P, 128])
        stats = sb("stats", [P, 32])
        ss_qk, ms_qk, rstd_qk = stats[:, 0:4], stats[:, 4:8], stats[:, 8:12]
        negmax, rowmax, rowsum, rrow = stats[:, 12:14], stats[:, 14:16], stats[:, 16:18], stats[:, 18:20]
        ss_o, ms_o, rstd_o = stats[:, 20:21], stats[:, 21:22], stats[:, 22:23]
        qkS = sb("qkS", [P, 4, 64])
        qkCos = sb("qkCos", [P, 4, 64])
        qkSin = sb("qkSin", [P, 4, 64])
        qkR = sb("qkR", [P, 4, 64])
        vg = sb("vg", [P, 2, 256])
        eg = sb("eg", [P, 128])
        sg = sb("sg", [P, 2, 128])
        qkT = sb("qkT", [P, 2, 256])
        sT = sb("sT", [P, 128])
        U = sb("U", [P, 2, 128])
        onR = sb("onR", [P, 128])
        gatedR = sb("gatedR", [P, 128])
        bstat = sb("bstat", [P, 16])
        head_c = sb("head_c", [P, 4])

        wC_at = [R_B, R_A]
        wC_in = [sb(f"wC_in{i}", [P, 24, 128], F32, at=wC_at[i]) for i in range(2)]
        wCL = [sb(f"wCL{i}", [P, 16, 128], F32R, at=wC_at[i]) for i in range(2)]
        wCH = [sb(f"wCH{i}", [P, 16, 128], F32R, at=wC_at[i] + 12 * KIB) for i in range(2)]
        merged = sb("merged", [P, N_KD, 1024], F32, at=R_WORK)
        mergedL = sb("mergedL", [P, N_KD, 1024], F32R, at=R_WORK)
        sig = sb("sig", [P, 2, 512], F32, at=R_WORK + 32 * KIB)
        mergedH = sb("mergedH", [P, N_KD, 1024], F32R, at=R_OT)
        wD_at = [R_B, R_HT]
        wD_in = [sb(f"wD_in{i}", [P, N_KD, 512], F32, at=wD_at[i]) for i in range(2)]
        wDL = [sb(f"wDL{i}", [P, N_KD, 512], F32R, at=wD_at[i]) for i in range(2)]
        wDH = [sb(f"wDH{i}", [P, N_KD, 512], F32R, at=wD_at[i] + 16 * KIB) for i in range(2)]
        x2 = sb("x2", [P, N_TILES, 1024], F32, at=R_HT + 32 * KIB)
        h2 = sb("h2", [P, 2, 1024], F32, at=R_A)
        h2T = sb("h2T", [P, N_KD, 128], F32, at=R_A + 8 * KIB)
        g2_row = sb("g2_row", [P, 1024], F32, at=R_A + 12 * KIB)
        x2_sq = sb("x2_sq", [P, 1024], F32, at=R_A + 16 * KIB)

        wr = sb("wr", [P, N_KD, 36], F32, at=R_A + 20 * KIB)
        br = sb("br", [P, 36], F32, at=R_A + 22 * KIB)
        route_at = [max(cursor[0], R_WORK + 37 * KIB)]

        def rt(name, shape, dt=F32):
            at = route_at[0]
            route_at[0] = (at + int(np.prod(shape[1:])) * 4 + 31) // 32 * 32
            assert route_at[0] <= limit, (name, route_at[0], limit)
            return nc.alloc_sbuf_tensor_at(name, shape, dt, offset=at)

        logits = rt("logits", [P, N_TILES, 36])
        n2 = rt("n2", [P, 4, 8])
        wsel = rt("wsel", [P, 2, N_TILES])
        q_at = [R_WORK]

        def rq(name, shape, dt=F32):
            at = q_at[0]
            q_at[0] = (at + int(np.prod(shape[1:])) * 4 + 31) // 32 * 32
            return nc.alloc_sbuf_tensor_at(name, shape, dt, offset=at)

        gmax = rq("gmax", [P, 8])
        gdiff = rq("gdiff", [P, 8, 4])
        gexp = rq("gexp", [P, 8, 4])
        gsum = rq("gsum", [P, 8])
        pgrp = rq("pgrp", [P, 8])
        gpen = rq("gpen", [P, 8, 4])
        gidx = rq("gidx", [P, 8])
        goh = rq("goh", [P, 8, 4])
        elsel = rq("elsel", [P, 4, 8, 8])
        esum = rq("esum", [P, 2, 8, 8])
        el8 = rq("el8", [P, 8, 8])
        vtop = rq("vtop", [P, 2, 8])
        epen = rq("epen", [P, 8, 8])
        eidx = rq("eidx", [P, 2, 8])
        eoh = rq("eoh", [P, 8, 8])
        el8b = rq("el8b", [P, 8, 8])
        vdiff = rq("vdiff", [P, 8])
        vexp = rq("vexp", [P, 8])
        vden = rq("vden", [P, 8])
        eglob = rq("eglob", [P, 2, 8])
        oh = rq("oh", [P, 2, 8, 32])
        mask = rq("mask", [P, 8, 32])
        before = rq("before", [P, 9, 32])
        posm = rq("posm", [P, 2, 8, 32])
        pos = rq("pos", [P, 2, 8])
        pos_i = rq("pos_i", [P, 2, 8], I32)
        slot_i = rq("slot_i", [P, 2, 8], I32)
        blk_i = rq("blk_i", [P, 2, 8], I32)
        slotf = rq("slotf", [P, 2, 8])
        blkf = rq("blkf", [P, 2, 8])
        key = rq("key", [P, 2, 8])
        pick = [rq(f"pick{i}", [P, 128]) for i in range(2)]
        keyid = [rq(f"keyid{i}", [P, 256]) for i in range(2)]
        padded = rq("padded", [P, 256])
        zf = rq("zf", [P, 256])
        ids_scatter = rt("ids_scatter", [P, 256], I32)
        ids_gather = rt("ids_gather", [P, 256], I32)
        counts_f = rq("counts_f", [P, 33])
        counts_i = rt("counts_i", [P, 33], I32)
        cur_gather = rt("cur_gather", [P, 1], I32)
        cur_scatter = rt("cur_scatter", [P, 1], I32)

        slot_at = [R_B, R_B + 16 * KIB, R_HT, R_HT + 16 * KIB, R_OT, R_OT + 16 * KIB]
        w_in6 = [sb(f"w_slot{i}", [P, 2048], F32, at=slot_at[i]) for i in range(6)]
        w_low = [sb(f"w_low{i}", [P, 2048], F32R, at=slot_at[i]) for i in range(6)]
        w_high = [sb(f"w_high{i}", [P, 2048], F32R, at=slot_at[i] + 8 * KIB) for i in range(6)]
        e_at = [max(R_WORK, 0)]

        def ex(name, shape, dt=F32):
            at = e_at[0]
            e_at[0] = at + int(np.prod(shape[1:])) * 4
            assert e_at[0] <= R_WORK + 36 * KIB
            return nc.alloc_sbuf_tensor_at(name, shape, dt, offset=at)

        xe = sb("xe", [P, 1024], F32, at=R_A)
        xeH = sb("xeH", [P, 8, 128], F32R, at=R_A + 4 * KIB)
        xeL = sb("xeL", [P, 8, 128], F32R, at=R_A + 8 * KIB)
        silu = sb("silu", [P, 512], F32, at=R_A + 12 * KIB)
        hid = sb("hid", [P, 512], F32, at=R_A + 14 * KIB)
        hidH = sb("hidH", [P, 4, 128], F32R, at=R_A + 16 * KIB)
        hidL = sb("hidL", [P, 4, 128], F32R, at=R_A + 18 * KIB)
        y = sb("y", [P, 1024], F32, at=R_A + 20 * KIB)
        comb = sb("comb", [P, 2, 2, 1024], F32, at=R_WORK + 8 * KIB)
        res = sb("res", [P, 2, 1024], F32, at=R_WORK + 24 * KIB)

        PROJ = [psum("proj0", [P, 512]), psum("proj1", [P, 512])]
        SC = psum("scores", [P, 2, 1024])
        TB = psum("turned", [P, 512])
        OB = psum("outs", [P, 512])

        h2_dram = nc.dram_tensor("h2_rows", (1024, 1024), F32, kind="Internal").ap()
        y_dram = nc.dram_tensor("y_rows", (2048, 1024), F32, kind="Internal").ap()

        w_in_v = T["w_in"][0].rearrange("(k p) c -> p k c", p=P)
        wa_v = T["w_branch_a"][0].rearrange("(k p) c -> p k c", p=P)
        wb_v = T["w_branch_b"][0].rearrange("(k p) c -> p k c", p=P)
        wo_v = T["w_out"][0].rearrange("(k p) c -> p k c", p=P)
        x_v = T["x"][0].rearrange("(i p) d -> p i d", p=P)
        out_v = T["out"][0].rearrange("(i p) d -> p i d", p=P)
        h2_v = h2_dram.rearrange("(i p) d -> p i d", p=P)
        y_v = y_dram.rearrange("(c i p) d -> p c i d", c=2, p=P)
        wg_v = T["w_gate"][0].rearrange("e (p k) f -> e p (k f)", p=P)
        wu_v = T["w_up"][0].rearrange("e (p k) f -> e p (k f)", p=P)
        wd_v = T["w_down"][0].rearrange("e (p k) n -> e p (k n)", p=P)

        def bank(n):
            if n < 4:
                return SC[:, n // 2, (n % 2) * 512:(n % 2) * 512 + 512]
            return [PROJ[0], PROJ[1], TB, OB][n - 4][:, :]

        names = """rows_stored consts_in small_in x_in0 x_in1 x_in2 x_in3 x_sq_done x_ms_done x_rstd_done xn_done xT_done hH_done
            hL_done lam_step lam_expd ang_step angle_done trig_done wA_landed wA_high wA_low
            wB_landed wB_high wB_low gn_landed t_free projA projB sqA_done vA_done ssA_done msA_done
            rstdA_done normA_done ropeA_step ropedA qkTA qkHA scored masked maxed negged exped
            rowsum_inv p1_scaled probs_done aT1 aT2 pv_done o_sq o_ms o_rstd oN_done oTA qkS_done
            vg_done eg_done cosB sinB ropedB eg1 egr sg_done qkTB kv_done U_done st_done sT_done oB
            bn_s bn_a bn_v bn_r onR_done gate_step gated gTB wC_landed0 wC_landed1 wC_high wC_low
            gates_done ys_done sig_exp sig_one sig_inv sig_mul merged_step wD_landed0 wD_landed1
            wD_high wD_low x2_in mH mL d_done x2_done g2_in router_in n2_sq n2_ms n2_rstd h2_done
            h2T_done h2T_out lg_done logit_done h2_stored0 h2_stored1 rstep ract pmm pick_done
            pick_used ids_done w_land0 w_land1 w_land2 w_land3 w_land4 w_land5 w_free_gu w_free_d
            idx_copied xe_landed xeT_done xeH_done xeL_done silu_done hid_done hidT_done hidH_done
            hidL_done y_out scattered comb_in0 comb_in1 comb_mid res_done out_stored0 out_stored1
            head_consts gu_high gu_low d_high d_low xe_zero v_w v_hi v_lo""".split()
        S = {n: sem(n) for n in names}

        block = ctx.enter_context(nc.Block())
        N_STEPS = 2 * N_TILES + 3
        PREP = {2: [0], 3: [1], 4: [2, 3], 5: [4], 6: [5], 7: [6, 7]}

        def tile_at(s):
            return ("A", s) if 0 <= s < N_TILES else ("B", s - N_TILES) if N_TILES <= s < 2 * N_TILES else (None, 0)


        def overflow(eng, block_of):
            most = eng.value_load(counts_i[0:1, 32:33], min_val=0, max_val=1024)
            with eng.If(most > BLOCK):
                n = eng.alloc_register()
                eng.reg_mov(n, 0)
                with eng.Fori(1, MAX_BLOCKS) as b:
                    with eng.Fori(0, N_EXP) as e:
                        held = eng.value_load(counts_i[0:1, DS(e, 1)], min_val=0, max_val=1024)
                        with eng.If(held > b * BLOCK):
                            block_of(eng.snap(n), e, b)
                            eng.reg_add(n, n, 1)
                        with eng.Else():
                            eng.nop()
                        eng.nop()
                eng.nop()
            with eng.Else():
                eng.nop()
            eng.nop()

        STARTS_FREE = """t_free ssA_done ropedB sg_done qkTA ropedA gated gTB U_done sT_done
            exped eg_done onR_done pv_done projB qkS_done sig_mul y_out""".split()

        @block.sync
        def _(sp):
            for name in STARTS_FREE:
                sp.sem_inc(S[name], FREE)
            sp.dma_start(x_all[:, 0:2, :], x_v[:, 0:2, :]).then_inc(S["x_in0"], DMA)
            sp.dma_start(consts[:], T["consts"]).then_inc(S["consts_in"], DMA)
            sp.dma_start(g1_cols, T["norm1_g"][0].rearrange("(k p) -> p k", p=P),
                         allow_slow_non_contiguous=True).then_inc(S["small_in"], DMA)
            for j in range(1, 4):
                sp.dma_start(x_all[:, 2 * j:2 * j + 2, :], x_v[:, 2 * j:2 * j + 2, :]).then_inc(S[f"x_in{j}"], DMA)
            sp.dma_start(subln_col, T["diff_subln_g"][0].rearrange("(p o) -> p o", o=1),
                         allow_slow_non_contiguous=True).then_inc(S["small_in"], DMA)
            sp.dma_start(posi[:], T["positions"][0].rearrange("(i p) -> p i", p=P),
                         allow_slow_non_contiguous=True).then_inc(S["small_in"], DMA)
            for j, n in enumerate(("lambda_q1", "lambda_k1", "lambda_q2", "lambda_k2")):
                sp.dma_start(lam_rows[:, j, :], T[n][0].partition_broadcast(P)).then_inc(S["small_in"], DMA)
            for j, n in enumerate(("q_norm_g", "k_norm_g")):
                sp.dma_start(gains[:, j, :], T[n][0].partition_broadcast(P)).then_inc(S["small_in"], DMA)

            def load_A(head):
                for j, col in enumerate((QA, KA, VA)):
                    sp.dma_start(wA_in[:, :, 128 * j:128 * j + 128],
                                 w_in_v[:, :, DS(head * 128 + col, 128)]).then_inc(S["wA_landed"], DMA)

            load_A(0)
            sp.wait_ge(S["xT_done"], 16)
            with sp.Fori(0, N_HEADS) as h:
                h8 = sp.snap(h * 8)
                sp.wait_ge(S["projB"], h8 + FREE)
                sp.wait_ge(S["gated"], h8 + FREE)
                for j, col in enumerate((QB, KB, VB, GB)):
                    sp.dma_start(wB_in[:, :, 128 * j:128 * j + 128],
                                 w_in_v[:, :, DS(h * 128 + col, 128)]).then_inc(S["wB_landed"], DMA)
                for j, n in enumerate(("ret_gn_g", "ret_gn_b")):
                    sp.dma_start(gn_rows[:, j, :],
                                 T[n][0][DS(h * 128, 128)].partition_broadcast(P)).then_inc(S["gn_landed"], DMA)
                sp.wait_ge(S["projA"], h8 + 8)
                load_A(h + 1)

            def load_C(m, slot):
                sp.dma_start(wC_in[slot][:, 0:8, :], w_in_v[:, :, DS(m * 128 + GATE_A, 128)]).then_inc(S[f"wC_landed{slot}"], DMA)
                sp.dma_start(wC_in[slot][:, 8:16, :], w_in_v[:, :, DS(m * 128 + GATE_B, 128)]).then_inc(S[f"wC_landed{slot}"], DMA)
                sp.dma_start(wC_in[slot][:, 16:20, :], wa_v[:, :, DS(m * 128, 128)]).then_inc(S[f"wC_landed{slot}"], DMA)
                sp.dma_start(wC_in[slot][:, 20:24, :], wb_v[:, :, DS(m * 128, 128)]).then_inc(S[f"wC_landed{slot}"], DMA)

            sp.wait_ge(S["projB"], 8 * N_HEADS + FREE)
            load_C(0, 0)
            sp.wait_ge(S["wA_low"], 8 * N_HEADS + 8)
            load_C(1, 1)
            with sp.Fori(1, 4) as j:
                sp.wait_ge(S["ys_done"], j * 4 - 2)
                load_C(j * 2, 0)
                sp.wait_ge(S["ys_done"], j * 4)
                load_C(j * 2 + 1, 1)
            sp.wait_ge(S["ys_done"], 14)
            sp.dma_start(wD_in[0][:], wo_v[:, :, 0:512]).then_inc(S["wD_landed0"], DMA)
            sp.wait_ge(S["ys_done"], 16)
            sp.dma_start(wD_in[1][:], wo_v[:, :, 512:1024]).then_inc(S["wD_landed1"], DMA)
            sp.dma_start(x2[:], x_v).then_inc(S["x2_in"], DMA)
            sp.dma_start(g2_row[:], T["norm2_g"][0].partition_broadcast(P)).then_inc(S["g2_in"], DMA)
            sp.dma_start(wr[:, :, 0:4], T["w_group_router"][0].rearrange("(k p) c -> p k c", p=P)).then_inc(S["router_in"], DMA)
            sp.dma_start(wr[:, :, 4:36], T["w_expert_router"][0].rearrange("(k p) c -> p k c", p=P)).then_inc(S["router_in"], DMA)
            sp.dma_start(br[:, 0:4], T["b_group_router"][0].partition_broadcast(P)).then_inc(S["router_in"], DMA)
            sp.dma_start(br[:, 4:36], T["b_expert_router"][0].partition_broadcast(P)).then_inc(S["router_in"], DMA)

            def load_gu(e, slots=range(4), land="w_land"):
                for c in slots:
                    v = (wg_v, wu_v)[c % 2]
                    sp.dma_start(w_in6[c][:], v[e][:, (c // 2) * 2048:(c // 2) * 2048 + 2048]).then_inc(S[f"w_land{c}"], DMA)

            def load_d(e, slots=(4, 5)):
                for c in slots:
                    sp.dma_start(w_in6[c][:], wd_v[e][:, (c - 4) * 2048:(c - 4) * 2048 + 2048]).then_inc(S[f"w_land{c}"], DMA)

            sp.wait_ge(S["d_done"], 8)
            load_gu(0, (0, 1))
            for i in range(N_TILES):
                sp.wait_ge(S["h2_done"], i + 1)
                sp.dma_start(h2_v[:, i, :], h2[:, i % 2, :]).then_inc(S[f"h2_stored{i % 2}"], DMA)
            sp.wait_ge(S["d_done"], 16)
            load_gu(0, (2, 3))
            load_d(0)
            for c in range(4):
                sp.wait_ge(S["w_free_gu"], c + 1)
                load_gu(1, (c,))
            with sp.Fori(1, N_EXP - 1) as e:
                for c in range(4):
                    sp.wait_ge(S["w_free_gu"], e * 4 + (c + 1))
                    load_gu(e + 1, (c,))
                for c in (4, 5):
                    sp.wait_ge(S["w_free_d"], e * 2 + (c - 5))
                    load_d(e, (c,))
            for c in (4, 5):
                sp.wait_ge(S["w_free_d"], 2 * (N_EXP - 1) + (c - 5))
                load_d(N_EXP - 1, (c,))

            sp.wait_ge(S["ids_done"], 1)

            def loads_again(n, e, b):
                sp.wait_ge(S["scattered"], n * DMA + DMA * N_EXP)
                for c in range(4):
                    sp.dma_start(w_in6[c][:], (wg_v, wu_v)[c % 2][e][:, (c // 2) * 2048:(c // 2) * 2048 + 2048]).then_inc(S["v_w"], DMA)
                for c in (4, 5):
                    sp.dma_start(w_in6[c][:], wd_v[e][:, (c - 4) * 2048:(c - 4) * 2048 + 2048]).then_inc(S["v_w"], DMA)

            overflow(sp, loads_again)
            sp.wait_ge(S["rows_stored"], 1)

            for i in range(N_TILES):
                if i >= 2:
                    sp.wait_ge(S["res_done"], i - 1)
                for c in range(2):
                    sp.dma_start(comb[:, i % 2, c, :], y_v[:, c, i, :]).then_inc(S[f"comb_in{i % 2}"], DMA)
            sp.wait_ge(S["out_stored0"], DMA * N_TILES // 2)
            sp.wait_ge(S["out_stored1"], DMA * N_TILES // 2)


        def turn_rows(pe, src_rows, dst, step, n):
            for k in range(n):
                last = pe.transpose(dst[:, k * 128:(k + 1) * 128], src_rows[:, DS(k, 128, step=step)], ident)
            return last

        def gate_up(pe, c):
            for k in range(4):
                kk = (c // 2) * 4 + k
                last = split3(pe, PROJ[c % 2][:, :], (xeH[:, kk, :], xeL[:, kk, :]),
                              (w_high[c][:, k * 512:(k + 1) * 512], w_low[c][:, k * 512:(k + 1) * 512]),
                              kk == 0, kk == 7)
            return last

        def down(pe, c):
            for k in range(2):
                kk = (c - 4) * 2 + k
                for half in range(2):
                    lo = k * 1024 + half * 512
                    last = split3(pe, SC[:, 1, half * 512:(half + 1) * 512], (hidH[:, kk, :], hidL[:, kk, :]),
                                  (w_high[c][:, lo:lo + 512], w_low[c][:, lo:lo + 512]), kk == 0, kk == 3)
            return last

        T_PER_HEAD = 28 + 16

        @block.tensor
        def _(pe):
            pe.wait_ge(S["consts_in"], DMA)
            for n in range(16):
                half, k = n // 8, n % 8
                pe.wait_ge(S["xn_done"], 4 * half + 4)
                if n >= 4:
                    pe.wait_ge(S["hL_done"], n - 3)
                for i in range(4):
                    last = pe.transpose(bank(n % 4)[:, i * 128:(i + 1) * 128],
                                        x_all[:, 4 * half + i, k * 128:(k + 1) * 128], ident)
                last.then_inc(S["xT_done"], 1)
            pe.wait_ge(S["hL_done"], 16)

            with pe.Fori(0, N_HEADS) as h:
                h8, h7, hT_ = pe.snap(h * 8), pe.snap(h * 7), pe.snap(h * T_PER_HEAD)
                t_used = [0]

                def take_turned():
                    pe.wait_ge(S["t_free"], hT_ + t_used[0] + FREE)
                    t_used[0] += 1

                def project(s, ks):
                    unit, i = tile_at(s)
                    if ks[0] == 0:
                        if s == 0:
                            pe.wait_ge(S["wA_low"], h8 + 8)
                        if s == N_TILES:
                            pe.wait_ge(S["wB_low"], h8 + 8)
                        before_unit, before_i = tile_at(s - 2)
                        if before_unit == "A":
                            pe.wait_ge(S["normA_done"], h8 + (before_i + 1))
                        elif before_unit == "B":
                            pe.wait_ge(S["eg_done"], h8 + (before_i + 1) + FREE)
                        else:
                            pe.wait_ge(S["eg_done"], h8 + FREE)
                    wh, wl, cols = (wAH, wAL, 384) if unit == "A" else (wBH, wBL, 512)
                    for k in ks:
                        last = split3(pe, PROJ[s % 2][:, 0:cols],
                                      (hTH[:, k, i * 128:(i + 1) * 128], hTL[:, k, i * 128:(i + 1) * 128]),
                                      (wh[:, k, :], wl[:, k, :]), k == 0, k == 7)
                    if ks[-1] == 7:
                        last.then_inc(S["projA" if unit == "A" else "projB"], 1)

                for s in range(N_STEPS):
                    projecting = s < 2 * N_TILES
                    (u1, i1), (u2, i2), (u3, i3) = tile_at(s - 1), tile_at(s - 2), tile_at(s - 3)
                    if u3 == "A":
                        pe.wait_ge(S["oN_done"], h8 + (i3 + 1))
                        take_turned()
                        pe.transpose(TB[:, 0:128], oN[:, :], ident).then_inc(S["oTA"], 1)
                    if u3 == "B":
                        pe.wait_ge(S["gated"], h8 + (i3 + 1) + FREE)
                        take_turned()
                        pe.transpose(TB[:, 0:128], gatedR[:, :], ident).then_inc(S["gTB"], 1)
                    if projecting:
                        project(s, [0, 1])
                    if u2 == "A":
                        pe.wait_ge(S["probs_done"], h8 + (i2 + 1))
                        take_turned()
                        for j in range(min(4, i2 + 1)):
                            last = pe.transpose(TB[:, j * 128:(j + 1) * 128], probs[:, 0, j * 128:(j + 1) * 128], ident)
                        last.then_inc(S["aT1"], 1)
                    if projecting:
                        project(s, [2, 3])
                    if u2 == "A" and i2 >= 4:
                        take_turned()
                        for j in range(4, i2 + 1):
                            last = pe.transpose(TB[:, (j - 4) * 128:(j - 3) * 128], probs[:, 0, j * 128:(j + 1) * 128], ident)
                        last.then_inc(S["aT2"], 1)
                    if projecting:
                        project(s, [4, 5])
                    if u1 == "A":
                        pe.wait_ge(S["ropedA"], h8 * 2 + (2 * i1 + 2) + FREE)
                        take_turned()
                        pe.transpose(TB[:, 0:128], qkA[:, 0:128], ident)
                        pe.transpose(TB[:, 128:256], qkA[:, 128:256], ident).then_inc(S["qkTA"], 1)
                    if u1 == "B":
                        pe.wait_ge(S["ropedB"], h8 * 2 + (2 * i1 + 2) + FREE)
                        take_turned()
                        pe.transpose(TB[:, 0:128], qkR[:, 0:2, :].rearrange("p a b -> p (a b)"), ident)
                        pe.transpose(TB[:, 128:256], qkR[:, 2:4, :].rearrange("p a b -> p (a b)"), ident).then_inc(S["qkTB"], 1)
                    if u2 == "A":
                        if i2 == 0:
                            pe.wait_ge(S["onR_done"], h8 + FREE)
                        else:
                            pe.wait_ge(S["oN_done"], h8 + i2)
                        if u1 is None:
                            pe.wait_ge(S["t_free"], hT_ + t_used[0] + FREE)
                        for j in range(i2 + 1):
                            last = pe.matmul(OB[:, 0:128], aT[:, j, :], V[:, j, :], start=(j == 0), stop=(j == i2))
                        last.then_inc(S["pv_done"], 1)
                    if u2 == "B":
                        pe.wait_ge(S["sT_done"], h8 + (i2 + 1) + FREE)
                        if i2 == 0:
                            pe.wait_ge(S["oN_done"], h8 + 8)
                        else:
                            pe.wait_ge(S["onR_done"], h8 + i2 + FREE)
                            pe.wait_ge(S["U_done"], h7 + i2 + FREE)
                        last = pe.matmul(OB[:, 0:128], sT[:, :], vg[:, i2 % 2, 0:128], start=True, stop=(i2 == 0))
                        if i2 > 0:
                            last = pe.matmul(OB[:, 0:128], qkT[:, i2 % 2, 0:128], U[:, i2 % 2, :], start=False, stop=True)
                        last.then_inc(S["oB"], 1)
                    if u1 == "B" and i1 < N_TILES - 1:
                        if i1 == 0:
                            pe.wait_ge(S["exped"], h8 * 2 + 16 + FREE)
                        pe.wait_ge(S["U_done"], h7 + i1 + FREE)
                        pe.wait_ge(S["vg_done"], h8 + (i1 + 1))
                        pe.matmul(bank(2)[:, 0:128], qkR[:, 2:4, :].rearrange("p a b -> p (a b)"), vg[:, i1 % 2, 0:128],
                                  start=True, stop=True).then_inc(S["kv_done"], 1)
                    if projecting:
                        project(s, [6, 7])
                    if u1 == "A":
                        if i1 == 0:
                            pe.wait_ge(S["sT_done"], h8 + FREE)
                            pe.wait_ge(S["U_done"], h7 + FREE)
                        pe.wait_ge(S["exped"], h8 * 2 + 2 * i1 + FREE)
                        pe.wait_ge(S["t_free"], hT_ + t_used[0] + FREE)
                        for c in range(2):
                            r = slice(c * 64, c * 64 + 64)
                            for k0 in range(0, (i1 + 1) * 128, 512):
                                k1 = min(k0 + 512, (i1 + 1) * 128)
                                last = split3(pe, SC[:, c, k0:k1], (QH[r, :], QL[r, :]), (KH[r, k0:k1], KL[r, k0:k1]),
                                              True, True)
                        last.then_inc(S["scored"], 1)
                    if u1 == "B":
                        pe.wait_ge(S["sT_done"], h8 + i1 + FREE)
                        pe.wait_ge(S["t_free"], hT_ + t_used[0] + FREE)
                        pe.matmul(bank(0)[:, 0:128], qkT[:, i1 % 2, 128:256], qkT[:, i1 % 2, 0:128],
                                  start=True, stop=True).then_inc(S["st_done"], 1)
                assert t_used[0] == T_PER_HEAD

            pe.wait_ge(S["t_free"], N_HEADS * T_PER_HEAD + FREE)
            pe.wait_ge(S["onR_done"], 8 * N_HEADS + FREE)
            pe.wait_ge(S["eg_done"], 8 * N_HEADS + FREE)
            pe.wait_ge(S["sT_done"], 8 * N_HEADS + FREE)
            pe.wait_ge(S["U_done"], 7 * N_HEADS + FREE)
            with pe.Fori(0, 4) as j:
                j4, j8 = pe.snap(j * 4), pe.snap(j * 8)
                for sub in range(2):
                    pe.wait_ge(S["wC_low"], j4 + (2 * sub + 2))
                    for th in range(2):
                        n = 2 * sub + th
                        b0 = 4 if th == 0 else 0
                        if n < 2:
                            pe.wait_ge(S["sig_mul"], j8 + FREE)
                        if n >= 2:
                            pe.wait_ge(S["sig_mul"], j8 + (2 * n - 2) + FREE)
                        tok = slice(th * 512, th * 512 + 512)
                        for g in range(2):
                            for k in range(8):
                                last = split3(pe, bank(b0 + g), (wCH[sub][:, g * 8 + k, :], wCL[sub][:, g * 8 + k, :]),
                                              (hTH[:, k, tok], hTL[:, k, tok]), k == 0, k == 7)
                        last.then_inc(S["gates_done"], 1)
                        for g in range(2):
                            for k in range(4):
                                last = pe.matmul(bank(b0 + 2 + g), wC_in[sub][:, 16 + 4 * g + k, :], oT[:, 4 * g + k, tok],
                                                 start=(k == 0), stop=(k == 3))
                        last.then_inc(S["ys_done"], 1)

            pe.wait_ge(S["sig_mul"], 32 + FREE)

            def out_proj(n, i):
                pe.wait_ge(S["wD_low"], 2 * n + 2)
                pe.wait_ge(S["mL"], i + 1)
                cnt = 8 * n + i
                if cnt >= 3:
                    pe.wait_ge(S["x2_done"], cnt - 2)
                tok = slice(i * 128, i * 128 + 128)
                for k in range(8):
                    last = split3(pe, bank(4 + cnt % 3), (mergedH[:, k, tok], mergedL[:, k, tok]),
                                  (wDH[n][:, k, :], wDL[n][:, k, :]), k == 0, k == 7)
                last.then_inc(S["d_done"], 1)

            for i in range(N_TILES):
                out_proj(0, i)
            for i in range(N_TILES + 2):
                if i < N_TILES:
                    out_proj(1, i)
                if 1 <= i <= N_TILES:
                    t = i - 1
                    pe.wait_ge(S["h2_done"], t + 1)
                    if t >= 2:
                        pe.wait_ge(S["h2T_out"], t - 1)
                    for k in range(8):
                        last = pe.transpose(SC[:, t % 2, k * 128:(k + 1) * 128], h2[:, t % 2, k * 128:(k + 1) * 128], ident)
                    last.then_inc(S["h2T_done"], 1)
                if i >= 2:
                    t = i - 2
                    pe.wait_ge(S["h2T_out"], t + 1)
                    pe.wait_ge(S["router_in"], 4 * DMA)
                    if t >= 1:
                        pe.wait_ge(S["logit_done"], t)
                    for k in range(8):
                        last = pe.matmul(OB[:, 0:36], h2T[:, k, :], wr[:, k, :], start=(k == 0), stop=(k == 7))
                    last.then_inc(S["lg_done"], 1)

            pe.wait_ge(S["rstep"], R_BEFORE)
            pe.matmul(bank(0)[:, 0:256], const("strict"), mask[:].rearrange("p a b -> p (a b)"), start=True, stop=False)
            pe.matmul(bank(0)[:, 0:256], const("ones"), before[:, 0:8, :].rearrange("p a b -> p (a b)"),
                      start=False, stop=True).then_inc(S["pmm"], 1)
            pe.matmul(bank(1)[:, 0:32], const("ones"), before[:, 8, :], start=True, stop=True).then_inc(S["pmm"], 1)
            for q in range(16):
                pe.wait_ge(S["pick_done"], q + 1)
                pe.matmul(bank(2)[:, 0:256], pick[q % 2][:, :], keyid[q % 2][:, :], start=(q == 0), stop=(q == 15)
                          ).then_inc(S["pick_used"], 1)

            def turn_x():
                turn_rows(pe, xe, SC[:, 0, :], 8, 8).then_inc(S["xeT_done"], 1)

            def run_gate_up(e4):
                for c in range(4):
                    pe.wait_ge(S["gu_low"], e4 + (c + 1))
                    last = gate_up(pe, c)
                    last.then_inc(S["w_free_gu"], 1)

            def run_down(e2):
                for c in (4, 5):
                    pe.wait_ge(S["d_low"], e2 + (c - 3))
                    down(pe, c).then_inc(S["w_free_d"], 1)

            pe.wait_ge(S["xe_landed"], DMA)
            turn_x()
            pe.wait_ge(S["xeL_done"], 1)
            run_gate_up(0)
            pe.wait_ge(S["xe_landed"], 2 * DMA)
            turn_x()
            pe.wait_ge(S["hid_done"], 1)
            turn_rows(pe, hid, TB, 4, 4).then_inc(S["hidT_done"], 1)

            def expert_step(e, more):
                e2, e4, e16 = (e * 2, e * 4, e * 16) if isinstance(e, int) else (pe.snap(e * 2), pe.snap(e * 4), pe.snap(e * 16))
                pe.wait_ge(S["xeL_done"], e + 1)
                pe.wait_ge(S["hid_done"], e)
                run_gate_up(e4)
                if more:
                    pe.wait_ge(S["xe_landed"], e16 + 2 * DMA)
                    turn_x()
                pe.wait_ge(S["hidL_done"], e)
                pe.wait_ge(S["y_out"], e - 1 + FREE)
                run_down(e2 - 2)
                pe.wait_ge(S["hid_done"], e + 1)
                turn_rows(pe, hid, TB, 4, 4).then_inc(S["hidT_done"], 1)

            with pe.Fori(1, N_EXP - 1) as e:
                expert_step(e, True)
            expert_step(N_EXP - 1, False)
            pe.wait_ge(S["hidL_done"], N_EXP)
            pe.wait_ge(S["y_out"], N_EXP - 1 + FREE)
            run_down(2 * N_EXP - 2)
            pe.wait_ge(S["y_out"], N_EXP + FREE)

            def block_products(n, e, b):
                pe.wait_ge(S["xe_landed"], n * DMA + DMA * (N_EXP + 1))
                turn_x()
                pe.wait_ge(S["xeL_done"], n + (N_EXP + 1))
                pe.wait_ge(S["v_lo"], n * 6 + 6)
                for c in range(4):
                    gate_up(pe, c).then_inc(S["w_free_gu"], 1)
                pe.wait_ge(S["hid_done"], n + (N_EXP + 1))
                turn_rows(pe, hid, TB, 4, 4).then_inc(S["hidT_done"], 1)
                pe.wait_ge(S["hidL_done"], n + (N_EXP + 1))
                for c in (4, 5):
                    down(pe, c).then_inc(S["w_free_d"], 1)
                pe.wait_ge(S["y_out"], n + (N_EXP + 1) + FREE)

            overflow(pe, block_products)

        @block.scalar
        def _(act):
            for i in range(N_TILES):
                act.wait_ge(S[f"x_in{i // 2}"], DMA)
                if i:
                    act.wait_ge(S["x_sq_done"], i)
                act.activation(x_sq[:], x_all[:, i, :], ACT.Square, accum_out=x_ss[:, i:i + 1]).then_inc(S["x_sq_done"], 1)
            act.wait_ge(S["small_in"], 9 * DMA)
            for n in range(16):
                half, k = n // 8, n % 8
                act.wait_ge(S["xT_done"], n + 1)
                act.activation(hTH[:, k, half * 512:(half + 1) * 512], bank(n % 4), ACT.Copy,
                               scale=g1_cols[:, k:k + 1]).then_inc(S["hH_done"], 1)
            act.wait_ge(S["angle_done"], 1)
            act.activation(sin_t[:], ang[:], ACT.Sin).then_inc(S["trig_done"], 1)
            act.activation(cos_t[:], turns[:], ACT.Sin, scale=-1.0, bias=const("half_pi")).then_inc(S["trig_done"], 1)
            act.wait_ge(S["lam_step"], 2)
            act.activation(lam_e, lam_s, ACT.Exp).then_inc(S["lam_expd"], 1)

            def high(dst, src_, landed, value, done, n=1):
                act.wait_ge(landed, value)
                act.activation(dst, src_, ACT.Copy).then_inc(done, n)

            for k in range(8):
                high(wAH[:, k, :], wA_in[:, k, :], S["wA_landed"], 3 * DMA, S["wA_high"])

            with act.Fori(0, N_HEADS) as h:
                h8, h48, h64 = act.snap(h * 8), act.snap(h * 48), act.snap(h * 64)
                for s in range(N_STEPS):
                    (u1, i1), (u2, i2), (u3, i3) = tile_at(s - 1), tile_at(s - 2), tile_at(s - 3)
                    src_bank = PROJ[(s - 1) % 2]
                    if u1 == "A":
                        act.wait_ge(S["projA"], h8 + (i1 + 1))
                        act.wait_ge(S["ssA_done"], h8 + i1 + FREE)
                        act.activation(sqA[:], src_bank[:, 0:256], ACT.Square).then_inc(S["sqA_done"], 1)
                        act.activation(V[:, i1, :], src_bank[:, 256:384], ACT.Copy).then_inc(S["vA_done"], 1)
                    if u1 == "B":
                        par = i1 % 2
                        act.wait_ge(S["projB"], h8 + (i1 + 1) + FREE)
                        if i1 == 0:
                            act.wait_ge(S["head_consts"], h + 1)
                        act.wait_ge(S["ropedB"], h8 * 2 + 2 * i1 + FREE)
                        if i1 >= 2:
                            act.wait_ge(S["oB"], h8 + (i1 - 1))
                            act.wait_ge(S["sg_done"], h8 + (i1 - 1) + FREE)
                        act.activation(qkS[:, 0:2, :], src_bank[:, 0:128].rearrange("p (a b) -> p a b", a=2), ACT.Copy,
                                       scale=head_c[:, 0:1]).then_inc(S["qkS_done"], 1)
                        act.activation(qkS[:, 2:4, :], src_bank[:, 128:256].rearrange("p (a b) -> p a b", a=2), ACT.Copy,
                                       scale=head_c[:, 1:2]).then_inc(S["qkS_done"], 1)
                        act.activation(vg[:, par, :], src_bank[:, 256:512], ACT.Copy).then_inc(S["vg_done"], 1)
                        act.wait_ge(S["sg_done"], h8 + i1 + FREE)
                        act.activation(eg[:], src_bank[:, 384:512], ACT.Exp, scale=-1.0).then_inc(S["eg_done"], 1)
                    if u3 == "A":
                        act.wait_ge(S["oTA"], h8 + (i3 + 1))
                        act.activation(oT[:, DS(h, 1), i3 * 128:(i3 + 1) * 128].rearrange("p a b -> p (a b)"), TB[:, 0:128],
                                       ACT.Copy, scale=subln_scaled).then_inc(S["t_free"], 1)
                    if u3 == "B":
                        act.wait_ge(S["gTB"], h8 + (i3 + 1) + FREE)
                        act.activation(oT[:, DS(h + 4, 1), i3 * 128:(i3 + 1) * 128].rearrange("p a b -> p (a b)"), TB[:, 0:128],
                                       ACT.Copy).then_inc(S["t_free"], 1)
                    if u2 == "A":
                        nb = min(4, i2 + 1)
                        act.wait_ge(S["aT1"], h8 + (i2 + 1))
                        act.activation(aT[:, 0:nb, :].rearrange("p a b -> p (a b)"), TB[:, 0:nb * 128], ACT.Copy
                                       ).then_inc(S["t_free"], 1)
                    if u1 == "A":
                        act.wait_ge(S["qkTA"], h8 + (i1 + 1) + FREE)
                        act.activation(QH[:], TB[:, 0:128], ACT.Copy).then_inc(S["qkHA"], 1)
                        act.activation(KH[:, i1 * 128:(i1 + 1) * 128], TB[:, 128:256], ACT.Copy).then_inc(S["qkHA"], 1)
                    if u1 == "B":
                        act.wait_ge(S["qkTB"], h8 + (i1 + 1))
                        act.activation(qkT[:, i1 % 2, :], TB[:, 0:256], ACT.Copy).then_inc(S["t_free"], 1)
                    if u2 == "A":
                        act.wait_ge(S["pv_done"], h8 + (i2 + 1) + FREE)
                        act.activation(oN[:], OB[:, 0:128], ACT.Square, accum_out=ss_o).then_inc(S["o_sq"], 1)
                    unit, _i = tile_at(s)
                    if s % 8 in PREP and unit is not None:
                        ks = PREP[s % 8]
                        if unit == "A":
                            high(wBH[:, ks[0]:ks[-1] + 1, :], wB_in[:, ks[0]:ks[-1] + 1, :],
                                 S["wB_landed"], h64 + 4 * DMA, S["wB_high"], len(ks))
                        else:
                            high(wAH[:, ks[0]:ks[-1] + 1, :], wA_in[:, ks[0]:ks[-1] + 1, :],
                                 S["wA_landed"], h48 + 6 * DMA, S["wA_high"], len(ks))
                    if u1 == "A":
                        L = (i1 + 1) * 128
                        act.wait_ge(S["negged"], h8 + (i1 + 1))
                        if i1 == 0:
                            act.wait_ge(S["pv_done"], h8 + FREE)
                        for c in range(2):
                            act.activation(probs[:, c, 0:L], SC[:, c, 0:L], ACT.Exp, bias=negmax[:, c:c + 1], scale=0.125,
                                           accum_out=rowsum[:, c:c + 1]).then_inc(S["exped"], 1)

            def high_C(m_value, sub, piece):
                act.wait_ge(S[f"wC_landed{sub}"], m_value)
                act.activation(wCH[sub][:, piece * 8:piece * 8 + 8, :], wC_in[sub][:, piece * 8:piece * 8 + 8, :],
                               ACT.Copy).then_inc(S["wC_high"], 1)

            high_C(4 * DMA, 0, 0)
            high_C(4 * DMA, 0, 1)

            def merge_pair(j, last):
                j4, j8 = (j * 4, j * 8) if isinstance(j, int) else (act.snap(j * 4), act.snap(j * 8))
                j64 = j * 64 if isinstance(j, int) else act.snap(j * 64)
                for sub in range(2):
                    for th in range(2):
                        n = 2 * sub + th
                        act.wait_ge(S["gates_done"], j4 + (n + 1))
                        act.wait_ge(S["sig_mul"], j8 + 2 * n + FREE)
                        for g in range(2):
                            act.activation(sig[:, g, :], bank((4 if th == 0 else 0) + g), ACT.Exp, scale=-1.0
                                           ).then_inc(S["sig_exp"], 1)
                        if sub == 0:
                            high_C(j64 + 4 * DMA, 1, th)
                        elif not last:
                            high_C(j64 + 8 * DMA, 0, th)

            with act.Fori(0, 3) as j:
                merge_pair(j, False)
            merge_pair(3, True)
            for piece in range(2):
                high(wDH[0][:, piece * 4:piece * 4 + 4, :], wD_in[0][:, piece * 4:piece * 4 + 4, :], S["wD_landed0"], DMA, S["wD_high"])
            act.wait_ge(S["sig_mul"], 32 + FREE)
            for i in range(N_TILES):
                act.activation(mergedH[:, :, i * 128:(i + 1) * 128], merged[:, :, i * 128:(i + 1) * 128], ACT.Copy
                               ).then_inc(S["mH"], 1)
            for piece in range(2):
                high(wDH[1][:, piece * 4:piece * 4 + 4, :], wD_in[1][:, piece * 4:piece * 4 + 4, :], S["wD_landed1"], DMA, S["wD_high"])
            for i in range(N_TILES + 1):
                if i < N_TILES:
                    act.wait_ge(S["x2_done"], 9 + i)
                    if i:
                        act.wait_ge(S["n2_sq"], i)
                    act.activation(x2_sq[:], x2[:, i, :], ACT.Square, accum_out=n2[:, 0, i:i + 1]).then_inc(S["n2_sq"], 1)
                if i >= 1:
                    t = i - 1
                    act.wait_ge(S["h2T_done"], t + 1)
                    if t >= 1:
                        act.wait_ge(S["lg_done"], t)
                    act.activation(h2T[:].rearrange("p a b -> p (a b)"), SC[:, t % 2, :], ACT.Copy).then_inc(S["h2T_out"], 1)
            act.wait_ge(S["rstep"], R_GDIFF)
            act.activation(gexp[:], gdiff[:], ACT.Exp).then_inc(S["ract"], 1)
            act.wait_ge(S["rstep"], R_VDIFF)
            act.activation(vexp[:], vdiff[:], ACT.Exp).then_inc(S["ract"], 1)

            def high_slot(c, value):
                act.wait_ge(S[f"w_land{c}"], value)
                act.activation(w_high[c][:], w_in6[c][:], ACT.Copy).then_inc(S["gu_high" if c < 4 else "d_high"], 1)

            def x_high(value):
                act.wait_ge(S["xeT_done"], value)
                act.activation(xeH[:].rearrange("p a b -> p (a b)"), SC[:, 0, :], ACT.Copy).then_inc(S["xeH_done"], 1)

            def hid_high(value):
                act.wait_ge(S["hidT_done"], value)
                act.activation(hidH[:].rearrange("p a b -> p (a b)"), TB[:, :], ACT.Copy).then_inc(S["hidH_done"], 1)

            def gate_silu(e):
                act.wait_ge(S["w_free_gu"], e * 4 + 4)
                act.wait_ge(S["hid_done"], e)
                act.activation(silu[:], PROJ[0][:, :], ACT.Silu).then_inc(S["silu_done"], 1)

            for c in range(4):
                high_slot(c, DMA)
            x_high(1)
            gate_silu(0)
            x_high(2)
            for c in range(4):
                high_slot(c, 2 * DMA)
            hid_high(1)

            def expert_step(e, more):
                e16 = e * 16 if isinstance(e, int) else act.snap(e * 16)
                high_slot(4, e16)
                high_slot(5, e16)
                if more:
                    high_slot(0, e16 + 2 * DMA)
                gate_silu(e)
                if more:
                    x_high(e + 2)
                    for c in (1, 2, 3):
                        high_slot(c, e16 + 2 * DMA)
                act.wait_ge(S["w_free_d"], e * 2)
                if not isinstance(e, int) or e > 1:
                    act.wait_ge(S["scattered"], e16 - DMA)
                act.activation(y[:], SC[:, 1, :], ACT.Copy).then_inc(S["y_out"], 1)
                hid_high(e + 1)

            expert_step(1, True)
            with act.Fori(2, N_EXP - 1) as e:
                expert_step(e, True)
            expert_step(N_EXP - 1, False)
            high_slot(4, N_EXP * DMA)
            high_slot(5, N_EXP * DMA)
            act.wait_ge(S["w_free_d"], 2 * N_EXP)
            act.wait_ge(S["scattered"], DMA * (N_EXP - 1))
            act.activation(y[:], SC[:, 1, :], ACT.Copy).then_inc(S["y_out"], 1)

            def block_steps(n, e, b):
                act.wait_ge(S["v_w"], n * (6 * DMA) + 6 * DMA)
                for c in range(6):
                    act.activation(w_high[c][:], w_in6[c][:], ACT.Copy).then_inc(S["v_hi"], 1)
                x_high(n + (N_EXP + 1))
                act.wait_ge(S["w_free_gu"], n * 4 + 4 * (N_EXP + 1))
                act.activation(silu[:], PROJ[0][:, :], ACT.Silu).then_inc(S["silu_done"], 1)
                hid_high(n + (N_EXP + 1))
                act.wait_ge(S["w_free_d"], n * 2 + 2 * (N_EXP + 1))
                act.activation(y[:], SC[:, 1, :], ACT.Copy).then_inc(S["y_out"], 1)

            act.wait_ge(S["scattered"], DMA * N_EXP)
            overflow(act, block_steps)
            for i in range(N_TILES):
                act.wait_ge(S["res_done"], i + 1)
                act.dma_start(out_v[:, i, :], res[:, i % 2, :]).then_inc(S[f"out_stored{i % 2}"], DMA)

        @block.gpsimd
        def _(pool):
            mhalf = const("minus_half")
            pool.wait_ge(S["consts_in"], DMA)
            for i in range(N_TILES):
                pool.wait_ge(S["x_ms_done"], i + 1)
                pool.tensor_tensor(x_rstd[:, i:i + 1], x_ms[:, i:i + 1], mhalf[:, 0:1], ALU.pow).then_inc(S["x_rstd_done"], 1)
            pool.wait_ge(S["trig_done"], 2)
            with pool.Fori(0, N_HEADS) as h:
                h8 = pool.snap(h * 8)
                for s in range(N_STEPS):
                    (u1, i1), (u2, i2) = tile_at(s - 1), tile_at(s - 2)
                    if s == 3:
                        pool.wait_ge(S["qkS_done"], h8 * 2 + FREE)
                        pool.wait_ge(S["sT_done"], h8 + FREE)
                        lo = CONST_AT["ret_q"][0]
                        pool.tensor_copy(head_c[:], consts[:, lo:lo + 16].rearrange("p (a b) -> p b a", b=4)[:, DS(h, 1), :]
                                         .rearrange("p a b -> p (a b)")).then_inc(S["head_consts"], 1)
                    if u1 == "A":
                        pool.wait_ge(S["msA_done"], h8 + (i1 + 1))
                        pool.tensor_tensor(rstd_qk, ms_qk, mhalf[:, 0:4], ALU.pow).then_inc(S["rstdA_done"], 1)
                        x4 = qkA[:].rearrange("p (g d) -> p g d", g=4)[:, :, 0:16].rearrange("p g (a b) -> p g a b", a=2)
                        cos = cos_t[:, i1, 0:8].unsqueeze(1).unsqueeze(1).to_broadcast([P, 4, 2, 8])
                        sin = sin_t[:, i1, 0:8].unsqueeze(1).to_broadcast([P, 4, 8])
                        pool.wait_ge(S["normA_done"], h8 + (i1 + 1))
                        pool.wait_ge(S["ropedA"], h8 * 2 + 2 * i1 + FREE)
                        pool.tensor_tensor(rope_cos[:], x4, cos, ALU.mult).then_inc(S["ropeA_step"], 1)
                        pool.tensor_tensor(rope_sin[:, :, 0, :], x4[:, :, 1, :], sin, ALU.mult).then_inc(S["ropeA_step"], 1)
                        pool.tensor_tensor(rope_sin[:, :, 1, :], x4[:, :, 0, :], sin, ALU.mult).then_inc(S["ropeA_step"], 1)
                        pool.wait_ge(S["ropeA_step"], h * 24 + (3 * i1 + 3))
                        pool.tensor_tensor(x4[:, :, 0, :], rope_cos[:, :, 0, :], rope_sin[:, :, 0, :], ALU.subtract).then_inc(S["ropedA"], 1)
                        pool.tensor_tensor(x4[:, :, 1, :], rope_cos[:, :, 1, :], rope_sin[:, :, 1, :], ALU.add).then_inc(S["ropedA"], 1)
                    if u1 == "B":
                        sin = sin_t[:, i1, 8:72].unsqueeze(1).to_broadcast([P, 2, 64])
                        pool.wait_ge(S["qkS_done"], h8 * 2 + (2 * i1 + 2) + FREE)
                        pool.wait_ge(S["ropedB"], h8 * 2 + 2 * i1 + FREE)
                        pool.tensor_tensor(qkSin[:, 0:4:2, :], qkS[:, 1:4:2, :], sin, ALU.mult).then_inc(S["sinB"], 1)
                        pool.tensor_tensor(qkSin[:, 1:4:2, :], qkS[:, 0:4:2, :], sin, ALU.mult).then_inc(S["sinB"], 1)
                        pool.wait_ge(S["egr"], h8 + (i1 + 1))
                        pool.wait_ge(S["gated"], h8 + max(i1 - 1, 0) + FREE)
                        pool.tensor_tensor(sg[:, i1 % 2, :], vg[:, i1 % 2, 128:256], eg[:], ALU.mult).then_inc(S["sg_done"], 1)
                    if u2 == "A":
                        pool.wait_ge(S["o_ms"], h8 + (i2 + 1))
                        pool.tensor_tensor(rstd_o, ms_o, mhalf[:, 0:1], ALU.pow).then_inc(S["o_rstd"], 1)
                    if u2 == "B":
                        pool.wait_ge(S["bn_v"], h8 + (i2 + 1))
                        pool.tensor_tensor(bstat[:, 9:10], bstat[:, 8:9], mhalf[:, 0:1], ALU.pow).then_inc(S["bn_r"], 1)
                        if i2 == 0:
                            pool.wait_ge(S["gn_landed"], h * 32 + 32)
                        pool.wait_ge(S["onR_done"], h8 + (i2 + 1) + FREE)
                        pool.tensor_tensor(onR[:], onR[:], gn_rows[:, 0, :], ALU.mult).then_inc(S["gate_step"], 1)
                        pool.wait_ge(S["gate_step"], h8 * 2 + (2 * i2 + 1))
                        pool.tensor_tensor(onR[:], onR[:], gn_rows[:, 1, :], ALU.add).then_inc(S["gate_step"], 1)
                        pool.wait_ge(S["gate_step"], h8 * 2 + (2 * i2 + 2))
                        pool.wait_ge(S["gTB"], h8 + i2 + FREE)
                        pool.tensor_tensor(gatedR[:], onR[:], sg[:, i2 % 2, :], ALU.mult).then_inc(S["gated"], 1)
                    if u1 == "A":
                        L = (i1 + 1) * 128
                        pool.wait_ge(S["exped"], h8 * 2 + (2 * i1 + 2) + FREE)
                        pool.wait_ge(S["rowsum_inv"], h8 * 2 + (2 * i1 + 2))
                        pool.tensor_tensor(probs[:, 1, 0:L], probs[:, 1, 0:L], rrow[:, 1:2].to_broadcast([P, L]), ALU.mult
                                           ).then_inc(S["p1_scaled"], 1)
            for i in range(N_TILES):
                pool.wait_ge(S["n2_ms"], i + 1)
                pool.tensor_tensor(n2[:, 2, i:i + 1], n2[:, 1, i:i + 1], mhalf[:, 0:1], ALU.pow).then_inc(S["n2_rstd"], 1)

            def gather(col, chain, done):
                pool.tensor_copy(cur_gather[:], ids_gather[:, col]).then_inc(S["idx_copied"], 1)
                pool.wait_ge(S["idx_copied"], chain)
                pool.indirect_dma_start(out=xe[:], out_offset=None, in_=h2_dram,
                                        in_offset=bass.IndirectOffsetOnAxis(ap=cur_gather[:, 0:1], axis=0),
                                        bounds_check=1023, oob_is_err=False).then_inc(S[done], DMA)

            def scatter(col, chain, done):
                pool.tensor_copy(cur_scatter[:], ids_scatter[:, col]).then_inc(S["idx_copied"], 1)
                pool.wait_ge(S["idx_copied"], chain)
                pool.indirect_dma_start(out=y_dram, out_offset=bass.IndirectOffsetOnAxis(ap=cur_scatter[:, 0:1], axis=0),
                                        in_=y[:], in_offset=None,
                                        bounds_check=2047, oob_is_err=False).then_inc(S[done], DMA)

            pool.wait_ge(S["ids_done"], 1)
            for i in range(2):
                pool.wait_ge(S[f"h2_stored{i}"], 4 * DMA)
            pool.wait_ge(S["h2T_out"], 8)
            pool.memset(xe[:], 0.0).then_inc(S["xe_zero"], 1)
            pool.wait_ge(S["xe_zero"], 1)
            gather(slice(0, 1), 1, "xe_landed")
            pool.wait_ge(S["xeT_done"], 1)
            gather(slice(1, 2), 2, "xe_landed")

            def expert_step(e, more):
                pool.sem_clear(S["idx_copied"])
                n = 0
                if more:
                    pool.wait_ge(S["xeT_done"], e + 1)
                    gather(DS(e + 1, 1), 1, "xe_landed")
                    n = 1
                pool.wait_ge(S["y_out"], e + FREE)
                scatter(DS(e - 1, 1), n + 1, "scattered")

            with pool.Fori(1, N_EXP - 1) as e:
                expert_step(e, True)
            expert_step(N_EXP - 1, False)
            pool.wait_ge(S["y_out"], N_EXP + FREE)
            pool.wait_ge(S["scattered"], DMA * (N_EXP - 1))
            scatter(slice(N_EXP - 1, N_EXP), 2, "scattered")
            pool.wait_ge(S["scattered"], DMA * N_EXP)

            def block_moves(n, e, b):
                pool.sem_clear(S["idx_copied"])
                col = pool.snap(b * N_EXP + e)
                gather(DS(col, 1), 1, "xe_landed")
                pool.wait_ge(S["y_out"], n + (N_EXP + 1) + FREE)
                scatter(DS(col, 1), 2, "scattered")
                pool.wait_ge(S["scattered"], n * DMA + DMA * (N_EXP + 1))

            overflow(pool, block_moves)
            pool.memset(cur_gather[:], 0).then_inc(S["rows_stored"], 1)

        @block.vector
        def _(dve):
            for i in range(N_TILES + 1):
                if i < N_TILES:
                    dve.wait_ge(S["x_sq_done"], i + 1)
                    dve.tensor_scalar(x_ms[:, i:i + 1], x_ss[:, i:i + 1], 1.0 / 1024, EPS, ALU.mult, ALU.add
                                      ).then_inc(S["x_ms_done"], 1)
                if i >= 1:
                    dve.wait_ge(S["x_rstd_done"], i)
                    dve.tensor_scalar(x_all[:, i - 1, :], x_all[:, i - 1, :], x_rstd[:, i - 1:i], None, ALU.mult
                                      ).then_inc(S["xn_done"], 1)
            for n in range(16):
                half, k = n // 8, n % 8
                dve.wait_ge(S["hH_done"], n + 1)
                dst = (slice(None), k, slice(half * 512, (half + 1) * 512))
                dve.scalar_tensor_tensor(hTL[dst], bank(n % 4), g1_cols[:, k:k + 1], hTH[dst].bitcast(F32),
                                         ALU.mult, ALU.subtract).then_inc(S["hL_done"], 1)
            steps = [0]

            def step(ins, name="ang_step"):
                steps[0] += 1
                ins.then_inc(S[name], 1)
                dve.wait_ge(S[name], steps[0])

            dve.wait_ge(S["small_in"], 9 * DMA)
            step(dve.tensor_copy(posf, posi[:]))
            step(dve.tensor_tensor(ang[:], posf.unsqueeze(2).to_broadcast([P, 8, 72]),
                                   const("freq").unsqueeze(1).to_broadcast([P, 8, 72]), ALU.mult))
            step(dve.tensor_scalar(turns[:], ang[:], 1.0 / (2 * math.pi), MAGIC, ALU.mult, ALU.add))
            step(dve.tensor_scalar(turns[:], turns[:], -MAGIC, None, ALU.add))
            for part in TWO_PI:
                step(dve.scalar_tensor_tensor(ang[:], turns[:], -part, ang[:], ALU.mult, ALU.add))
            step(dve.tensor_scalar(ang[:], ang[:], PI_BELOW, -PI_BELOW, ALU.min, ALU.max))
            dve.scalar_tensor_tensor(turns[:], ang[:], -1.0, ang[:], ALU.mult, ALU.max).then_inc(S["angle_done"], 1)
            dve.tensor_tensor(lam_prod[:], lam_rows[:, 0:4:2, :], lam_rows[:, 1:4:2, :], ALU.mult).then_inc(S["lam_step"], 1)
            dve.wait_ge(S["lam_step"], 1)
            dve.tensor_reduce(lam_s, lam_prod[:], AX_X, ALU.add).then_inc(S["lam_step"], 1)
            dve.wait_ge(S["lam_expd"], 1)
            dve.scalar_tensor_tensor(lam, lam_e[:, 0:1], LAM_INIT, lam_e[:, 1:2], ALU.add, ALU.subtract).then_inc(S["lam_step"], 1)
            dve.tensor_scalar(subln_scaled, subln_col, 1.0 - LAM_INIT, None, ALU.mult).then_inc(S["lam_step"], 1)

            def low(dst, src_, high_, ready, value, done, n=1):
                dve.wait_ge(ready, value)
                dve.tensor_tensor(dst, src_, high_.bitcast(F32), ALU.subtract).then_inc(done, n)

            for k in range(8):
                low(wAL[:, k, :], wA_in[:, k, :], wAH[:, k, :], S["wA_high"], k + 1, S["wA_low"])

            with dve.Fori(0, N_HEADS) as h:
                h8, h7 = dve.snap(h * 8), dve.snap(h * 7)
                for s in range(N_STEPS):
                    (u1, i1), (u2, i2) = tile_at(s - 1), tile_at(s - 2)
                    src_bank = PROJ[(s - 1) % 2]
                    if u1 == "A":
                        dve.wait_ge(S["sqA_done"], h8 + (i1 + 1))
                        dve.tensor_reduce(ss_qk, sqA[:].rearrange("p (g d) -> p g d", g=4), AX_X, ALU.add).then_inc(S["ssA_done"], 1)
                        dve.wait_ge(S["ssA_done"], h8 + (i1 + 1) + FREE)
                        dve.tensor_scalar(ms_qk, ss_qk, 1.0 / 64, EPS, ALU.mult, ALU.add).then_inc(S["msA_done"], 1)
                    if u1 == "B":
                        cos = cos_t[:, i1, 8:72].unsqueeze(1).to_broadcast([P, 4, 64])
                        dve.wait_ge(S["qkS_done"], h8 * 2 + (2 * i1 + 2) + FREE)
                        dve.tensor_tensor(qkCos[:], qkS[:], cos, ALU.mult).then_inc(S["cosB"], 1)
                        dve.wait_ge(S["eg_done"], h8 + (i1 + 1) + FREE)
                        dve.tensor_scalar(eg[:], eg[:], 1.0, None, ALU.add).then_inc(S["eg1"], 1)
                        dve.wait_ge(S["eg1"], h8 + (i1 + 1))
                        dve.reciprocal(eg[:], eg[:]).then_inc(S["egr"], 1)
                        dve.wait_ge(S["sinB"], h8 * 2 + (2 * i1 + 2))
                        if i1:
                            dve.wait_ge(S["kv_done"], h7 + i1)
                        dve.tensor_tensor(qkR[:, 0:4:2, :], qkCos[:, 0:4:2, :], qkSin[:, 0:4:2, :], ALU.subtract).then_inc(S["ropedB"], 1)
                        dve.tensor_tensor(qkR[:, 1:4:2, :], qkCos[:, 1:4:2, :], qkSin[:, 1:4:2, :], ALU.add).then_inc(S["ropedB"], 1)
                    if u1 == "A":
                        dve.wait_ge(S["rstdA_done"], h8 + (i1 + 1))
                        dve.wait_ge(S["vA_done"], h8 + (i1 + 1))
                        dve.wait_ge(S["qkTA"], h8 + i1 + FREE)
                        for g in range(4):
                            last = dve.scalar_tensor_tensor(qkA[:, g * 64:(g + 1) * 64], src_bank[:, g * 64:(g + 1) * 64],
                                                            rstd_qk[:, g:g + 1], gains[:, g // 2, :], ALU.mult, ALU.mult)
                        last.then_inc(S["normA_done"], 1)
                    if u2 == "A" and i2 >= 4:
                        dve.wait_ge(S["aT2"], h * 4 + (i2 - 3))
                        dve.tensor_copy(aT[:, 4:i2 + 1, :].rearrange("p a b -> p (a b)"), TB[:, 0:(i2 - 3) * 128]
                                        ).then_inc(S["t_free"], 1)
                    if u1 == "A":
                        dve.wait_ge(S["qkHA"], h8 * 2 + (2 * i1 + 2))
                        keys = slice(i1 * 128, (i1 + 1) * 128)
                        dve.tensor_tensor(QL[:], TB[:, 0:128], QH[:].bitcast(F32), ALU.subtract)
                        dve.tensor_tensor(KL[:, keys], TB[:, 128:256], KH[:, keys].bitcast(F32), ALU.subtract
                                          ).then_inc(S["t_free"], 1)
                    if u2 == "B":
                        dve.wait_ge(S["oB"], h8 + (i2 + 1))
                        dve.bn_stats(bstat[:, 0:6], OB[:, 0:128]).then_inc(S["bn_s"], 1)
                        dve.wait_ge(S["bn_s"], 1)
                        dve.wait_ge(S["bn_s"], h8 + (i2 + 1))
                        dve.bn_aggr(bstat[:, 6:8], bstat[:, 0:6]).then_inc(S["bn_a"], 1)
                        dve.wait_ge(S["bn_a"], h8 + (i2 + 1))
                        dve.tensor_scalar(bstat[:, 8:9], bstat[:, 7:8], EPS, None, ALU.add).then_inc(S["bn_v"], 1)
                    if u2 == "A":
                        dve.wait_ge(S["o_sq"], h8 + (i2 + 1))
                        dve.tensor_scalar(ms_o, ss_o, 1.0 / 128, EPS, ALU.mult, ALU.add).then_inc(S["o_ms"], 1)
                    if u1 == "B" and i1 < N_TILES - 1:
                        dve.wait_ge(S["kv_done"], h7 + (i1 + 1))
                        if i1 == 0:
                            dve.tensor_copy(U[:, 1, :], bank(2)[:, 0:128]).then_inc(S["U_done"], 1)
                        else:
                            dve.wait_ge(S["U_done"], h7 + i1 + FREE)
                            dve.scalar_tensor_tensor(U[:, (i1 + 1) % 2, :], U[:, i1 % 2, :], head_c[:, 2:3], bank(2)[:, 0:128],
                                                     ALU.mult, ALU.add).then_inc(S["U_done"], 1)
                    unit, _i = tile_at(s)
                    if s % 8 in PREP and unit is not None:
                        ks = PREP[s % 8]
                        kk = slice(ks[0], ks[-1] + 1)
                        if unit == "A":
                            low(wBL[:, kk, :], wB_in[:, kk, :], wBH[:, kk, :], S["wB_high"], h8 + kk.stop, S["wB_low"], len(ks))
                        else:
                            low(wAL[:, kk, :], wA_in[:, kk, :], wAH[:, kk, :], S["wA_high"], h8 + (8 + kk.stop), S["wA_low"], len(ks))
                    if u2 == "A":
                        dve.wait_ge(S["o_rstd"], h8 + (i2 + 1))
                        dve.tensor_scalar(oN[:], OB[:, 0:128], rstd_o, None, ALU.mult).then_inc(S["oN_done"], 1)
                    if u2 == "B":
                        dve.wait_ge(S["bn_r"], h8 + (i2 + 1))
                        dve.wait_ge(S["gated"], h8 + i2 + FREE)
                        dve.tensor_scalar(onR[:], OB[:, 0:128], bstat[:, 6:7], bstat[:, 9:10], ALU.subtract, ALU.mult
                                          ).then_inc(S["onR_done"], 1)
                    if u1 == "A":
                        L = (i1 + 1) * 128
                        dve.wait_ge(S["scored"], h8 + (i1 + 1))
                        dve.tensor_tensor(SC[:, :, L - 128:L], SC[:, :, L - 128:L],
                                          const("causal").unsqueeze(1).to_broadcast([P, 2, 128]), ALU.add).then_inc(S["masked"], 1)
                        dve.wait_ge(S["masked"], h8 + (i1 + 1))
                        dve.tensor_reduce(rowmax, SC[:, :, 0:L], AX_X, ALU.max).then_inc(S["maxed"], 1)
                        dve.wait_ge(S["maxed"], h8 + (i1 + 1))
                        dve.tensor_scalar(negmax, rowmax, -0.125, None, ALU.mult).then_inc(S["negged"], 1)
                        dve.wait_ge(S["exped"], h8 * 2 + (2 * i1 + 2) + FREE)
                        dve.reciprocal(rrow, rowsum).then_inc(S["rowsum_inv"], 1)
                        dve.wait_ge(S["rowsum_inv"], h8 * 2 + (2 * i1 + 1))
                        dve.tensor_tensor(rrow[:, 1:2], rrow[:, 1:2], lam, ALU.mult).then_inc(S["rowsum_inv"], 1)
                        dve.wait_ge(S["p1_scaled"], h8 + (i1 + 1))
                        dve.scalar_tensor_tensor(probs[:, 0, 0:L], probs[:, 0, 0:L], rrow[:, 0:1], probs[:, 1, 0:L],
                                                 ALU.mult, ALU.subtract).then_inc(S["probs_done"], 1)
                    if u1 == "B":
                        dve.wait_ge(S["st_done"], h8 + (i1 + 1))
                        dve.scalar_tensor_tensor(sT[:], bank(0)[:, 0:128], head_c[:, 3:4], const("tri"), ALU.mult, ALU.mult
                                                 ).then_inc(S["sT_done"], 1)

            def low_C(value, sub, piece):
                dve.wait_ge(S["wC_high"], value)
                r = slice(piece * 8, piece * 8 + 8)
                dve.tensor_tensor(wCL[sub][:, r, :], wC_in[sub][:, r, :], wCH[sub][:, r, :].bitcast(F32), ALU.subtract
                                  ).then_inc(S["wC_low"], 1)

            low_C(1, 0, 0)
            low_C(2, 0, 1)

            def merge_pair(j, last):
                j4, j8 = (j * 4, j * 8) if isinstance(j, int) else (dve.snap(j * 4), dve.snap(j * 8))
                for sub in range(2):
                    for th in range(2):
                        n = 2 * sub + th
                        b0 = 4 if th == 0 else 0
                        dve.wait_ge(S["sig_exp"], j8 + (2 * n + 2))
                        dve.tensor_scalar(sig[:], sig[:], 1.0, None, ALU.add).then_inc(S["sig_one"], 1)
                        dve.wait_ge(S["sig_one"], j4 + (n + 1))
                        dve.reciprocal(sig[:], sig[:]).then_inc(S["sig_inv"], 1)
                        dve.wait_ge(S["sig_inv"], j4 + (n + 1))
                        dve.wait_ge(S["ys_done"], j4 + (n + 1))
                        for g in range(2):
                            dve.tensor_tensor(sig[:, g, :], sig[:, g, :], bank(b0 + 2 + g), ALU.mult).then_inc(S["merged_step"], 1)
                        dve.wait_ge(S["merged_step"], j8 + (2 * n + 2))
                        m = 2 * j + sub
                        dve.tensor_tensor(merged[:, DS(m, 1), th * 512:(th + 1) * 512].rearrange("p a b -> p (a b)"),
                                          sig[:, 0, :], sig[:, 1, :], ALU.add).then_inc(S["sig_mul"], 2)
                        if sub == 0:
                            low_C(j4 + (3 + th), 1, th)
                        elif not last:
                            low_C(j4 + (5 + th), 0, th)

            with dve.Fori(0, 3) as j:
                merge_pair(j, False)
            merge_pair(3, True)
            for piece in range(2):
                r = slice(piece * 4, piece * 4 + 4)
                low(wDL[0][:, r, :], wD_in[0][:, r, :], wDH[0][:, r, :], S["wD_high"], piece + 1, S["wD_low"])

            def add_residual(n, i):
                cnt = 8 * n + i
                cols = slice(n * 512, n * 512 + 512)
                if cnt == 0:
                    dve.wait_ge(S["x2_in"], DMA)
                dve.wait_ge(S["d_done"], cnt + 1)
                dve.tensor_tensor(x2[:, i, cols], bank(4 + cnt % 3), x2[:, i, cols], ALU.add).then_inc(S["x2_done"], 1)

            for i in range(N_TILES):
                dve.wait_ge(S["mH"], i + 1)
                tok = slice(i * 128, i * 128 + 128)
                dve.tensor_tensor(mergedL[:, :, tok], merged[:, :, tok], mergedH[:, :, tok].bitcast(F32), ALU.subtract
                                  ).then_inc(S["mL"], 1)
                if i >= 2:
                    add_residual(0, i - 2)
            for piece in range(2):
                r = slice(piece * 4, piece * 4 + 4)
                low(wDL[1][:, r, :], wD_in[1][:, r, :], wDH[1][:, r, :], S["wD_high"], piece + 3, S["wD_low"])
            add_residual(0, 6)
            add_residual(0, 7)

            dve.wait_ge(S["g2_in"], DMA)
            dve.wait_ge(S["router_in"], 4 * DMA)
            for i in range(N_TILES + 2):
                if i < N_TILES:
                    add_residual(1, i)
                    dve.wait_ge(S["n2_sq"], i + 1)
                    dve.tensor_scalar(n2[:, 1, i:i + 1], n2[:, 0, i:i + 1], 1.0 / 1024, EPS, ALU.mult, ALU.add
                                      ).then_inc(S["n2_ms"], 1)
                    dve.wait_ge(S["n2_rstd"], i + 1)
                    if i >= 2:
                        dve.wait_ge(S[f"h2_stored{i % 2}"], DMA * (i // 2))
                        dve.wait_ge(S["h2T_done"], i - 1)
                    dve.scalar_tensor_tensor(h2[:, i % 2, :], x2[:, i, :], n2[:, 2, i:i + 1], g2_row[:], ALU.mult, ALU.mult
                                             ).then_inc(S["h2_done"], 1)
                if i >= 2:
                    dve.wait_ge(S["lg_done"], i - 1)
                    dve.tensor_tensor(logits[:, i - 2, :], OB[:, 0:36], br[:], ALU.add).then_inc(S["logit_done"], 1)

            steps[0] = 0

            def rstep(ins):
                step(ins, "rstep")

            def b3(ap, shape):
                return ap.to_broadcast(shape)

            iota8 = const("iota_exp8").unsqueeze(1).to_broadcast([P, 8, 8])
            iota4 = const("iota_grp").unsqueeze(1).to_broadcast([P, 8, 4])
            dve.wait_ge(S["logit_done"], 8)
            gl = logits[:, :, 0:4]
            rstep(dve.tensor_reduce(gmax[:], gl, AX_X, ALU.max))
            rstep(dve.tensor_tensor(gdiff[:], gl, gmax[:].unsqueeze(2).to_broadcast([P, 8, 4]), ALU.subtract))
            assert steps[0] == R_GDIFF
            rstep(dve.tensor_scalar(gpen[:], gdiff[:], 0.0, 8.0, ALU.is_lt, ALU.mult))
            rstep(dve.tensor_tensor(gpen[:], gpen[:], iota4, ALU.add))
            rstep(dve.tensor_reduce(gidx[:], gpen[:], AX_X, ALU.min))
            rstep(dve.tensor_tensor(goh[:], gidx[:].unsqueeze(2).to_broadcast([P, 8, 4]), iota4, ALU.is_equal))
            for g in range(4):
                rstep(dve.tensor_tensor(elsel[:, g, :, :], logits[:, :, 4 + 8 * g:12 + 8 * g],
                                        goh[:, :, g:g + 1].to_broadcast([P, 8, 8]), ALU.mult))
            rstep(dve.tensor_tensor(esum[:], elsel[:, 0:2, :, :], elsel[:, 2:4, :, :], ALU.add))
            rstep(dve.tensor_tensor(el8[:], esum[:, 0, :, :], esum[:, 1, :, :], ALU.add))

            def best(values, c):
                rstep(dve.tensor_reduce(vtop[:, c, :], values[:], AX_X, ALU.max))
                rstep(dve.tensor_tensor(epen[:], values[:], vtop[:, c, :].unsqueeze(2).to_broadcast([P, 8, 8]), ALU.is_lt))
                rstep(dve.scalar_tensor_tensor(epen[:], epen[:], 16.0, iota8, ALU.mult, ALU.add))
                rstep(dve.tensor_reduce(eidx[:, c, :], epen[:], AX_X, ALU.min))

            best(el8, 0)
            rstep(dve.tensor_tensor(eoh[:], eidx[:, 0, :].unsqueeze(2).to_broadcast([P, 8, 8]), iota8, ALU.is_equal))
            rstep(dve.scalar_tensor_tensor(el8b[:], eoh[:], BIG_NEG, el8[:], ALU.mult, ALU.add))
            best(el8b, 1)
            rstep(dve.tensor_tensor(vdiff[:], vtop[:, 1, :], vtop[:, 0, :], ALU.subtract))
            assert steps[0] == R_VDIFF, steps[0]
            for c in range(2):
                rstep(dve.scalar_tensor_tensor(eglob[:, c, :], gidx[:], 8.0, eidx[:, c, :], ALU.mult, ALU.add))
            for c in range(2):
                rstep(dve.tensor_tensor(oh[:, c, :, :], eglob[:, c, :].unsqueeze(2).to_broadcast([P, 8, 32]),
                                        const("iota", 0, 32).unsqueeze(1).to_broadcast([P, 8, 32]), ALU.is_equal))
            rstep(dve.tensor_tensor(mask[:], oh[:, 0, :, :], oh[:, 1, :, :], ALU.add))
            rstep(dve.memset(before[:, 0, :], 0.0))
            for i in range(8):
                rstep(dve.tensor_tensor(before[:, i + 1, :], before[:, i, :], mask[:, i, :], ALU.add))
            assert steps[0] == R_BEFORE, steps[0]
            dve.wait_ge(S["ract"], 2)
            rstep(dve.tensor_reduce(gsum[:], gexp[:], AX_X, ALU.add))
            rstep(dve.reciprocal(pgrp[:], gsum[:]))
            rstep(dve.tensor_scalar(vden[:], vexp[:], 1.0, None, ALU.add))
            rstep(dve.reciprocal(vden[:], vden[:]))
            rstep(dve.tensor_tensor(wsel[:, 0, :], pgrp[:], vden[:], ALU.mult))
            rstep(dve.tensor_tensor(wsel[:, 1, :], wsel[:, 0, :], vexp[:], ALU.mult))
            dve.wait_ge(S["pmm"], 2)
            for c in range(2):
                rstep(dve.tensor_tensor(posm[:, c, :, :], oh[:, c, :, :],
                                        bank(0)[:, 0:256].rearrange("p (a b) -> p a b", a=8), ALU.mult))
            rstep(dve.tensor_reduce(pos[:].rearrange("p a b -> p (a b)"), posm[:].rearrange("p a b c -> p (a b) c"), AX_X, ALU.add))
            rstep(dve.tensor_copy(pos_i[:], pos[:]))
            rstep(dve.tensor_scalar(slot_i[:], pos_i[:], BLOCK - 1, None, ALU.bitwise_and))
            rstep(dve.tensor_scalar(blk_i[:], pos_i[:], BLOCK_BITS, None, ALU.logical_shift_right))
            rstep(dve.tensor_copy(slotf[:], slot_i[:]))
            rstep(dve.tensor_copy(blkf[:], blk_i[:]))
            rstep(dve.scalar_tensor_tensor(key[:], blkf[:], 32.0, eglob[:], ALU.mult, ALU.add))
            rstep(dve.tensor_copy(counts_f[:, 0:32], bank(1)[:, 0:32]))
            rstep(dve.tensor_reduce(counts_f[:, 32:33], counts_f[:, 0:32], AX_X, ALU.max))
            rstep(dve.tensor_copy(counts_i[:], counts_f[:]))
            for q in range(16):
                c, i = q // 8, q % 8
                if q >= 2:
                    dve.wait_ge(S["pick_used"], q - 1)
                dve.tensor_scalar(pick[q % 2][:], const("iota", 0, 128), slotf[:, c, i:i + 1], None, ALU.is_equal)
                dve.tensor_scalar(keyid[q % 2][:], const("iota"), key[:, c, i:i + 1], const("token1", q, q + 1),
                                  ALU.is_equal, ALU.mult).then_inc(S["pick_done"], 1)
            dve.wait_ge(S["pick_used"], 16)
            rstep(dve.tensor_scalar(padded[:], bank(2)[:, 0:256], 0.0, 4096.0, ALU.is_equal, ALU.mult))
            rstep(dve.scalar_tensor_tensor(zf[:], bank(2)[:, 0:256], -1.0, padded[:], ALU.add, ALU.add))
            rstep(dve.tensor_copy(ids_scatter[:], zf[:]))
            dve.tensor_scalar(ids_gather[:], ids_scatter[:], 3071, None, ALU.bitwise_and).then_inc(S["ids_done"], 1)

            def low_slot(c, value):
                dve.wait_ge(S["gu_high" if c < 4 else "d_high"], value)
                dve.tensor_tensor(w_low[c][:], w_in6[c][:], w_high[c][:].bitcast(F32), ALU.subtract
                                  ).then_inc(S["gu_low" if c < 4 else "d_low"], 1)

            def x_low(value):
                dve.wait_ge(S["xeH_done"], value)
                dve.tensor_tensor(xeL[:].rearrange("p a b -> p (a b)"), SC[:, 0, :],
                                  xeH[:].rearrange("p a b -> p (a b)").bitcast(F32), ALU.subtract).then_inc(S["xeL_done"], 1)

            def hidden(value):
                dve.wait_ge(S["silu_done"], value)
                dve.tensor_tensor(hid[:], silu[:], PROJ[1][:, :], ALU.mult).then_inc(S["hid_done"], 1)

            def hid_low(value):
                dve.wait_ge(S["hidH_done"], value)
                dve.tensor_tensor(hidL[:].rearrange("p a b -> p (a b)"), TB[:, :],
                                  hidH[:].rearrange("p a b -> p (a b)").bitcast(F32), ALU.subtract).then_inc(S["hidL_done"], 1)

            for c in range(4):
                low_slot(c, c + 1)
            x_low(1)
            hidden(1)
            x_low(2)
            for c in range(4):
                low_slot(c, 4 + c + 1)
            hid_low(1)

            def expert_step(e, more):
                e4, e2 = (e * 4, e * 2) if isinstance(e, int) else (dve.snap(e * 4), dve.snap(e * 2))
                low_slot(4, e2 - 1)
                low_slot(5, e2)
                if more:
                    low_slot(0, e4 + 5)
                hidden(e + 1)
                if more:
                    x_low(e + 2)
                    for c in (1, 2, 3):
                        low_slot(c, e4 + (5 + c))
                hid_low(e + 1)

            with dve.Fori(1, N_EXP - 1) as e:
                expert_step(e, True)
            expert_step(N_EXP - 1, False)
            low_slot(4, 2 * N_EXP - 1)
            low_slot(5, 2 * N_EXP)

            def block_lows(n, e, b):
                for c in range(6):
                    dve.wait_ge(S["v_hi"], n * 6 + (c + 1))
                    dve.tensor_tensor(w_low[c][:], w_in6[c][:], w_high[c][:].bitcast(F32), ALU.subtract).then_inc(S["v_lo"], 1)
                x_low(n + (N_EXP + 1))
                hidden(n + (N_EXP + 1))
                hid_low(n + (N_EXP + 1))

            dve.wait_ge(S["scattered"], DMA * N_EXP)
            overflow(dve, block_lows)
            for i in range(N_TILES):
                b = i % 2
                dve.wait_ge(S[f"comb_in{b}"], 2 * DMA * (i // 2 + 1))
                if i >= 2:
                    dve.wait_ge(S[f"out_stored{b}"], DMA * (i // 2))
                dve.scalar_tensor_tensor(res[:, b, :], comb[:, b, 0, :], wsel[:, 0, i:i + 1], x2[:, i, :], ALU.mult, ALU.add
                                         ).then_inc(S["comb_mid"], 1)
                dve.wait_ge(S["comb_mid"], i + 1)
                dve.scalar_tensor_tensor(res[:, b, :], comb[:, b, 1, :], wsel[:, 1, i:i + 1], res[:, b, :], ALU.mult, ALU.add
                                         ).then_inc(S["res_done"], 1)


R_GDIFF, R_VDIFF, R_BEFORE = 2, 23, 37
BLOCK_BITS = 7
MAGIC = 1.5 * 2.0 ** 23
TWO_PI = (6.28125, 0.001934051513671875, 1.2556659146e-6)
PI_BELOW = 3.1415925

_INS = ["x", "positions", "norm1_g", "w_in", "q_norm_g", "k_norm_g", "lambda_q1", "lambda_k1", "lambda_q2", "lambda_k2",
        "diff_subln_g", "ret_gn_g", "ret_gn_b", "w_branch_a", "w_branch_b", "w_out", "norm2_g",
        "w_group_router", "b_group_router", "w_expert_router", "b_expert_router", "w_gate", "w_up", "w_down"]


def kernel(**inputs):
    import concourse.bacc as bacc
    from concourse.bass_utils import run_bass_kernel_spmd

    nc = bacc.Bacc("TRN2", target_bir_lowering=False, num_devices=1)
    arrays, tensors = {}, {}
    for name in _INS:
        arrays[f"in_{name}"] = np.ascontiguousarray(inputs[name])
    arrays["in_consts"] = constants()
    for full, a in arrays.items():
        tensors[full[3:]] = nc.dram_tensor(full, a.shape, mybir.dt.from_np(a.dtype), kind="ExternalInput").ap()
    tensors["out"] = nc.dram_tensor("out_0", (1, 1024, 1024), F32, kind="ExternalOutput").ap()
    decoder_layer(nc, tensors)
    r = run_bass_kernel_spmd(nc, [arrays], core_ids=[0])
    return r.results[0]["out_0"]
```

```python
from contextlib import ExitStack
import math

import numpy as np

import concourse.bass as bass
from concourse import mybir

ALU = mybir.AluOpType
ACT = mybir.ActivationFunctionType
AX_X = mybir.AxisListType.X
F32 = mybir.dt.float32
F32R = mybir.dt.float32r
I32 = mybir.dt.int32
DS = bass.ds

P = 128
EPS = 1e-6
BIG_NEG = -1.0e30
QA, KA, VA, QB, KB, VB, GB, GATE_A, GATE_B = 0, 512, 1024, 1536, 2048, 2560, 3072, 3584, 4608
N_TILES = 8
N_KD = 8
N_HEADS = 4
N_EXP = 32
N_GRP = 4
EPG = 8
FF = 512
LAM_INIT = 0.8 - 0.6 * math.exp(-0.3 * 0)
BLOCK = 128
MAX_BLOCKS = 8
FREE = 1
SIG_FREE = 3
DMA = 16

CONST_WIDTHS = [
    ("ident", 128), ("tri", 128), ("causal", 128), ("strict", 128), ("ones", 128), ("iota", 256),
    ("freq", 72), ("ret_q", 4), ("ret_k", 4), ("ret_g", 4), ("ret_ginv", 4),
    ("token1", 16), ("minus_half", 16), ("half_pi", 1), ("iota_grp", 4), ("iota_exp8", 8),
]
CONST_AT = {}
_at = 0
for _name, _width in CONST_WIDTHS:
    CONST_AT[_name] = (_at, _at + _width)
    _at += _width
N_CONST = _at


def constants():
    p = np.arange(P)
    c = {}
    c["ident"] = np.eye(P)
    c["tri"] = (p[:, None] <= p[None, :]).astype(np.float64)
    c["causal"] = np.where(p[None, :] <= p[:, None], 0.0, BIG_NEG)
    c["strict"] = (p[:, None] < p[None, :]).astype(np.float64)
    c["ones"] = np.ones((P, P))
    c["iota"] = np.tile(np.arange(256.0), (P, 1))
    fa = np.power(np.float32(500000.0), (-2.0 * np.arange(8, dtype=np.float32) / np.float32(16)).astype(np.float32))
    fr = np.power(np.float32(10000.0), (-2.0 * np.arange(64, dtype=np.float32) / np.float32(128)).astype(np.float32))
    c["freq"] = np.tile(np.concatenate([fa, fr]), (P, 1))
    gamma = 1.0 - 2.0 ** (-5.0 - np.arange(4.0))
    c["ret_q"] = gamma[None, :] ** (p[:, None] + 1.0 + P)
    c["ret_k"] = gamma[None, :] ** (-(p[:, None] + 1.0)) * P ** -0.5
    c["ret_g"] = np.tile(gamma ** P, (P, 1))
    c["ret_ginv"] = np.tile(gamma ** -P, (P, 1))
    c["token1"] = (p[:, None] + 1.0) + 128.0 * np.arange(16)[None, :]
    c["minus_half"] = np.full((P, 16), -0.5)
    c["half_pi"] = np.full((P, 1), np.pi / 2)
    c["iota_grp"] = np.tile(np.arange(4.0), (P, 1))
    c["iota_exp8"] = np.tile(np.arange(8.0), (P, 1))
    return np.concatenate([c[name] for name, _ in CONST_WIDTHS], axis=1).astype(np.float32)


def split3(pe, out, left, right, start, stop):
    (lh, ll), (rh, rl) = left, right
    pe.matmul(out, lh, rh, start=start, stop=False)
    pe.matmul(out, lh, rl, start=False, stop=False)
    return pe.matmul(out, ll, rh, start=False, stop=stop)




def decoder_layer(nc, T):
    with ExitStack() as ctx:
        limit = nc.sbuf_usable_end
        cursor = [(nc.sbuf_base + 63) // 64 * 64]

        def place(size):
            at = cursor[0]
            cursor[0] = (at + size + 31) // 32 * 32
            assert cursor[0] <= limit, (cursor[0], limit)
            return at

        def sb(name, shape, dt=F32, at=None):
            size = int(np.prod(shape[1:])) * 4
            return nc.alloc_sbuf_tensor_at(name, shape, dt, offset=place(size) if at is None else at)

        def psum(name, shape):
            return ctx.enter_context(nc.psum_tensor(name, shape, F32))

        def sem(name):
            return ctx.enter_context(nc.semaphore(name))

        KIB = 1024

        consts = sb("consts", [P, N_CONST])

        def const(name, a=0, b=None):
            lo, hi = CONST_AT[name]
            return consts[:, lo + a:(hi if b is None else lo + b)]

        ident = const("ident")
        small = sb("small", [P, 64])
        g1_cols = small[:, 0:8]
        subln_col = small[:, 8:9]
        subln_scaled = small[:, 9:10]
        lam = small[:, 10:11]
        lam_e = small[:, 12:14]
        lam_s = small[:, 14:16]
        x_ss = small[:, 16:24]
        x_rstd = small[:, 24:32]
        x_ms = small[:, 32:40]
        posf = small[:, 40:48]
        posi = sb("posi", [P, 8], I32)

        R_HT, R_A, R_B, R_OT = place(64 * KIB), place(24 * KIB), place(32 * KIB), place(32 * KIB)
        R_WORK = cursor[0]

        hTH = sb("hTH", [P, N_KD, 1024], F32R, at=R_HT)
        hTL = sb("hTL", [P, N_KD, 1024], F32R, at=R_HT + 32 * KIB)
        wA_in = sb("wA_in", [P, N_KD, 384], F32, at=R_A)
        wAL = sb("wAL", [P, N_KD, 384], F32R, at=R_A)
        wAH = sb("wAH", [P, N_KD, 384], F32R, at=R_A + 12 * KIB)
        wB_in = sb("wB_in", [P, N_KD, 512], F32, at=R_B)
        wBL = sb("wBL", [P, N_KD, 512], F32R, at=R_B)
        wBH = sb("wBH", [P, N_KD, 512], F32R, at=R_B + 16 * KIB)
        x_all = sb("x_all", [P, N_TILES, 1024], F32, at=R_B)
        oT = sb("oT", [P, 8, 1024], F32, at=R_OT)
        x_sq = sb("x_sq", [P, 1024], F32, at=R_OT)
        lam_rows = sb("lam_rows", [P, 4, 64], F32, at=R_OT + 4 * KIB)
        lam_prod = sb("lam_prod", [P, 2, 64], F32, at=R_OT + 6 * KIB)
        ang = sb("ang", [P, N_TILES, 72], F32, at=R_OT + 8 * KIB)
        turns = sb("turns", [P, N_TILES, 72], F32, at=R_OT + 12 * KIB)

        sin_t = sb("sin_t", [P, N_TILES, 72])
        cos_t = sb("cos_t", [P, N_TILES, 72])
        gains = sb("gains", [P, 2, 64])
        gn_rows = sb("gn_rows", [P, 2, 128])
        KH = sb("KH", [P, 1024], F32R)
        KL = sb("KL", [P, 1024], F32R)
        QH = sb("QH", [P, 128], F32R)
        QL = sb("QL", [P, 128], F32R)
        V = sb("V", [P, N_TILES, 128])
        probs = sb("probs", [P, 2, 1024])
        aT = sb("aT", [P, N_TILES, 128])
        sqA = sb("sqA", [P, 256])
        qkA = sb("qkA", [P, 256])
        rope_cos = sb("rope_cos", [P, 4, 2, 8])
        rope_sin = sb("rope_sin", [P, 4, 2, 8])
        oN = sb("oN", [P, 128])
        stats = sb("stats", [P, 32])
        ss_qk, ms_qk, rstd_qk = stats[:, 0:4], stats[:, 4:8], stats[:, 8:12]
        negmax, rowmax, rowsum, rrow = stats[:, 12:14], stats[:, 14:16], stats[:, 16:18], stats[:, 18:20]
        ss_o, ms_o, rstd_o = stats[:, 20:21], stats[:, 21:22], stats[:, 22:23]
        qkS = sb("qkS", [P, 4, 64])
        qkCos = sb("qkCos", [P, 4, 64])
        qkSin = sb("qkSin", [P, 4, 64])
        qkR = sb("qkR", [P, 4, 64])
        vg = sb("vg", [P, 2, 256])
        eg = sb("eg", [P, 128])
        sg = sb("sg", [P, 2, 128])
        qkT = sb("qkT", [P, 2, 256])
        sT = sb("sT", [P, 2, 128])
        U = sb("U", [P, 2, 128])
        onR = sb("onR", [P, 128])
        gatedR = sb("gatedR", [P, 128])
        bstat = sb("bstat", [P, 16])
        head_c = sb("head_c", [P, 4])

        wC_at = [R_B, R_A]
        wC_in = [sb(f"wC_in{i}", [P, 24, 128], F32, at=wC_at[i]) for i in range(2)]
        wCL = [sb(f"wCL{i}", [P, 16, 128], F32R, at=wC_at[i]) for i in range(2)]
        wCH = [sb(f"wCH{i}", [P, 16, 128], F32R, at=wC_at[i] + 12 * KIB) for i in range(2)]
        merged = sb("merged", [P, N_KD, 1024], F32, at=R_WORK)
        mergedL = sb("mergedL", [P, N_KD, 1024], F32R, at=R_WORK)
        sig = sb("sig", [P, 2, 512], F32, at=R_WORK + 32 * KIB)
        mergedH = sb("mergedH", [P, N_KD, 1024], F32R, at=R_OT)
        wD_at = [R_B, R_HT]
        wD_in = [sb(f"wD_in{i}", [P, N_KD, 512], F32, at=wD_at[i]) for i in range(2)]
        wDL = [sb(f"wDL{i}", [P, N_KD, 512], F32R, at=wD_at[i]) for i in range(2)]
        wDH = [sb(f"wDH{i}", [P, N_KD, 512], F32R, at=wD_at[i] + 16 * KIB) for i in range(2)]
        x2 = sb("x2", [P, N_TILES, 1024], F32, at=R_HT + 32 * KIB)
        h2 = sb("h2", [P, 2, 1024], F32, at=R_A)
        h2T = sb("h2T", [P, 2, N_KD, 128], F32, at=R_A + 8 * KIB)
        g2_row = sb("g2_row", [P, 1024], F32, at=R_A + 16 * KIB)

        wr = sb("wr", [P, N_KD, 36], F32, at=R_A + 20 * KIB)
        br = sb("br", [P, 36], F32, at=R_A + 22 * KIB)
        route_at = [max(cursor[0], R_WORK + 37 * KIB)]

        def rt(name, shape, dt=F32):
            at = route_at[0]
            route_at[0] = (at + int(np.prod(shape[1:])) * 4 + 31) // 32 * 32
            assert route_at[0] <= limit, (name, route_at[0], limit)
            return nc.alloc_sbuf_tensor_at(name, shape, dt, offset=at)

        logits = rt("logits", [P, N_TILES, 36])
        n2 = rt("n2", [P, 4, 8])
        wsel = rt("wsel", [P, 2, N_TILES])
        q_at = [R_WORK]

        def rq(name, shape, dt=F32):
            at = q_at[0]
            q_at[0] = (at + int(np.prod(shape[1:])) * 4 + 31) // 32 * 32
            return nc.alloc_sbuf_tensor_at(name, shape, dt, offset=at)

        gmax = rq("gmax", [P, 8])
        gdiff = rq("gdiff", [P, 8, 4])
        gexp = rq("gexp", [P, 8, 4])
        gsum = rq("gsum", [P, 8])
        pgrp = rq("pgrp", [P, 8])
        gpen = rq("gpen", [P, 8, 4])
        gidx = rq("gidx", [P, 8])
        goh = rq("goh", [P, 8, 4])
        elsel = rq("elsel", [P, 8, 4, 8])
        el8 = rq("el8", [P, 8, 8])
        vtop = rq("vtop", [P, 2, 8])
        epen = rq("epen", [P, 8, 8])
        eidx = rq("eidx", [P, 2, 8])
        eoh = rq("eoh", [P, 8, 8])
        el8b = rq("el8b", [P, 8, 8])
        vdiff = rq("vdiff", [P, 8])
        vexp = rq("vexp", [P, 8])
        vden = rq("vden", [P, 8])
        eglob = rq("eglob", [P, 2, 8])
        oh = rq("oh", [P, 2, 8, 32])
        mask = rq("mask", [P, 8, 32])
        before = rq("before", [P, 9, 32])
        posm = rq("posm", [P, 2, 8, 32])
        pos = rq("pos", [P, 2, 8])
        pos_i = rq("pos_i", [P, 2, 8], I32)
        slot_i = rq("slot_i", [P, 2, 8], I32)
        blk_i = rq("blk_i", [P, 2, 8], I32)
        slotf = rq("slotf", [P, 2, 8])
        blkf = rq("blkf", [P, 2, 8])
        key = rq("key", [P, 2, 8])
        pick = rq("pick", [P, 16, 128], F32R)
        keyid1f = rq("keyid1f", [P, 16, 32])
        keyid1 = rq("keyid1", [P, 16, 32], F32R)
        keyid = [rq(f"keyid{i}", [P, 256], F32R) for i in range(2)]
        padded = rq("padded", [P, 256])
        zf = rq("zf", [P, 256])
        ids_scatter = rt("ids_scatter", [P, 256], I32)
        ids_gather = rt("ids_gather", [P, 256], I32)
        counts_f = rq("counts_f", [P, 33])
        counts_i = rt("counts_i", [P, 33], I32)
        cur_gather = rt("cur_gather", [P, 1], I32)
        cur_scatter = rt("cur_scatter", [P, 1], I32)

        slot_at = [R_B, R_B + 16 * KIB, R_HT, R_HT + 16 * KIB, R_OT, R_OT + 16 * KIB]
        w_in6 = [sb(f"w_slot{i}", [P, 2048], F32, at=slot_at[i]) for i in range(6)]
        w_low = [sb(f"w_low{i}", [P, 2048], F32R, at=slot_at[i]) for i in range(6)]
        w_high = [sb(f"w_high{i}", [P, 2048], F32R, at=slot_at[i] + 8 * KIB) for i in range(6)]
        e_at = [max(R_WORK, 0)]

        def ex(name, shape, dt=F32):
            at = e_at[0]
            e_at[0] = at + int(np.prod(shape[1:])) * 4
            assert e_at[0] <= R_WORK + 36 * KIB
            return nc.alloc_sbuf_tensor_at(name, shape, dt, offset=at)

        xe = sb("xe", [P, 1024], F32, at=R_A)
        xeH = sb("xeH", [P, 8, 128], F32R, at=R_A + 4 * KIB)
        xeL = sb("xeL", [P, 8, 128], F32R, at=R_A + 8 * KIB)
        silu = sb("silu", [P, 512], F32, at=R_A + 12 * KIB)
        hid = sb("hid", [P, 512], F32, at=R_A + 14 * KIB)
        hidH = sb("hidH", [P, 4, 128], F32R, at=R_A + 16 * KIB)
        hidL = sb("hidL", [P, 4, 128], F32R, at=R_A + 18 * KIB)
        y = sb("y", [P, 1024], F32, at=R_A + 20 * KIB)
        comb = sb("comb", [P, 4, 2, 1024], F32, at=R_OT)
        res = sb("res", [P, 4, 1024], F32, at=R_B)

        PROJ = [psum("proj0", [P, 512]), psum("proj1", [P, 512])]
        SC = psum("scores", [P, 2, 1024])
        TB = psum("turned", [P, 512])
        OB = psum("outs", [P, 512])

        h2_dram = nc.dram_tensor("h2_rows", (1024, 1024), F32, kind="Internal").ap()
        y_dram = nc.dram_tensor("y_rows", (2048, 1024), F32, kind="Internal").ap()

        w_in_v = T["w_in"][0].rearrange("(k p) c -> p k c", p=P)
        wa_v = T["w_branch_a"][0].rearrange("(k p) c -> p k c", p=P)
        wb_v = T["w_branch_b"][0].rearrange("(k p) c -> p k c", p=P)
        wo_v = T["w_out"][0].rearrange("(k p) c -> p k c", p=P)
        x_v = T["x"][0].rearrange("(i p) d -> p i d", p=P)
        out_v = T["out"][0].rearrange("(i p) d -> p i d", p=P)
        h2_v = h2_dram.rearrange("(i p) d -> p i d", p=P)
        y_v = y_dram.rearrange("(c i p) d -> p c i d", c=2, p=P)
        wg_v = T["w_gate"][0].rearrange("e (p k) f -> e p (k f)", p=P)
        wu_v = T["w_up"][0].rearrange("e (p k) f -> e p (k f)", p=P)
        wd_v = T["w_down"][0].rearrange("e (p k) n -> e p (k n)", p=P)

        def bank(n):
            if n < 4:
                return SC[:, n // 2, (n % 2) * 512:(n % 2) * 512 + 512]
            return [PROJ[0], PROJ[1], TB, OB][n - 4][:, :]

        names = """rows_stored consts_in small_in x_in0 x_in1 x_in2 x_in3 x_sq_done x_ms_done x_rstd_done xn_done xT_done hH_done
            hL_done lam_step lam_expd ang_step angle_done trig_done wA_landed wA_high wA_low
            wB_landed wB_high wB_low gn_landed t_free projA projB sqA_done vA_done ssA_done msA_done
            rstdA_done normA_done ropeA_step ropedA qkTA qkHA scored masked maxed negged exped
            rowsum_inv p1_scaled probs_done aT1 aT2 pv_done o_sq o_ms o_rstd oN_done oTA qkS_done
            vg_done eg_done cosB sinB ropedB eg1 egr sg_done qkTB kv_done U_done st_done sT_done oB
            bn_s bn_a bn_v bn_r onR_done gate_step gated gTB wC_landed0 wC_landed1 wC_high wC_low
            gates_done ys_done sig_exp sig_one sig_inv sig_mul merged_step wD_landed0 wD_landed1
            wD_high wD_low x2_in mH mL d_done x2_done g2_in router_in n2_sq n2_ms n2_rstd h2_done
            h2T_done h2T_out lg_done logit_done h2_stored0 h2_stored1 rstep ract pmm pick_done
            pick_used ids_done w_land0 w_land1 w_land2 w_land3 w_land4 w_land5 w_free_gu w_free_d
            idx_copied xe_landed xeT_done xeH_done xeL_done silu_done hid_done hidT_done hidH_done
            hidL_done y_out scattered comb_in0 comb_in1 comb_in2 comb_in3 comb_mid res_done out_stored0 out_stored1 out_stored2 out_stored3
            head_consts gu_high gu_low d_high d_low xe_zero v_w v_hi v_lo""".split()
        S = {n: sem(n) for n in names}

        block = ctx.enter_context(nc.Block())
        FILL, ROUND = range(0, 3), range(3, 19)
        PREP = {3: [0, 1], 4: [2], 5: [3, 4], 6: [5], 7: [6, 7]}

        def tile_at(s):
            if s < 0:
                return None, 0, 0
            if s < 2 * N_TILES:
                return "AB"[s // N_TILES], s % N_TILES, s % N_TILES
            return "A", s - 2 * N_TILES, s - N_TILES

        def times(eng, h, n):
            return h * n if isinstance(h, int) else eng.snap(h * n)

        def overflow(eng, block_of, first=None):
            most = eng.value_load(counts_i[0:1, 32:33], min_val=0, max_val=1024)
            with eng.If(most > BLOCK):
                if first:
                    first()
                n = eng.alloc_register()
                eng.reg_mov(n, 0)
                with eng.Fori(1, MAX_BLOCKS) as b:
                    with eng.Fori(0, N_EXP) as e:
                        held = eng.value_load(counts_i[0:1, DS(e, 1)], min_val=0, max_val=1024)
                        with eng.If(held > b * BLOCK):
                            block_of(eng.snap(n), e, b)
                            eng.reg_add(n, n, 1)
                        with eng.Else():
                            eng.nop()
                        eng.nop()
                eng.nop()
            with eng.Else():
                eng.nop()
            eng.nop()

        STARTS_FREE = """t_free ssA_done ropedB sg_done qkTA ropedA gated gTB U_done sT_done
            exped eg_done onR_done pv_done projB qkS_done y_out""".split()

        @block.sync
        def _(sp):
            for name in STARTS_FREE:
                sp.sem_inc(S[name], FREE)
            sp.sem_inc(S["sig_mul"], SIG_FREE)
            sp.dma_start(x_all[:, 0:2, :], x_v[:, 0:2, :]).then_inc(S["x_in0"], DMA)
            sp.dma_start(consts[:], T["consts"]).then_inc(S["consts_in"], DMA)
            sp.dma_start(g1_cols, T["norm1_g"][0].rearrange("(k p) -> p k", p=P),
                         allow_slow_non_contiguous=True).then_inc(S["small_in"], DMA)
            for j in range(1, 4):
                sp.dma_start(x_all[:, 2 * j:2 * j + 2, :], x_v[:, 2 * j:2 * j + 2, :]).then_inc(S[f"x_in{j}"], DMA)
            sp.dma_start(subln_col, T["diff_subln_g"][0].rearrange("(p o) -> p o", o=1),
                         allow_slow_non_contiguous=True).then_inc(S["small_in"], DMA)
            sp.dma_start(posi[:], T["positions"][0].rearrange("(i p) -> p i", p=P),
                         allow_slow_non_contiguous=True).then_inc(S["small_in"], DMA)
            for j, n in enumerate(("lambda_q1", "lambda_k1", "lambda_q2", "lambda_k2")):
                sp.dma_start(lam_rows[:, j, :], T[n][0].partition_broadcast(P)).then_inc(S["small_in"], DMA)
            for j, n in enumerate(("q_norm_g", "k_norm_g")):
                sp.dma_start(gains[:, j, :], T[n][0].partition_broadcast(P)).then_inc(S["small_in"], DMA)

            def load_A(head):
                for j, col in enumerate((QA, KA, VA)):
                    sp.dma_start(wA_in[:, :, 128 * j:128 * j + 128],
                                 w_in_v[:, :, DS(head * 128 + col, 128)]).then_inc(S["wA_landed"], DMA)

            load_A(0)
            sp.wait_ge(S["xT_done"], 16)
            with sp.Fori(0, N_HEADS) as h:
                h8 = sp.snap(h * 8)
                sp.wait_ge(S["projB"], h8 + FREE)
                for j, col in enumerate((QB, KB, VB, GB)):
                    sp.dma_start(wB_in[:, :, 128 * j:128 * j + 128],
                                 w_in_v[:, :, DS(h * 128 + col, 128)]).then_inc(S["wB_landed"], DMA)
                sp.wait_ge(S["xT_done"], 16)
                sp.wait_ge(S["gated"], h8 + FREE)
                for j, n in enumerate(("ret_gn_g", "ret_gn_b")):
                    sp.dma_start(gn_rows[:, j, :],
                                 T[n][0][DS(h * 128, 128)].partition_broadcast(P)).then_inc(S["gn_landed"], DMA)
                sp.wait_ge(S["projA"], h8 + 8)
                load_A(h + 1)

            def load_C(m, slot):
                sp.dma_start(wC_in[slot][:, 0:8, :], w_in_v[:, :, DS(m * 128 + GATE_A, 128)]).then_inc(S[f"wC_landed{slot}"], DMA)
                sp.dma_start(wC_in[slot][:, 8:16, :], w_in_v[:, :, DS(m * 128 + GATE_B, 128)]).then_inc(S[f"wC_landed{slot}"], DMA)
                sp.dma_start(wC_in[slot][:, 16:20, :], wa_v[:, :, DS(m * 128, 128)]).then_inc(S[f"wC_landed{slot}"], DMA)
                sp.dma_start(wC_in[slot][:, 20:24, :], wb_v[:, :, DS(m * 128, 128)]).then_inc(S[f"wC_landed{slot}"], DMA)

            sp.wait_ge(S["projB"], 8 * N_HEADS + FREE)
            load_C(0, 0)
            sp.wait_ge(S["gates_done"], 1)
            load_C(1, 1)
            with sp.Fori(1, 4) as j:
                sp.wait_ge(S["ys_done"], j * 4 - 2)
                load_C(j * 2, 0)
                sp.wait_ge(S["ys_done"], j * 4)
                load_C(j * 2 + 1, 1)
            sp.wait_ge(S["ys_done"], 14)
            sp.dma_start(wD_in[0][:], wo_v[:, :, 0:512]).then_inc(S["wD_landed0"], DMA)
            sp.wait_ge(S["gates_done"], 16)
            for j in range(4):
                sp.dma_start(x2[:, 2 * j:2 * j + 2, :], x_v[:, 2 * j:2 * j + 2, :]).then_inc(S[f"x_in{j}"], DMA)
            sp.dma_start(wD_in[1][:], wo_v[:, :, 512:1024]).then_inc(S["wD_landed1"], DMA)
            sp.dma_start(g2_row[:], T["norm2_g"][0].partition_broadcast(P)).then_inc(S["g2_in"], DMA)
            sp.dma_start(wr[:, :, 0:4], T["w_group_router"][0].rearrange("(k p) c -> p k c", p=P)).then_inc(S["router_in"], DMA)
            sp.dma_start(wr[:, :, 4:36], T["w_expert_router"][0].rearrange("(k p) c -> p k c", p=P)).then_inc(S["router_in"], DMA)
            sp.dma_start(br[:, 0:4], T["b_group_router"][0].partition_broadcast(P)).then_inc(S["router_in"], DMA)
            sp.dma_start(br[:, 4:36], T["b_expert_router"][0].partition_broadcast(P)).then_inc(S["router_in"], DMA)

            def load_gu(e, slots=range(4), land="w_land"):
                for c in slots:
                    v = (wg_v, wu_v)[c % 2]
                    sp.dma_start(w_in6[c][:], v[e][:, (c // 2) * 2048:(c // 2) * 2048 + 2048]).then_inc(S[f"w_land{c}"], DMA)

            def load_d(e, slots=(4, 5)):
                for c in slots:
                    sp.dma_start(w_in6[c][:], wd_v[e][:, (c - 4) * 2048:(c - 4) * 2048 + 2048]).then_inc(S[f"w_land{c}"], DMA)

            sp.wait_ge(S["d_done"], 8)
            load_gu(0, (0, 1))
            for i in range(N_TILES):
                sp.wait_ge(S["h2_done"], i + 1)
                sp.dma_start(h2_v[:, i, :], h2[:, i % 2, :]).then_inc(S[f"h2_stored{i % 2}"], DMA)
            sp.wait_ge(S["d_done"], 16)
            load_gu(0, (2, 3))
            load_d(0)
            for c in range(4):
                sp.wait_ge(S["w_free_gu"], c + 1)
                load_gu(1, (c,))
            for c in (4, 5):
                sp.wait_ge(S["w_free_d"], c - 3)
                load_d(1, (c,))
            for c in range(4):
                sp.wait_ge(S["w_free_gu"], c + 5)
                load_gu(2, (c,))
            with sp.Fori(2, N_EXP - 1) as e:
                for c in range(4):
                    sp.wait_ge(S["w_free_gu"], e * 4 + (c + 1))
                    load_gu(e + 1, (c,))
                for c in (4, 5):
                    sp.wait_ge(S["w_free_d"], e * 2 + (c - 5))
                    load_d(e, (c,))
            for c in range(2):
                sp.wait_ge(S["w_free_gu"], 4 * (N_EXP - 1) + c + 1)
                sp.dma_start(w_in6[c][:], wd_v[N_EXP - 1][:, c * 2048:(c + 1) * 2048]).then_inc(S[f"w_land{c}"], DMA)

            sp.wait_ge(S["ids_done"], 1)

            def loads_again(n, e, b):
                sp.wait_ge(S["scattered"], n * DMA + DMA * N_EXP)
                for c in range(4):
                    sp.dma_start(w_in6[c][:], (wg_v, wu_v)[c % 2][e][:, (c // 2) * 2048:(c // 2) * 2048 + 2048]).then_inc(S["v_w"], DMA)
                for c in (4, 5):
                    sp.dma_start(w_in6[c][:], wd_v[e][:, (c - 4) * 2048:(c - 4) * 2048 + 2048]).then_inc(S["v_w"], DMA)

            overflow(sp, loads_again)
            sp.wait_ge(S["rows_stored"], 1)

            for i in range(N_TILES):
                if i >= 4:
                    sp.wait_ge(S["res_done"], i - 3)
                for c in range(2):
                    sp.dma_start(comb[:, i % 4, c, :], y_v[:, c, i, :]).then_inc(S[f"comb_in{i % 4}"], DMA)
            for b in range(4):
                sp.wait_ge(S[f"out_stored{b}"], DMA * N_TILES // 4)


        def turn_rows(pe, src_rows, dst, step, n):
            for k in range(n):
                last = pe.transpose(dst[:, k * 128:(k + 1) * 128], src_rows[:, DS(k, 128, step=step)], ident)
            return last

        def gate_up(pe, c):
            for k in range(4):
                kk = (c // 2) * 4 + k
                last = split3(pe, PROJ[c % 2][:, :], (xeH[:, kk, :], xeL[:, kk, :]),
                              (w_high[c][:, k * 512:(k + 1) * 512], w_low[c][:, k * 512:(k + 1) * 512]),
                              kk == 0, kk == 7)
            return last

        def down(pe, c, slot=None):
            slot = c if slot is None else slot
            for k in range(2):
                kk = (c - 4) * 2 + k
                for half in range(2):
                    lo = k * 1024 + half * 512
                    last = split3(pe, SC[:, 1, half * 512:(half + 1) * 512], (hidH[:, kk, :], hidL[:, kk, :]),
                                  (w_high[slot][:, lo:lo + 512], w_low[slot][:, lo:lo + 512]), kk == 0, kk == 3)
            return last

        T_FILL, T_ROUND = 3, 28 + 16

        @block.tensor
        def _(pe):
            pe.wait_ge(S["consts_in"], DMA)
            for n in range(16):
                half, k = n // 8, n % 8
                pe.wait_ge(S["xn_done"], 4 * half + 4)
                if n >= 4:
                    pe.wait_ge(S["hL_done"], n - 3)
                for i in range(4):
                    last = pe.transpose(bank(n % 4)[:, i * 128:(i + 1) * 128],
                                        x_all[:, 4 * half + i, k * 128:(k + 1) * 128], ident)
                last.then_inc(S["xT_done"], 1)
            pe.wait_ge(S["hL_done"], 16)

            def head_steps(h, steps):
                h8, h7, hT = times(pe, h, 8), times(pe, h, 7), times(pe, h, T_ROUND)
                t_used = [0 if steps is FILL else T_FILL]

                def turned_free():
                    pe.wait_ge(S["t_free"], hT + t_used[0] + FREE)

                def take_turned():
                    turned_free()
                    t_used[0] += 1

                def project(s, ks):
                    unit, i, n = tile_at(s)
                    if ks[0] == 0:
                        last_unit, _, last_n = tile_at(s - 2)
                        if last_unit == "A":
                            pe.wait_ge(S["normA_done"], h8 + (last_n + 1))
                        elif last_unit == "B":
                            pe.wait_ge(S["eg_done"], h8 + (last_n + 1) + FREE)
                    wh, wl, cols = (wAH, wAL, 384) if unit == "A" else (wBH, wBL, 512)
                    for k in ks:
                        if i == 0:
                            pe.wait_ge(S[f"w{unit}_low"], h8 + (n + k + 1))
                        last = split3(pe, PROJ[s % 2][:, 0:cols],
                                      (hTH[:, k, i * 128:(i + 1) * 128], hTL[:, k, i * 128:(i + 1) * 128]),
                                      (wh[:, k, :], wl[:, k, :]), k == 0, k == 7)
                    if ks[-1] == 7:
                        last.then_inc(S["proj" + unit], 1)

                if steps is FILL:
                    project(0, [0, 1])
                for s in steps:
                    (u0, _, _), (u1, i1, n1), (u2, i2, n2_), (u3, i3, n3) = [tile_at(s - lag) for lag in range(4)]
                    project(s, [2, 3])
                    if u1 == "A":
                        pe.wait_ge(S["ropedA"], h8 * 2 + (2 * n1 + 2) + FREE)
                        take_turned()
                        pe.transpose(TB[:, 0:128], qkA[:, 0:128], ident)
                        pe.transpose(TB[:, 128:256], qkA[:, 128:256], ident).then_inc(S["qkTA"], 1)
                    if u1 == "B":
                        pe.wait_ge(S["ropedB"], h8 * 2 + (2 * n1 + 2) + FREE)
                        take_turned()
                        pe.transpose(TB[:, 0:128], qkR[:, 0:2, :].rearrange("p a b -> p (a b)"), ident)
                        pe.transpose(TB[:, 128:256], qkR[:, 2:4, :].rearrange("p a b -> p (a b)"), ident).then_inc(S["qkTB"], 1)
                    project(s, [4, 5])
                    if u1 == "A":
                        if i1 == 0:
                            pe.wait_ge(S["sT_done"], h8 + n1 + FREE)
                            pe.wait_ge(S["U_done"], h7 + 7 * (n1 // 8) + FREE)
                        pe.wait_ge(S["exped"], h8 * 2 + 2 * n1 + FREE)
                        turned_free()
                        for c in range(2):
                            r = slice(c * 64, c * 64 + 64)
                            for k0 in range(0, (i1 + 1) * 128, 512):
                                k1 = min(k0 + 512, (i1 + 1) * 128)
                                last = split3(pe, SC[:, c, k0:k1], (QH[r, :], QL[r, :]), (KH[r, k0:k1], KL[r, k0:k1]),
                                              True, True)
                        last.then_inc(S["scored"], 1)
                    if u1 == "B":
                        if i1 == 0:
                            pe.wait_ge(S["exped"], h8 * 2 + 16 + FREE)
                        pe.wait_ge(S["sT_done"], h8 + n1 + FREE)
                        turned_free()
                        pe.matmul(bank(0)[:, 0:128], qkT[:, i1 % 2, 128:256], qkT[:, i1 % 2, 0:128],
                                  start=True, stop=True).then_inc(S["st_done"], 1)
                    if u3 == "A":
                        pe.wait_ge(S["oN_done"], h8 + (n3 + 1))
                        take_turned()
                        pe.transpose(TB[:, 0:128], oN[:, :], ident).then_inc(S["oTA"], 1)
                    if u3 == "B":
                        pe.wait_ge(S["gated"], h8 + (n3 + 1) + FREE)
                        take_turned()
                        pe.transpose(TB[:, 0:128], gatedR[:, :], ident).then_inc(S["gTB"], 1)
                    if u2 == "B":
                        pe.wait_ge(S["sT_done"], h8 + (n2_ + 1) + FREE)
                        if i2 == 0:
                            pe.wait_ge(S["oN_done"], h8 + 8)
                        else:
                            pe.wait_ge(S["onR_done"], h8 + n2_ + FREE)
                            pe.wait_ge(S["U_done"], h7 + n2_ + FREE)
                        last = pe.matmul(OB[:, 0:128], sT[:, i2 % 2, :], vg[:, i2 % 2, 0:128], start=True, stop=(i2 == 0))
                        if i2 > 0:
                            last = pe.matmul(OB[:, 0:128], qkT[:, i2 % 2, 0:128], U[:, i2 % 2, :], start=False, stop=True)
                        last.then_inc(S["oB"], 1)
                    if u1 == "B" and i1 < N_TILES - 1:
                        pe.wait_ge(S["U_done"], h7 + n1 + FREE)
                        pe.wait_ge(S["vg_done"], h8 + (n1 + 1))
                        pe.matmul(bank(2)[:, 0:128], qkR[:, 2:4, :].rearrange("p a b -> p (a b)"), vg[:, i1 % 2, 0:128],
                                  start=True, stop=True).then_inc(S["kv_done"], 1)
                    project(s, [6, 7])
                    if u2 == "A":
                        pe.wait_ge(S["probs_done"], h8 + (n2_ + 1))
                        take_turned()
                        for j in range(min(4, i2 + 1)):
                            last = pe.transpose(TB[:, j * 128:(j + 1) * 128], probs[:, 0, j * 128:(j + 1) * 128], ident)
                        last.then_inc(S["aT1"], 1)
                    project(s + 1, [0])
                    if u2 == "A" and i2 >= 4:
                        take_turned()
                        for j in range(4, i2 + 1):
                            last = pe.transpose(TB[:, (j - 4) * 128:(j - 3) * 128], probs[:, 0, j * 128:(j + 1) * 128], ident)
                        last.then_inc(S["aT2"], 1)
                    project(s + 1, [1])
                    if u2 == "A":
                        if i2 == 0:
                            pe.wait_ge(S["onR_done"], h8 + n2_ + FREE)
                        else:
                            pe.wait_ge(S["oN_done"], h8 + n2_)
                        turned_free()
                        for j in range(i2 + 1):
                            last = pe.matmul(OB[:, 0:128], aT[:, j, :], V[:, j, :], start=(j == 0), stop=(j == i2))
                        last.then_inc(S["pv_done"], 1)
                assert t_used[0] == T_FILL + (0 if steps is FILL else T_ROUND), t_used

            head_steps(0, FILL)
            with pe.Fori(0, N_HEADS) as h:
                head_steps(h, ROUND)
            pe.matmul(PROJ[(ROUND[-1] + 1) % 2][:, 0:384], hTH[:, 0, 0:128], wAH[:, 0, :], start=False, stop=True)

            pe.wait_ge(S["t_free"], N_HEADS * T_ROUND + T_FILL + FREE)
            pe.wait_ge(S["onR_done"], 8 * N_HEADS + FREE)
            pe.wait_ge(S["normA_done"], 8 * N_HEADS + 3)
            pe.wait_ge(S["exped"], 2 * (8 * N_HEADS + 2) + FREE)
            pe.wait_ge(S["eg_done"], 8 * N_HEADS + FREE)
            pe.wait_ge(S["sT_done"], 8 * N_HEADS + FREE)
            pe.wait_ge(S["U_done"], 7 * N_HEADS + FREE)

            def merge_pair(j, last_pair):
                j4, j8 = times(pe, j, 4), times(pe, j, 8)
                for sub in range(2):
                    pe.wait_ge(S["wC_low"], j4 + (2 * sub + 2))
                    for th in range(2):
                        n = 2 * sub + th
                        b0 = 4 if th == 0 else 0
                        pe.wait_ge(S["sig_mul"], j8 + (2 * n - 2) + SIG_FREE)
                        tok = slice(th * 512, th * 512 + 512)

                        def gates():
                            for g in range(2):
                                for k in range(8):
                                    last = split3(pe, bank(b0 + g), (wCH[sub][:, g * 8 + k, :], wCL[sub][:, g * 8 + k, :]),
                                                  (hTH[:, k, tok], hTL[:, k, tok]), k == 0, k == 7)
                            last.then_inc(S["gates_done"], 1)

                        def branches():
                            for g in range(2):
                                for k in range(4):
                                    last = pe.matmul(bank(b0 + 2 + g), wC_in[sub][:, 16 + 4 * g + k, :], oT[:, 4 * g + k, tok],
                                                     start=(k == 0), stop=(k == 3))
                            last.then_inc(S["ys_done"], 1)

                        if last_pair and n == 3:
                            branches()
                            gates()
                        else:
                            gates()
                            branches()

            with pe.Fori(0, 3) as j:
                merge_pair(j, False)
            merge_pair(3, True)

            pe.wait_ge(S["sig_mul"], 30 + SIG_FREE)

            def out_proj(n, i):
                pe.wait_ge(S["wD_low"], 2 * n + 2)
                pe.wait_ge(S["mL"], i + 1)
                cnt = 8 * n + i
                if cnt >= 3:
                    pe.wait_ge(S["x2_done"], cnt - 2)
                tok = slice(i * 128, i * 128 + 128)
                for k in range(8):
                    last = split3(pe, bank(4 + cnt % 3), (mergedH[:, k, tok], mergedL[:, k, tok]),
                                  (wDH[n][:, k, :], wDL[n][:, k, :]), k == 0, k == 7)
                last.then_inc(S["d_done"], 1)

            for i in range(N_TILES):
                out_proj(0, i)
            for i in range(N_TILES + 2):
                if i < N_TILES:
                    out_proj(1, i)
                if i >= 2:
                    t = i - 2
                    pe.wait_ge(S["h2T_out"], t + 1)
                    pe.wait_ge(S["router_in"], 4 * DMA)
                    if t >= 1:
                        pe.wait_ge(S["logit_done"], t)
                    for k in range(8):
                        last = pe.matmul(OB[:, 0:36], h2T[:, t % 2, k, :], wr[:, k, :], start=(k == 0), stop=(k == 7))
                    last.then_inc(S["lg_done"], 1)
                if 1 <= i <= N_TILES:
                    t = i - 1
                    pe.wait_ge(S["h2_done"], t + 1)
                    if t >= 2:
                        pe.wait_ge(S["h2T_out"], t - 1)
                    for k in range(8):
                        last = pe.transpose(SC[:, t % 2, k * 128:(k + 1) * 128], h2[:, t % 2, k * 128:(k + 1) * 128], ident)
                    last.then_inc(S["h2T_done"], 1)

            pe.wait_ge(S["rstep"], R_BEFORE)
            pe.matmul(bank(0)[:, 0:256], const("strict"), mask[:].rearrange("p a b -> p (a b)"), start=True, stop=False)
            pe.matmul(bank(0)[:, 0:256], const("ones"), before[:, 0:8, :].rearrange("p a b -> p (a b)"),
                      start=False, stop=True).then_inc(S["pmm"], 1)
            pe.matmul(bank(1)[:, 0:32], const("ones"), before[:, 8, :], start=True, stop=True).then_inc(S["pmm"], 1)
            for q in range(16):
                if q % 8 == 0:
                    pe.wait_ge(S["pick_done"], q // 8 + 1)
                last = pe.matmul(bank(2)[:, 0:32], pick[:, q, :], keyid1[:, q, :], start=(q == 0), stop=(q == 15))
            last.then_inc(S["pmm"], 1)

            def all_tables():
                for q in range(16):
                    pe.wait_ge(S["pick_done"], q + 3)
                    pe.matmul(bank(2)[:, 0:256], pick[:, q, :], keyid[q % 2][:, :], start=(q == 0), stop=(q == 15)
                              ).then_inc(S["pick_used"], 1)

            def turn_x():
                turn_rows(pe, xe, SC[:, 0, :], 8, 8).then_inc(S["xeT_done"], 1)

            def run_gate_up(e4):
                for c in range(4):
                    pe.wait_ge(S["gu_low"], e4 + (c + 1))
                    last = gate_up(pe, c)
                    last.then_inc(S["w_free_gu"], 1)

            def run_down(e2):
                for c in (4, 5):
                    pe.wait_ge(S["d_low"], e2 + (c - 3))
                    down(pe, c).then_inc(S["w_free_d"], 1)

            pe.wait_ge(S["xe_landed"], DMA)
            turn_x()
            pe.wait_ge(S["xeL_done"], 1)
            run_gate_up(0)
            pe.wait_ge(S["xe_landed"], 2 * DMA)
            turn_x()
            pe.wait_ge(S["hid_done"], 1)
            turn_rows(pe, hid, TB, 4, 4).then_inc(S["hidT_done"], 1)
            pe.wait_ge(S["hidL_done"], 1)
            run_down(0)

            def expert_step(e, more):
                e2, e4, e16 = (e * 2, e * 4, e * 16) if isinstance(e, int) else (pe.snap(e * 2), pe.snap(e * 4), pe.snap(e * 16))
                pe.wait_ge(S["xeL_done"], e + 1)
                pe.wait_ge(S["hid_done"], e)
                run_gate_up(e4)
                if more:
                    pe.wait_ge(S["xe_landed"], e16 + 2 * DMA)
                    turn_x()
                if not isinstance(e, int) or e > 1:
                    pe.wait_ge(S["hidL_done"], e)
                    pe.wait_ge(S["y_out"], e - 1 + FREE)
                    run_down(e2 - 2)
                pe.wait_ge(S["hid_done"], e + 1)
                turn_rows(pe, hid, TB, 4, 4).then_inc(S["hidT_done"], 1)

            expert_step(1, True)
            with pe.Fori(2, N_EXP - 1) as e:
                expert_step(e, True)
            expert_step(N_EXP - 1, False)
            pe.wait_ge(S["hidL_done"], N_EXP)
            pe.wait_ge(S["y_out"], N_EXP - 1 + FREE)
            for c in range(2):
                pe.wait_ge(S["gu_low"], 4 * N_EXP + c + 1)
                down(pe, 4 + c, slot=c).then_inc(S["w_free_d"], 1)
            pe.wait_ge(S["y_out"], N_EXP + FREE)

            def block_products(n, e, b):
                pe.wait_ge(S["xe_landed"], n * DMA + DMA * (N_EXP + 1))
                turn_x()
                pe.wait_ge(S["xeL_done"], n + (N_EXP + 1))
                pe.wait_ge(S["v_lo"], n * 6 + 6)
                for c in range(4):
                    gate_up(pe, c).then_inc(S["w_free_gu"], 1)
                pe.wait_ge(S["hid_done"], n + (N_EXP + 1))
                turn_rows(pe, hid, TB, 4, 4).then_inc(S["hidT_done"], 1)
                pe.wait_ge(S["hidL_done"], n + (N_EXP + 1))
                for c in (4, 5):
                    down(pe, c).then_inc(S["w_free_d"], 1)
                pe.wait_ge(S["y_out"], n + (N_EXP + 1) + FREE)

            overflow(pe, block_products, all_tables)

        @block.scalar
        def _(act):
            for i in range(N_TILES):
                act.wait_ge(S[f"x_in{i // 2}"], DMA)
                if i:
                    act.wait_ge(S["x_sq_done"], i)
                act.activation(x_sq[:], x_all[:, i, :], ACT.Square, accum_out=x_ss[:, i:i + 1]).then_inc(S["x_sq_done"], 1)
            act.wait_ge(S["small_in"], 9 * DMA)
            for n in range(16):
                half, k = n // 8, n % 8
                act.wait_ge(S["xT_done"], n + 1)
                act.activation(hTH[:, k, half * 512:(half + 1) * 512], bank(n % 4), ACT.Copy,
                               scale=g1_cols[:, k:k + 1]).then_inc(S["hH_done"], 1)
            act.wait_ge(S["angle_done"], 1)
            act.activation(sin_t[:], ang[:], ACT.Sin).then_inc(S["trig_done"], 1)
            act.activation(cos_t[:], turns[:], ACT.Sin, scale=-1.0, bias=const("half_pi")).then_inc(S["trig_done"], 1)
            act.wait_ge(S["lam_step"], 2)
            act.activation(lam_e, lam_s, ACT.Exp).then_inc(S["lam_expd"], 1)

            def high(dst, src_, landed, value, done, n=1):
                act.wait_ge(landed, value)
                act.activation(dst, src_, ACT.Copy).then_inc(done, n)

            for k in range(8):
                high(wAH[:, k, :], wA_in[:, k, :], S["wA_landed"], 3 * DMA, S["wA_high"])

            def head_steps(h, steps):
                h8, h48, h64 = times(act, h, 8), times(act, h, 48), times(act, h, 64)
                for s in steps:
                    (u0, i0, n0), (u1, i1, n1), (u2, i2, n2_), (u3, i3, n3) = [tile_at(s - lag) for lag in range(4)]
                    src_bank = PROJ[s % 2]
                    if u1 == "A":
                        act.wait_ge(S["qkTA"], h8 + (n1 + 1) + FREE)
                        act.activation(QH[:], TB[:, 0:128], ACT.Copy).then_inc(S["qkHA"], 1)
                        act.activation(KH[:, i1 * 128:(i1 + 1) * 128], TB[:, 128:256], ACT.Copy).then_inc(S["qkHA"], 1)
                    if u1 == "B":
                        act.wait_ge(S["qkTB"], h8 + (n1 + 1))
                        act.activation(qkT[:, i1 % 2, :], TB[:, 0:256], ACT.Copy).then_inc(S["t_free"], 1)
                    if u3 == "A":
                        act.wait_ge(S["pv_done"], h8 + (n3 + 1) + FREE)
                        act.activation(oN[:], OB[:, 0:128], ACT.Square, accum_out=ss_o).then_inc(S["o_sq"], 1)
                        act.wait_ge(S["oTA"], h8 + (n3 + 1))
                        act.activation(oT[:, DS(h, 1), i3 * 128:(i3 + 1) * 128].rearrange("p a b -> p (a b)"), TB[:, 0:128],
                                       ACT.Copy, scale=subln_scaled).then_inc(S["t_free"], 1)
                    if u3 == "B":
                        act.wait_ge(S["gTB"], h8 + (n3 + 1) + FREE)
                        act.activation(oT[:, DS(h + 4, 1), i3 * 128:(i3 + 1) * 128].rearrange("p a b -> p (a b)"), TB[:, 0:128],
                                       ACT.Copy).then_inc(S["t_free"], 1)
                    if s % 8 in PREP:
                        ks = PREP[s % 8]
                        if u0 == "A":
                            high(wBH[:, ks[0]:ks[-1] + 1, :], wB_in[:, ks[0]:ks[-1] + 1, :],
                                 S["wB_landed"], h64 + 4 * DMA, S["wB_high"], len(ks))
                        else:
                            high(wAH[:, ks[0]:ks[-1] + 1, :], wA_in[:, ks[0]:ks[-1] + 1, :],
                                 S["wA_landed"], h48 + 6 * DMA, S["wA_high"], len(ks))
                    if u0 == "A":
                        act.wait_ge(S["projA"], h8 + (n0 + 1))
                        act.wait_ge(S["ssA_done"], h8 + n0 + FREE)
                        act.activation(sqA[:], src_bank[:, 0:256], ACT.Square).then_inc(S["sqA_done"], 1)
                        act.activation(V[:, i0, :], src_bank[:, 256:384], ACT.Copy).then_inc(S["vA_done"], 1)
                    if u0 == "B":
                        par = i0 % 2
                        act.wait_ge(S["projB"], h8 + (n0 + 1) + FREE)
                        if i0 == 0:
                            act.wait_ge(S["head_consts"], h + 1)
                        act.wait_ge(S["ropedB"], h8 * 2 + 2 * n0 + FREE)
                        if i0 >= 2:
                            act.wait_ge(S["oB"], h8 + (n0 - 1))
                            act.wait_ge(S["sg_done"], h8 + (n0 - 1) + FREE)
                        act.activation(qkS[:, 0:2, :], src_bank[:, 0:128].rearrange("p (a b) -> p a b", a=2), ACT.Copy,
                                       scale=head_c[:, 0:1]).then_inc(S["qkS_done"], 1)
                        act.activation(qkS[:, 2:4, :], src_bank[:, 128:256].rearrange("p (a b) -> p a b", a=2), ACT.Copy,
                                       scale=head_c[:, 1:2]).then_inc(S["qkS_done"], 1)
                        act.activation(vg[:, par, :], src_bank[:, 256:512], ACT.Copy).then_inc(S["vg_done"], 1)
                        act.wait_ge(S["sg_done"], h8 + n0 + FREE)
                        act.activation(eg[:], src_bank[:, 384:512], ACT.Exp, scale=-1.0).then_inc(S["eg_done"], 1)
                    L = (i1 + 1) * 128

                    def exponentials(c):
                        act.activation(probs[:, c, 0:L], SC[:, c, 0:L], ACT.Exp, bias=negmax[:, c:c + 1], scale=0.125,
                                       accum_out=rowsum[:, c:c + 1]).then_inc(S["exped"], 1)

                    if u2 == "A":
                        nb = min(4, i2 + 1)
                        act.wait_ge(S["aT1"], h8 + (n2_ + 1))
                        act.activation(aT[:, 0:nb, :].rearrange("p a b -> p (a b)"), TB[:, 0:nb * 128], ACT.Copy
                                       ).then_inc(S["t_free"], 1)
                    if u1 == "A":
                        act.wait_ge(S["negged"], h8 + (n1 + 1))
                        exponentials(1)
                        if u2 == "A" and i2 >= 4:
                            act.wait_ge(S["aT2"], h * 4 + (i2 - 3))
                        exponentials(0)

            head_steps(0, FILL)
            with act.Fori(0, N_HEADS) as h:
                head_steps(h, ROUND)

            def high_C(m_value, sub, piece):
                act.wait_ge(S[f"wC_landed{sub}"], m_value)
                act.activation(wCH[sub][:, piece * 8:piece * 8 + 8, :], wC_in[sub][:, piece * 8:piece * 8 + 8, :],
                               ACT.Copy).then_inc(S["wC_high"], 1)

            high_C(4 * DMA, 0, 0)
            high_C(4 * DMA, 0, 1)
            act.wait_ge(S["p1_scaled"], 8 * N_HEADS + 2)
            act.wait_ge(S["rowsum_inv"], 2 * (8 * N_HEADS + 2))

            def merge_pair(j, last):
                j4, j8 = (j * 4, j * 8) if isinstance(j, int) else (act.snap(j * 4), act.snap(j * 8))
                j64 = j * 64 if isinstance(j, int) else act.snap(j * 64)
                for sub in range(2):
                    for th in range(2):
                        n = 2 * sub + th
                        if last and n == 3:
                            high_merged(0)
                        act.wait_ge(S["gates_done"], j4 + (n + 1))
                        act.wait_ge(S["sig_mul"], j8 + 2 * n + SIG_FREE)
                        for g in range(2):
                            act.activation(sig[:, g, :], bank((4 if th == 0 else 0) + g), ACT.Exp, scale=-1.0
                                           ).then_inc(S["sig_exp"], 1)
                        for piece in range(2):
                            if n == 0:
                                high_C(j64 + 4 * DMA, 1, piece)
                            if n == 2 and not last:
                                high_C(j64 + 8 * DMA, 0, piece)
                            if n == 2 and last:
                                high(wDH[0][:, piece * 4:piece * 4 + 4, :], wD_in[0][:, piece * 4:piece * 4 + 4, :],
                                     S["wD_landed0"], DMA, S["wD_high"])

            def high_merged(th):
                if th == 0:
                    act.wait_ge(S["ys_done"], 16)
                act.wait_ge(S["sig_mul"], 30 + 2 * th + SIG_FREE)
                for i in range(4 * th, 4 * th + 4):
                    act.activation(mergedH[:, :, i * 128:(i + 1) * 128], merged[:, :, i * 128:(i + 1) * 128], ACT.Copy
                                   ).then_inc(S["mH"], 1)

            with act.Fori(0, 3) as j:
                merge_pair(j, False)
            merge_pair(3, True)
            high_merged(1)
            for piece in range(2):
                high(wDH[1][:, piece * 4:piece * 4 + 4, :], wD_in[1][:, piece * 4:piece * 4 + 4, :], S["wD_landed1"], DMA, S["wD_high"])
            for i in range(N_TILES + 1):
                if i < N_TILES:
                    act.wait_ge(S["x2_done"], 9 + i)
                    if i >= 2:
                        act.wait_ge(S[f"h2_stored{i % 2}"], DMA * (i // 2))
                        act.wait_ge(S["h2T_done"], i - 1)
                    act.activation(h2[:, i % 2, :], x2[:, i, :], ACT.Square, accum_out=n2[:, 0, i:i + 1]).then_inc(S["n2_sq"], 1)
                if i >= 1:
                    t = i - 1
                    act.wait_ge(S["h2T_done"], t + 1)
                    if t >= 2:
                        act.wait_ge(S["lg_done"], t - 1)
                    act.activation(h2T[:, t % 2, :, :].rearrange("p a b -> p (a b)"), SC[:, t % 2, :], ACT.Copy).then_inc(S["h2T_out"], 1)
            act.wait_ge(S["rstep"], R_GDIFF)
            act.activation(gexp[:], gdiff[:], ACT.Exp).then_inc(S["ract"], 1)
            act.wait_ge(S["rstep"], R_VDIFF)
            act.activation(vexp[:], vdiff[:], ACT.Exp).then_inc(S["ract"], 1)

            def high_slot(c, value):
                act.wait_ge(S[f"w_land{c}"], value)
                act.activation(w_high[c][:], w_in6[c][:], ACT.Copy).then_inc(S["gu_high" if c < 4 else "d_high"], 1)

            def x_high(value):
                act.wait_ge(S["xeT_done"], value)
                act.activation(xeH[:].rearrange("p a b -> p (a b)"), SC[:, 0, :], ACT.Copy).then_inc(S["xeH_done"], 1)

            def hid_high(value):
                act.wait_ge(S["hidT_done"], value)
                act.activation(hidH[:].rearrange("p a b -> p (a b)"), TB[:, :], ACT.Copy).then_inc(S["hidH_done"], 1)

            def gate_silu(e):
                act.wait_ge(S["w_free_gu"], e * 4 + 4)
                act.wait_ge(S["hid_done"], e)
                act.activation(silu[:], PROJ[0][:, :], ACT.Silu).then_inc(S["silu_done"], 1)

            for c in range(6):
                high_slot(c, DMA)
            x_high(1)
            high_slot(0, 2 * DMA)
            gate_silu(0)
            x_high(2)
            hid_high(1)
            for c in range(1, 4):
                high_slot(c, 2 * DMA)
            act.wait_ge(S["w_free_d"], 2)
            act.activation(y[:], SC[:, 1, :], ACT.Copy).then_inc(S["y_out"], 1)

            def expert_step(e, more):
                e16 = times(act, e, 16)
                if not isinstance(e, int) or e > 1:
                    high_slot(4, e16)
                    high_slot(5, e16)
                if more:
                    high_slot(0, e16 + 2 * DMA)
                gate_silu(e)
                if more:
                    x_high(e + 2)
                    for c in (1, 2, 3):
                        high_slot(c, e16 + 2 * DMA)
                else:
                    for c in (0, 1):
                        high_slot(c, e16 + 2 * DMA)
                if not isinstance(e, int) or e > 1:
                    act.wait_ge(S["w_free_d"], e * 2)
                    act.wait_ge(S["scattered"], e16 - DMA)
                    act.activation(y[:], SC[:, 1, :], ACT.Copy).then_inc(S["y_out"], 1)
                hid_high(e + 1)

            expert_step(1, True)
            with act.Fori(2, N_EXP - 1) as e:
                expert_step(e, True)
            expert_step(N_EXP - 1, False)
            act.wait_ge(S["w_free_d"], 2 * N_EXP)
            act.wait_ge(S["scattered"], DMA * (N_EXP - 1))
            act.activation(y[:], SC[:, 1, :], ACT.Copy).then_inc(S["y_out"], 1)

            def block_steps(n, e, b):
                act.wait_ge(S["v_w"], n * (6 * DMA) + 6 * DMA)
                for c in range(6):
                    act.activation(w_high[c][:], w_in6[c][:], ACT.Copy).then_inc(S["v_hi"], 1)
                x_high(n + (N_EXP + 1))
                act.wait_ge(S["w_free_gu"], n * 4 + 4 * (N_EXP + 1))
                act.activation(silu[:], PROJ[0][:, :], ACT.Silu).then_inc(S["silu_done"], 1)
                hid_high(n + (N_EXP + 1))
                act.wait_ge(S["w_free_d"], n * 2 + 2 * (N_EXP + 1))
                act.activation(y[:], SC[:, 1, :], ACT.Copy).then_inc(S["y_out"], 1)

            act.wait_ge(S["scattered"], DMA * N_EXP)
            overflow(act, block_steps)
            for i in range(N_TILES):
                act.wait_ge(S["res_done"], i + 1)
                act.dma_start(out_v[:, i, :], res[:, i % 4, :]).then_inc(S[f"out_stored{i % 4}"], DMA)

        @block.gpsimd
        def _(pool):
            mhalf = const("minus_half")
            pool.wait_ge(S["consts_in"], DMA)
            for i in range(N_TILES):
                pool.wait_ge(S["x_ms_done"], i + 1)
                pool.tensor_tensor(x_rstd[:, i:i + 1], x_ms[:, i:i + 1], mhalf[:, 0:1], ALU.pow).then_inc(S["x_rstd_done"], 1)
            pool.wait_ge(S["trig_done"], 2)
            def head_steps(h, steps):
                h8 = times(pool, h, 8)
                for s in steps:
                    (u0, i0, n0), (u1, i1, n1), (u2, i2, n2_), (u3, i3, n3) = [tile_at(s - lag) for lag in range(4)]
                    if s == 3:
                        pool.wait_ge(S["qkS_done"], h8 * 2 + FREE)
                        pool.wait_ge(S["sT_done"], h8 + FREE)
                        lo = CONST_AT["ret_q"][0]
                        pool.tensor_copy(head_c[:], consts[:, lo:lo + 16].rearrange("p (a b) -> p b a", b=4)[:, DS(h, 1), :]
                                         .rearrange("p a b -> p (a b)")).then_inc(S["head_consts"], 1)
                    if u3 == "A":
                        pool.wait_ge(S["o_ms"], h8 + (n3 + 1))
                        pool.tensor_tensor(rstd_o, ms_o, mhalf[:, 0:1], ALU.pow).then_inc(S["o_rstd"], 1)
                    if u3 == "B":
                        if i3 == 0:
                            pool.wait_ge(S["gn_landed"], h * 32 + 32)
                        pool.wait_ge(S["onR_done"], h8 + (n3 + 1) + FREE)
                        pool.tensor_tensor(onR[:], onR[:], gn_rows[:, 0, :], ALU.mult).then_inc(S["gate_step"], 1)
                        pool.wait_ge(S["gate_step"], h8 * 2 + (2 * n3 + 1))
                        pool.tensor_tensor(onR[:], onR[:], gn_rows[:, 1, :], ALU.add).then_inc(S["gate_step"], 1)
                        pool.wait_ge(S["gate_step"], h8 * 2 + (2 * n3 + 2))
                        pool.wait_ge(S["gTB"], h8 + n3 + FREE)
                        pool.tensor_tensor(gatedR[:], onR[:], sg[:, i3 % 2, :], ALU.mult).then_inc(S["gated"], 1)
                    if u1 == "B":
                        pool.wait_ge(S["egr"], h8 + (n1 + 1))
                        pool.wait_ge(S["gated"], h8 + max(n1 - 1, 0) + FREE)
                        pool.tensor_tensor(sg[:, i1 % 2, :], vg[:, i1 % 2, 128:256], eg[:], ALU.mult).then_inc(S["sg_done"], 1)
                    if u2 == "B":
                        pool.wait_ge(S["bn_v"], h8 + (n2_ + 1))
                        pool.tensor_tensor(bstat[:, 9:10], bstat[:, 8:9], mhalf[:, 0:1], ALU.pow).then_inc(S["bn_r"], 1)
                    if u0 == "A":
                        pool.wait_ge(S["msA_done"], h8 + (n0 + 1))
                        pool.tensor_tensor(rstd_qk, ms_qk, mhalf[:, 0:4], ALU.pow).then_inc(S["rstdA_done"], 1)
                    if u0 == "B":
                        sin = sin_t[:, i0, 8:72].unsqueeze(1).to_broadcast([P, 2, 64])
                        pool.wait_ge(S["qkS_done"], h8 * 2 + (2 * n0 + 2) + FREE)
                        pool.wait_ge(S["ropedB"], h8 * 2 + 2 * n0 + FREE)
                        pool.tensor_tensor(qkSin[:, 0:4:2, :], qkS[:, 1:4:2, :], sin, ALU.mult).then_inc(S["sinB"], 1)
                        pool.tensor_tensor(qkSin[:, 1:4:2, :], qkS[:, 0:4:2, :], sin, ALU.mult).then_inc(S["sinB"], 1)
                    if u1 == "A":
                        L = (i1 + 1) * 128
                        pool.wait_ge(S["exped"], h8 * 2 + (2 * n1 + 2) + FREE)
                        pool.wait_ge(S["rowsum_inv"], h8 * 2 + (2 * n1 + 2))
                        pool.tensor_tensor(probs[:, 1, 0:L], probs[:, 1, 0:L], rrow[:, 1:2].to_broadcast([P, L]), ALU.mult
                                           ).then_inc(S["p1_scaled"], 1)

            head_steps(0, FILL)
            with pool.Fori(0, N_HEADS) as h:
                head_steps(h, ROUND)
            for i in range(N_TILES):
                pool.wait_ge(S["n2_ms"], i + 1)
                pool.tensor_tensor(n2[:, 2, i:i + 1], n2[:, 1, i:i + 1], mhalf[:, 0:1], ALU.pow).then_inc(S["n2_rstd"], 1)

            def gather(col, chain, done):
                pool.tensor_copy(cur_gather[:], ids_gather[:, col]).then_inc(S["idx_copied"], 1)
                pool.wait_ge(S["idx_copied"], chain)
                pool.indirect_dma_start(out=xe[:], out_offset=None, in_=h2_dram,
                                        in_offset=bass.IndirectOffsetOnAxis(ap=cur_gather[:, 0:1], axis=0),
                                        bounds_check=1023, oob_is_err=False).then_inc(S[done], DMA)

            def scatter(col, chain, done):
                pool.tensor_copy(cur_scatter[:], ids_scatter[:, col]).then_inc(S["idx_copied"], 1)
                pool.wait_ge(S["idx_copied"], chain)
                pool.indirect_dma_start(out=y_dram, out_offset=bass.IndirectOffsetOnAxis(ap=cur_scatter[:, 0:1], axis=0),
                                        in_=y[:], in_offset=None,
                                        bounds_check=2047, oob_is_err=False).then_inc(S[done], DMA)

            for i in range(2):
                pool.wait_ge(S[f"h2_stored{i}"], 4 * DMA)
            pool.wait_ge(S["h2T_out"], 8)
            pool.memset(xe[:], 0.0).then_inc(S["xe_zero"], 1)
            pool.wait_ge(S["xe_zero"], 1)
            pool.wait_ge(S["ids_done"], 1)
            gather(slice(0, 1), 1, "xe_landed")
            pool.wait_ge(S["xeT_done"], 1)
            gather(slice(1, 2), 2, "xe_landed")
            pool.wait_ge(S["xeT_done"], 2)
            gather(slice(2, 3), 3, "xe_landed")

            def expert_step(e, more):
                pool.sem_clear(S["idx_copied"])
                n = 0
                if more:
                    pool.wait_ge(S["xeT_done"], e + 2)
                    gather(DS(e + 2, 1), 1, "xe_landed")
                    n = 1
                pool.wait_ge(S["y_out"], e + FREE)
                scatter(DS(e - 1, 1), n + 1, "scattered")

            with pool.Fori(1, N_EXP - 2) as e:
                expert_step(e, True)
            expert_step(N_EXP - 2, False)
            expert_step(N_EXP - 1, False)
            pool.wait_ge(S["y_out"], N_EXP + FREE)
            pool.wait_ge(S["scattered"], DMA * (N_EXP - 1))
            scatter(slice(N_EXP - 1, N_EXP), 2, "scattered")
            pool.wait_ge(S["scattered"], DMA * N_EXP)

            def block_moves(n, e, b):
                pool.sem_clear(S["idx_copied"])
                col = pool.snap(b * N_EXP + e)
                gather(DS(col, 1), 1, "xe_landed")
                pool.wait_ge(S["y_out"], n + (N_EXP + 1) + FREE)
                scatter(DS(col, 1), 2, "scattered")
                pool.wait_ge(S["scattered"], n * DMA + DMA * (N_EXP + 1))

            def tables_ready():
                pool.wait_ge(S["ids_done"], 2)

            overflow(pool, block_moves, tables_ready)
            pool.memset(cur_gather[:], 0).then_inc(S["rows_stored"], 1)

        @block.vector
        def _(dve):
            for i in range(N_TILES + 1):
                if i < N_TILES:
                    dve.wait_ge(S["x_sq_done"], i + 1)
                    dve.tensor_scalar(x_ms[:, i:i + 1], x_ss[:, i:i + 1], 1.0 / 1024, EPS, ALU.mult, ALU.add
                                      ).then_inc(S["x_ms_done"], 1)
                if i >= 1:
                    dve.wait_ge(S["x_rstd_done"], i)
                    dve.tensor_scalar(x_all[:, i - 1, :], x_all[:, i - 1, :], x_rstd[:, i - 1:i], None, ALU.mult
                                      ).then_inc(S["xn_done"], 1)
            for n in range(16):
                half, k = n // 8, n % 8
                dve.wait_ge(S["hH_done"], n + 1)
                dst = (slice(None), k, slice(half * 512, (half + 1) * 512))
                dve.scalar_tensor_tensor(hTL[dst], bank(n % 4), g1_cols[:, k:k + 1], hTH[dst].bitcast(F32),
                                         ALU.mult, ALU.subtract).then_inc(S["hL_done"], 1)
            steps = [0]

            def step(ins, name="ang_step"):
                steps[0] += 1
                ins.then_inc(S[name], 1)
                dve.wait_ge(S[name], steps[0])

            dve.wait_ge(S["small_in"], 9 * DMA)
            step(dve.tensor_copy(posf, posi[:]))
            step(dve.tensor_tensor(ang[:], posf.unsqueeze(2).to_broadcast([P, 8, 72]),
                                   const("freq").unsqueeze(1).to_broadcast([P, 8, 72]), ALU.mult))
            step(dve.tensor_scalar(turns[:], ang[:], 1.0 / (2 * math.pi), MAGIC, ALU.mult, ALU.add))
            step(dve.tensor_scalar(turns[:], turns[:], -MAGIC, None, ALU.add))
            for part in TWO_PI:
                step(dve.scalar_tensor_tensor(ang[:], turns[:], -part, ang[:], ALU.mult, ALU.add))
            step(dve.tensor_scalar(ang[:], ang[:], PI_BELOW, -PI_BELOW, ALU.min, ALU.max))
            dve.scalar_tensor_tensor(turns[:], ang[:], -1.0, ang[:], ALU.mult, ALU.max).then_inc(S["angle_done"], 1)
            dve.tensor_tensor(lam_prod[:], lam_rows[:, 0:4:2, :], lam_rows[:, 1:4:2, :], ALU.mult).then_inc(S["lam_step"], 1)
            dve.wait_ge(S["lam_step"], 1)
            dve.tensor_reduce(lam_s, lam_prod[:], AX_X, ALU.add).then_inc(S["lam_step"], 1)
            dve.wait_ge(S["lam_expd"], 1)
            dve.scalar_tensor_tensor(lam, lam_e[:, 0:1], LAM_INIT, lam_e[:, 1:2], ALU.add, ALU.subtract).then_inc(S["lam_step"], 1)
            dve.tensor_scalar(subln_scaled, subln_col, 1.0 - LAM_INIT, None, ALU.mult).then_inc(S["lam_step"], 1)

            def low(dst, src_, high_, ready, value, done, n=1):
                dve.wait_ge(ready, value)
                dve.tensor_tensor(dst, src_, high_.bitcast(F32), ALU.subtract).then_inc(done, n)

            for k in range(8):
                low(wAL[:, k, :], wA_in[:, k, :], wAH[:, k, :], S["wA_high"], k + 1, S["wA_low"])

            def head_steps(h, steps):
                h8, h7, h24 = times(dve, h, 8), times(dve, h, 7), times(dve, h, 24)

                def split_weights(s):
                    ks = PREP[s % 8]
                    kk = slice(ks[0], ks[-1] + 1)
                    if tile_at(s)[0] == "A":
                        low(wBL[:, kk, :], wB_in[:, kk, :], wBH[:, kk, :], S["wB_high"], h8 + kk.stop, S["wB_low"], len(ks))
                    else:
                        low(wAL[:, kk, :], wA_in[:, kk, :], wAH[:, kk, :], S["wA_high"], h8 + (8 + kk.stop), S["wA_low"], len(ks))

                for s in steps:
                    (u0, i0, n0), (u1, i1, n1), (u2, i2, n2_), (u3, i3, n3) = [tile_at(s - lag) for lag in range(4)]
                    src_bank = PROJ[s % 2]

                    def turned_weights():
                        dve.wait_ge(S["aT2"], h * 4 + (i2 - 3))
                        dve.tensor_copy(aT[:, 4:i2 + 1, :].rearrange("p a b -> p (a b)"), TB[:, 0:(i2 - 3) * 128]
                                        ).then_inc(S["t_free"], 1)

                    if u1 == "A":
                        dve.wait_ge(S["qkHA"], h8 * 2 + (2 * n1 + 2))
                        keys = slice(i1 * 128, (i1 + 1) * 128)
                        dve.tensor_tensor(QL[:], TB[:, 0:128], QH[:].bitcast(F32), ALU.subtract)
                        dve.tensor_tensor(KL[:, keys], TB[:, 128:256], KH[:, keys].bitcast(F32), ALU.subtract
                                          ).then_inc(S["t_free"], 1)
                    if u2 == "A":
                        L = (i2 + 1) * 128
                        dve.wait_ge(S["p1_scaled"], h8 + (n2_ + 1))
                        dve.scalar_tensor_tensor(probs[:, 0, 0:L], probs[:, 0, 0:L], rrow[:, 0:1], probs[:, 1, 0:L],
                                                 ALU.mult, ALU.subtract).then_inc(S["probs_done"], 1)
                    if u3 == "A":
                        dve.wait_ge(S["o_sq"], h8 + (n3 + 1))
                        dve.tensor_scalar(ms_o, ss_o, 1.0 / 128, EPS, ALU.mult, ALU.add).then_inc(S["o_ms"], 1)
                        dve.wait_ge(S["o_rstd"], h8 + (n3 + 1))
                        dve.tensor_scalar(oN[:], OB[:, 0:128], rstd_o, None, ALU.mult).then_inc(S["oN_done"], 1)
                    if u1 == "A":
                        L = (i1 + 1) * 128
                        dve.wait_ge(S["scored"], h8 + (n1 + 1))
                        dve.tensor_tensor(SC[:, :, L - 128:L], SC[:, :, L - 128:L],
                                          const("causal").unsqueeze(1).to_broadcast([P, 2, 128]), ALU.add).then_inc(S["masked"], 1)
                        dve.wait_ge(S["masked"], h8 + (n1 + 1))
                        dve.tensor_reduce(rowmax, SC[:, :, 0:L], AX_X, ALU.max).then_inc(S["maxed"], 1)
                        dve.wait_ge(S["maxed"], h8 + (n1 + 1))
                        dve.tensor_scalar(negmax, rowmax, -0.125, None, ALU.mult).then_inc(S["negged"], 1)
                    if u1 == "B":
                        dve.wait_ge(S["st_done"], h8 + (n1 + 1))
                        dve.scalar_tensor_tensor(sT[:, i1 % 2, :], bank(0)[:, 0:128], head_c[:, 3:4], const("tri"), ALU.mult, ALU.mult
                                                 ).then_inc(S["sT_done"], 1)
                    if u2 == "B":
                        dve.wait_ge(S["oB"], h8 + (n2_ + 1))
                        dve.bn_stats(bstat[:, 0:6], OB[:, 0:128]).then_inc(S["bn_s"], 1)
                        dve.wait_ge(S["bn_s"], 1)
                        dve.wait_ge(S["bn_s"], h8 + (n2_ + 1))
                        dve.bn_aggr(bstat[:, 6:8], bstat[:, 0:6]).then_inc(S["bn_a"], 1)
                        dve.wait_ge(S["bn_a"], h8 + (n2_ + 1))
                        dve.tensor_scalar(bstat[:, 8:9], bstat[:, 7:8], EPS, None, ALU.add).then_inc(S["bn_v"], 1)
                    if u1 == "B" and i1 < N_TILES - 1:
                        dve.wait_ge(S["kv_done"], h7 + (n1 + 1))
                        if i1 == 0:
                            dve.tensor_copy(U[:, 1, :], bank(2)[:, 0:128]).then_inc(S["U_done"], 1)
                        else:
                            dve.wait_ge(S["U_done"], h7 + n1 + FREE)
                            dve.scalar_tensor_tensor(U[:, (i1 + 1) % 2, :], U[:, i1 % 2, :], head_c[:, 2:3], bank(2)[:, 0:128],
                                                     ALU.mult, ALU.add).then_inc(S["U_done"], 1)
                    if s % 8 in PREP and u0 == "B":
                        split_weights(s)
                    if u2 == "B":
                        dve.wait_ge(S["bn_r"], h8 + (n2_ + 1))
                        dve.wait_ge(S["gated"], h8 + n2_ + FREE)
                        dve.tensor_scalar(onR[:], OB[:, 0:128], bstat[:, 6:7], bstat[:, 9:10], ALU.subtract, ALU.mult
                                          ).then_inc(S["onR_done"], 1)
                    if u0 == "A":
                        dve.wait_ge(S["sqA_done"], h8 + (n0 + 1))
                        dve.tensor_reduce(ss_qk, sqA[:].rearrange("p (g d) -> p g d", g=4), AX_X, ALU.add).then_inc(S["ssA_done"], 1)
                        dve.wait_ge(S["ssA_done"], h8 + (n0 + 1) + FREE)
                        dve.tensor_scalar(ms_qk, ss_qk, 1.0 / 64, EPS, ALU.mult, ALU.add).then_inc(S["msA_done"], 1)
                        if u2 == "A" and i2 >= 4:
                            turned_weights()
                        if s % 8 in PREP:
                            split_weights(s)
                        dve.wait_ge(S["rstdA_done"], h8 + (n0 + 1))
                        dve.wait_ge(S["vA_done"], h8 + (n0 + 1))
                        dve.wait_ge(S["qkTA"], h8 + n0 + FREE)
                        for g in range(4):
                            last = dve.scalar_tensor_tensor(qkA[:, g * 64:(g + 1) * 64], src_bank[:, g * 64:(g + 1) * 64],
                                                            rstd_qk[:, g:g + 1], gains[:, g // 2, :], ALU.mult, ALU.mult)
                        last.then_inc(S["normA_done"], 1)
                        dve.wait_ge(S["normA_done"], h8 + (n0 + 1))
                        x4 = qkA[:].rearrange("p (g d) -> p g d", g=4)[:, :, 0:16].rearrange("p g (a b) -> p g a b", a=2)
                        cos = cos_t[:, i0, 0:8].unsqueeze(1).unsqueeze(1).to_broadcast([P, 4, 2, 8])
                        sin = sin_t[:, i0, 0:8].unsqueeze(1).to_broadcast([P, 4, 8])
                        dve.wait_ge(S["ropedA"], h8 * 2 + 2 * n0 + FREE)
                        dve.tensor_tensor(rope_cos[:], x4, cos, ALU.mult).then_inc(S["ropeA_step"], 1)
                        dve.tensor_tensor(rope_sin[:, :, 0, :], x4[:, :, 1, :], sin, ALU.mult).then_inc(S["ropeA_step"], 1)
                        dve.tensor_tensor(rope_sin[:, :, 1, :], x4[:, :, 0, :], sin, ALU.mult).then_inc(S["ropeA_step"], 1)
                        dve.wait_ge(S["ropeA_step"], h24 + (3 * n0 + 3))
                        dve.tensor_tensor(x4[:, :, 0, :], rope_cos[:, :, 0, :], rope_sin[:, :, 0, :], ALU.subtract).then_inc(S["ropedA"], 1)
                        dve.tensor_tensor(x4[:, :, 1, :], rope_cos[:, :, 1, :], rope_sin[:, :, 1, :], ALU.add).then_inc(S["ropedA"], 1)
                    if u0 == "B":
                        cos = cos_t[:, i0, 8:72].unsqueeze(1).to_broadcast([P, 4, 64])
                        dve.wait_ge(S["qkS_done"], h8 * 2 + (2 * n0 + 2) + FREE)
                        dve.tensor_tensor(qkCos[:], qkS[:], cos, ALU.mult).then_inc(S["cosB"], 1)
                        dve.wait_ge(S["cosB"], h8 + (n0 + 1))
                        dve.wait_ge(S["sinB"], h8 * 2 + (2 * n0 + 2))
                        if i0:
                            dve.wait_ge(S["kv_done"], h7 + n0)
                        dve.tensor_tensor(qkR[:, 0:4:2, :], qkCos[:, 0:4:2, :], qkSin[:, 0:4:2, :], ALU.subtract).then_inc(S["ropedB"], 1)
                        dve.tensor_tensor(qkR[:, 1:4:2, :], qkCos[:, 1:4:2, :], qkSin[:, 1:4:2, :], ALU.add).then_inc(S["ropedB"], 1)
                        dve.wait_ge(S["eg_done"], h8 + (n0 + 1) + FREE)
                        dve.tensor_scalar(eg[:], eg[:], 1.0, None, ALU.add).then_inc(S["eg1"], 1)
                        dve.wait_ge(S["eg1"], h8 + (n0 + 1))
                        dve.reciprocal(eg[:], eg[:]).then_inc(S["egr"], 1)
                    if u2 == "A" and i2 >= 4 and u0 == "B":
                        turned_weights()
                    if u1 == "A":
                        dve.wait_ge(S["exped"], h8 * 2 + (2 * n1 + 2) + FREE)
                        dve.reciprocal(rrow, rowsum).then_inc(S["rowsum_inv"], 1)
                        dve.wait_ge(S["rowsum_inv"], h8 * 2 + (2 * n1 + 1))
                        dve.tensor_tensor(rrow[:, 1:2], rrow[:, 1:2], lam, ALU.mult).then_inc(S["rowsum_inv"], 1)

            head_steps(0, FILL)
            with dve.Fori(0, N_HEADS) as h:
                head_steps(h, ROUND)

            def low_C(value, sub, piece):
                dve.wait_ge(S["wC_high"], value)
                r = slice(piece * 8, piece * 8 + 8)
                dve.tensor_tensor(wCL[sub][:, r, :], wC_in[sub][:, r, :], wCH[sub][:, r, :].bitcast(F32), ALU.subtract
                                  ).then_inc(S["wC_low"], 1)

            dve.wait_ge(S["p1_scaled"], 8 * N_HEADS + 2)
            low_C(1, 0, 0)
            low_C(2, 0, 1)

            def merge_pair(j, last):
                j4, j8 = (j * 4, j * 8) if isinstance(j, int) else (dve.snap(j * 4), dve.snap(j * 8))
                for sub in range(2):
                    for th in range(2):
                        n = 2 * sub + th
                        b0 = 4 if th == 0 else 0
                        dve.wait_ge(S["sig_exp"], j8 + (2 * n + 2))
                        dve.tensor_scalar(sig[:], sig[:], 1.0, None, ALU.add).then_inc(S["sig_one"], 1)
                        dve.wait_ge(S["sig_one"], j4 + (n + 1))
                        dve.reciprocal(sig[:], sig[:]).then_inc(S["sig_inv"], 1)
                        dve.wait_ge(S["sig_inv"], j4 + (n + 1))
                        dve.wait_ge(S["ys_done"], j4 + (n + 1))
                        for g in range(2):
                            dve.tensor_tensor(sig[:, g, :], sig[:, g, :], bank(b0 + 2 + g), ALU.mult).then_inc(S["merged_step"], 1)
                        dve.wait_ge(S["merged_step"], j8 + (2 * n + 2))
                        m = 2 * j + sub
                        dve.tensor_tensor(merged[:, DS(m, 1), th * 512:(th + 1) * 512].rearrange("p a b -> p (a b)"),
                                          sig[:, 0, :], sig[:, 1, :], ALU.add).then_inc(S["sig_mul"], 2)
                        for piece in range(2):
                            r = slice(piece * 4, piece * 4 + 4)
                            if n == 0:
                                low_C(j4 + (3 + piece), 1, piece)
                            if n == 2 and not last:
                                low_C(j4 + (5 + piece), 0, piece)
                            if n == 2 and last:
                                low(wDL[0][:, r, :], wD_in[0][:, r, :], wDH[0][:, r, :], S["wD_high"], piece + 1, S["wD_low"])
                        if n == 2 and last:
                            for i in range(4):
                                low_merged(i)

            def low_merged(i):
                dve.wait_ge(S["mH"], i + 1)
                tok = slice(i * 128, i * 128 + 128)
                dve.tensor_tensor(mergedL[:, :, tok], merged[:, :, tok], mergedH[:, :, tok].bitcast(F32), ALU.subtract
                                  ).then_inc(S["mL"], 1)

            with dve.Fori(0, 3) as j:
                merge_pair(j, False)
            merge_pair(3, True)

            def add_residual(n, i):
                cnt = 8 * n + i
                cols = slice(n * 512, n * 512 + 512)
                if n == 0 and i % 2 == 0:
                    dve.wait_ge(S[f"x_in{i // 2}"], 2 * DMA)
                dve.wait_ge(S["d_done"], cnt + 1)
                dve.tensor_tensor(x2[:, i, cols], bank(4 + cnt % 3), x2[:, i, cols], ALU.add).then_inc(S["x2_done"], 1)

            for i in range(4, N_TILES):
                add_residual(0, i - 4)
                low_merged(i)
            add_residual(0, 4)
            add_residual(0, 5)
            for piece in range(2):
                r = slice(piece * 4, piece * 4 + 4)
                low(wDL[1][:, r, :], wD_in[1][:, r, :], wDH[1][:, r, :], S["wD_high"], piece + 3, S["wD_low"])
            add_residual(0, 6)
            add_residual(0, 7)

            dve.wait_ge(S["g2_in"], DMA)
            dve.wait_ge(S["router_in"], 4 * DMA)
            for i in range(N_TILES + 2):
                if i < N_TILES:
                    add_residual(1, i)
                    dve.wait_ge(S["n2_sq"], i + 1)
                    dve.tensor_scalar(n2[:, 1, i:i + 1], n2[:, 0, i:i + 1], 1.0 / 1024, EPS, ALU.mult, ALU.add
                                      ).then_inc(S["n2_ms"], 1)
                    dve.wait_ge(S["n2_rstd"], i + 1)
                    if i >= 2:
                        dve.wait_ge(S[f"h2_stored{i % 2}"], DMA * (i // 2))
                        dve.wait_ge(S["h2T_done"], i - 1)
                    dve.scalar_tensor_tensor(h2[:, i % 2, :], x2[:, i, :], n2[:, 2, i:i + 1], g2_row[:], ALU.mult, ALU.mult
                                             ).then_inc(S["h2_done"], 1)
                if i >= 2:
                    dve.wait_ge(S["lg_done"], i - 1)
                    dve.tensor_tensor(logits[:, i - 2, :], OB[:, 0:36], br[:], ALU.add).then_inc(S["logit_done"], 1)

            steps[0] = 0

            def rstep(ins):
                step(ins, "rstep")

            def b3(ap, shape):
                return ap.to_broadcast(shape)

            iota8 = const("iota_exp8").unsqueeze(1).to_broadcast([P, 8, 8])
            iota4 = const("iota_grp").unsqueeze(1).to_broadcast([P, 8, 4])
            dve.wait_ge(S["logit_done"], 8)
            gl = logits[:, :, 0:4]
            rstep(dve.tensor_reduce(gmax[:], gl, AX_X, ALU.max))
            rstep(dve.tensor_tensor(gdiff[:], gl, gmax[:].unsqueeze(2).to_broadcast([P, 8, 4]), ALU.subtract))
            assert steps[0] == R_GDIFF
            rstep(dve.tensor_scalar(gpen[:], gdiff[:], 0.0, 8.0, ALU.is_lt, ALU.mult))
            rstep(dve.tensor_tensor(gpen[:], gpen[:], iota4, ALU.add))
            rstep(dve.tensor_reduce(gidx[:], gpen[:], AX_X, ALU.min))
            rstep(dve.tensor_tensor(goh[:], gidx[:].unsqueeze(2).to_broadcast([P, 8, 4]), iota4, ALU.is_equal))
            rstep(dve.tensor_tensor(elsel[:], logits[:, :, 4:36].rearrange("p t (g e) -> p t g e", g=4),
                                    goh[:].unsqueeze(3).to_broadcast([P, 8, 4, 8]), ALU.mult))
            rstep(dve.tensor_reduce(el8[:], elsel[:].rearrange("p t g e -> p t e g"), AX_X, ALU.add))

            def best(values, c):
                rstep(dve.tensor_reduce(vtop[:, c, :], values[:], AX_X, ALU.max))
                rstep(dve.tensor_tensor(epen[:], values[:], vtop[:, c, :].unsqueeze(2).to_broadcast([P, 8, 8]), ALU.is_lt))
                rstep(dve.scalar_tensor_tensor(epen[:], epen[:], 16.0, iota8, ALU.mult, ALU.add))
                rstep(dve.tensor_reduce(eidx[:, c, :], epen[:], AX_X, ALU.min))

            best(el8, 0)
            rstep(dve.tensor_tensor(eoh[:], eidx[:, 0, :].unsqueeze(2).to_broadcast([P, 8, 8]), iota8, ALU.is_equal))
            rstep(dve.scalar_tensor_tensor(el8b[:], eoh[:], BIG_NEG, el8[:], ALU.mult, ALU.add))
            best(el8b, 1)
            rstep(dve.tensor_tensor(vdiff[:], vtop[:, 1, :], vtop[:, 0, :], ALU.subtract))
            assert steps[0] == R_VDIFF, steps[0]
            for c in range(2):
                rstep(dve.scalar_tensor_tensor(eglob[:, c, :], gidx[:], 8.0, eidx[:, c, :], ALU.mult, ALU.add))
            for c in range(2):
                rstep(dve.tensor_tensor(oh[:, c, :, :], eglob[:, c, :].unsqueeze(2).to_broadcast([P, 8, 32]),
                                        const("iota", 0, 32).unsqueeze(1).to_broadcast([P, 8, 32]), ALU.is_equal))
            rstep(dve.tensor_tensor(mask[:], oh[:, 0, :, :], oh[:, 1, :, :], ALU.add))
            rstep(dve.memset(before[:, 0, :], 0.0))
            for i in range(8):
                rstep(dve.tensor_tensor(before[:, i + 1, :], before[:, i, :], mask[:, i, :], ALU.add))
            assert steps[0] == R_BEFORE, steps[0]
            dve.wait_ge(S["ract"], 2)
            rstep(dve.tensor_reduce(gsum[:], gexp[:], AX_X, ALU.add))
            rstep(dve.reciprocal(pgrp[:], gsum[:]))
            rstep(dve.tensor_scalar(vden[:], vexp[:], 1.0, None, ALU.add))
            rstep(dve.reciprocal(vden[:], vden[:]))
            rstep(dve.tensor_tensor(wsel[:, 0, :], pgrp[:], vden[:], ALU.mult))
            rstep(dve.tensor_tensor(wsel[:, 1, :], wsel[:, 0, :], vexp[:], ALU.mult))
            dve.wait_ge(S["pmm"], 2)
            for c in range(2):
                rstep(dve.tensor_tensor(posm[:, c, :, :], oh[:, c, :, :],
                                        bank(0)[:, 0:256].rearrange("p (a b) -> p a b", a=8), ALU.mult))
            rstep(dve.tensor_reduce(pos[:].rearrange("p a b -> p (a b)"), posm[:].rearrange("p a b c -> p (a b) c"), AX_X, ALU.add))
            rstep(dve.tensor_copy(pos_i[:], pos[:]))
            rstep(dve.tensor_scalar(slot_i[:], pos_i[:], BLOCK - 1, None, ALU.bitwise_and))
            rstep(dve.tensor_scalar(blk_i[:], pos_i[:], BLOCK_BITS, None, ALU.logical_shift_right))
            rstep(dve.tensor_copy(slotf[:], slot_i[:]))
            rstep(dve.tensor_copy(blkf[:], blk_i[:]))
            rstep(dve.scalar_tensor_tensor(key[:], blkf[:], 32.0, eglob[:], ALU.mult, ALU.add))
            key16 = key[:].rearrange("p a b -> p (a b)").unsqueeze(2)
            rstep(dve.tensor_tensor(keyid1f[:], key16.to_broadcast([P, 16, 32]),
                                    const("iota", 0, 32).unsqueeze(1).to_broadcast([P, 16, 32]), ALU.is_equal))
            rstep(dve.tensor_tensor(keyid1[:], keyid1f[:], const("token1").unsqueeze(2).to_broadcast([P, 16, 32]), ALU.mult))
            for c in range(2):
                dve.tensor_tensor(pick[:, 8 * c:8 * c + 8, :], slotf[:, c, :].unsqueeze(2).to_broadcast([P, 8, 128]),
                                  const("iota", 0, 128).unsqueeze(1).to_broadcast([P, 8, 128]), ALU.is_equal
                                  ).then_inc(S["pick_done"], 1)
            rstep(dve.tensor_copy(counts_f[:, 0:32], bank(1)[:, 0:32]))
            rstep(dve.tensor_reduce(counts_f[:, 32:33], counts_f[:, 0:32], AX_X, ALU.max))
            rstep(dve.tensor_copy(counts_i[:], counts_f[:]))

            def row_ids(n_keys):
                rstep(dve.tensor_scalar(padded[:, 0:n_keys], bank(2)[:, 0:n_keys], 0.0, 4096.0, ALU.is_equal, ALU.mult))
                rstep(dve.scalar_tensor_tensor(zf[:, 0:n_keys], bank(2)[:, 0:n_keys], -1.0, padded[:, 0:n_keys], ALU.add, ALU.add))
                rstep(dve.tensor_copy(ids_scatter[:, 0:n_keys], zf[:, 0:n_keys]))
                dve.tensor_scalar(ids_gather[:, 0:n_keys], ids_scatter[:, 0:n_keys], 3071, None, ALU.bitwise_and
                                  ).then_inc(S["ids_done"], 1)

            def low_slot(c, value):
                dve.wait_ge(S["gu_high" if c < 4 else "d_high"], value)
                dve.tensor_tensor(w_low[c][:], w_in6[c][:], w_high[c][:].bitcast(F32), ALU.subtract
                                  ).then_inc(S["gu_low" if c < 4 else "d_low"], 1)

            low_slot(0, 1)
            dve.wait_ge(S["pmm"], 3)
            row_ids(32)

            def all_tables():
                for q in range(16):
                    c, i = q // 8, q % 8
                    if q >= 2:
                        dve.wait_ge(S["pick_used"], q - 1)
                    dve.tensor_scalar(keyid[q % 2][:], const("iota"), key[:, c, i:i + 1], const("token1", q, q + 1),
                                      ALU.is_equal, ALU.mult).then_inc(S["pick_done"], 1)
                dve.wait_ge(S["pick_used"], 16)
                row_ids(32 * MAX_BLOCKS)

            def x_low(value):
                dve.wait_ge(S["xeH_done"], value)
                dve.tensor_tensor(xeL[:].rearrange("p a b -> p (a b)"), SC[:, 0, :],
                                  xeH[:].rearrange("p a b -> p (a b)").bitcast(F32), ALU.subtract).then_inc(S["xeL_done"], 1)

            def hidden(value):
                dve.wait_ge(S["silu_done"], value)
                dve.tensor_tensor(hid[:], silu[:], PROJ[1][:, :], ALU.mult).then_inc(S["hid_done"], 1)

            def hid_low(value):
                dve.wait_ge(S["hidH_done"], value)
                dve.tensor_tensor(hidL[:].rearrange("p a b -> p (a b)"), TB[:, :],
                                  hidH[:].rearrange("p a b -> p (a b)").bitcast(F32), ALU.subtract).then_inc(S["hidL_done"], 1)

            for c in (1, 2):
                low_slot(c, c + 1)
            x_low(1)
            low_slot(3, 4)
            low_slot(4, 1)
            low_slot(5, 2)
            low_slot(0, 5)
            hidden(1)
            x_low(2)
            hid_low(1)
            for c in range(1, 4):
                low_slot(c, 4 + c + 1)

            def expert_step(e, more):
                e4, e2 = times(dve, e, 4), times(dve, e, 2)
                if not isinstance(e, int) or e > 1:
                    low_slot(4, e2 - 1)
                    low_slot(5, e2)
                if more:
                    low_slot(0, e4 + 5)
                hidden(e + 1)
                if more:
                    x_low(e + 2)
                    for c in (1, 2, 3):
                        low_slot(c, e4 + (5 + c))
                else:
                    for c in (0, 1):
                        low_slot(c, e4 + (5 + c))
                hid_low(e + 1)

            expert_step(1, True)
            with dve.Fori(2, N_EXP - 1) as e:
                expert_step(e, True)
            expert_step(N_EXP - 1, False)

            def block_lows(n, e, b):
                for c in range(6):
                    dve.wait_ge(S["v_hi"], n * 6 + (c + 1))
                    dve.tensor_tensor(w_low[c][:], w_in6[c][:], w_high[c][:].bitcast(F32), ALU.subtract).then_inc(S["v_lo"], 1)
                x_low(n + (N_EXP + 1))
                hidden(n + (N_EXP + 1))
                hid_low(n + (N_EXP + 1))

            dve.wait_ge(S["scattered"], DMA * N_EXP)
            overflow(dve, block_lows, all_tables)
            for i in range(N_TILES):
                b = i % 4
                dve.wait_ge(S[f"comb_in{b}"], 2 * DMA * (i // 4 + 1))
                if i >= 4:
                    dve.wait_ge(S[f"out_stored{b}"], DMA * (i // 4))
                dve.scalar_tensor_tensor(res[:, b, :], comb[:, b, 0, :], wsel[:, 0, i:i + 1], x2[:, i, :], ALU.mult, ALU.add
                                         ).then_inc(S["comb_mid"], 1)
                dve.wait_ge(S["comb_mid"], i + 1)
                dve.scalar_tensor_tensor(res[:, b, :], comb[:, b, 1, :], wsel[:, 1, i:i + 1], res[:, b, :], ALU.mult, ALU.add
                                         ).then_inc(S["res_done"], 1)


R_GDIFF, R_VDIFF, R_BEFORE = 2, 19, 33
BLOCK_BITS = 7
MAGIC = 1.5 * 2.0 ** 23
TWO_PI = (6.28125, 0.001934051513671875, 1.2556659146e-6)
PI_BELOW = 3.1415925

_INS = ["x", "positions", "norm1_g", "w_in", "q_norm_g", "k_norm_g", "lambda_q1", "lambda_k1", "lambda_q2", "lambda_k2",
        "diff_subln_g", "ret_gn_g", "ret_gn_b", "w_branch_a", "w_branch_b", "w_out", "norm2_g",
        "w_group_router", "b_group_router", "w_expert_router", "b_expert_router", "w_gate", "w_up", "w_down"]


def kernel(**inputs):
    import concourse.bacc as bacc
    from concourse.bass_utils import run_bass_kernel_spmd

    nc = bacc.Bacc("TRN2", target_bir_lowering=False, num_devices=1)
    arrays, tensors = {}, {}
    for name in _INS:
        arrays[f"in_{name}"] = np.ascontiguousarray(inputs[name])
    arrays["in_consts"] = constants()
    for full, a in arrays.items():
        tensors[full[3:]] = nc.dram_tensor(full, a.shape, mybir.dt.from_np(a.dtype), kind="ExternalInput").ap()
    tensors["out"] = nc.dram_tensor("out_0", (1, 1024, 1024), F32, kind="ExternalOutput").ap()
    decoder_layer(nc, tensors)
    r = run_bass_kernel_spmd(nc, [arrays], core_ids=[0])
    return r.results[0]["out_0"]
```

```python
from contextlib import ExitStack
import math

import numpy as np

import concourse.bass as bass
from concourse import mybir

ALU = mybir.AluOpType
ACT = mybir.ActivationFunctionType
AX_X = mybir.AxisListType.X
F32 = mybir.dt.float32
F32R = mybir.dt.float32r
I32 = mybir.dt.int32
DS = bass.ds

P = 128
EPS = 1e-6
BIG_NEG = -1.0e30
QA, KA, VA, QB, KB, VB, GB, GATE_A, GATE_B = 0, 512, 1024, 1536, 2048, 2560, 3072, 3584, 4608
N_TILES = 8
N_KD = 8
N_HEADS = 4
N_EXP = 32
LAM_INIT = 0.8 - 0.6 * math.exp(-0.3 * 0)
BLOCK = 128
MAX_BLOCKS = 8
FREE = 1
SIG_FREE = 3
DMA = 16

R_GDIFF, R_VDIFF, R_BEFORE = 2, 19, 33
BLOCK_BITS = 7
MAGIC = 1.5 * 2.0 ** 23
TWO_PI = (6.28125, 0.001934051513671875, 1.2556659146e-6)
PI_BELOW = 3.1415925

CONST_WIDTHS = [
    ("ident", 128), ("tri", 128), ("causal", 128), ("strict", 128), ("ones", 128), ("iota", 256),
    ("freq", 72), ("ret_q", 4), ("ret_k", 4), ("ret_g", 4), ("ret_ginv", 4),
    ("token1", 16), ("minus_half", 16), ("half_pi", 1), ("iota_grp", 4), ("iota_exp8", 8),
]
CONST_AT = {}
_at = 0
for _name, _width in CONST_WIDTHS:
    CONST_AT[_name] = (_at, _at + _width)
    _at += _width
N_CONST = _at


def constants():
    p = np.arange(P)
    c = {}
    c["ident"] = np.eye(P)
    c["tri"] = (p[:, None] <= p[None, :]).astype(np.float64)
    c["causal"] = np.where(p[None, :] <= p[:, None], 0.0, BIG_NEG)
    c["strict"] = (p[:, None] < p[None, :]).astype(np.float64)
    c["ones"] = np.ones((P, P))
    c["iota"] = np.tile(np.arange(256.0), (P, 1))
    fa = np.power(np.float32(500000.0), (-2.0 * np.arange(8, dtype=np.float32) / np.float32(16)).astype(np.float32))
    fr = np.power(np.float32(10000.0), (-2.0 * np.arange(64, dtype=np.float32) / np.float32(128)).astype(np.float32))
    c["freq"] = np.tile(np.concatenate([fa, fr]), (P, 1))
    gamma = 1.0 - 2.0 ** (-5.0 - np.arange(4.0))
    c["ret_q"] = gamma[None, :] ** (p[:, None] + 1.0 + P)
    c["ret_k"] = gamma[None, :] ** (-(p[:, None] + 1.0)) * P ** -0.5
    c["ret_g"] = np.tile(gamma ** P, (P, 1))
    c["ret_ginv"] = np.tile(gamma ** -P, (P, 1))
    c["token1"] = (p[:, None] + 1.0) + 128.0 * np.arange(16)[None, :]
    c["minus_half"] = np.full((P, 16), -0.5)
    c["half_pi"] = np.full((P, 1), np.pi / 2)
    c["iota_grp"] = np.tile(np.arange(4.0), (P, 1))
    c["iota_exp8"] = np.tile(np.arange(8.0), (P, 1))
    return np.concatenate([c[name] for name, _ in CONST_WIDTHS], axis=1).astype(np.float32)


def split3(pe, out, left, right, start, stop):
    (lh, ll), (rh, rl) = left, right
    pe.matmul(out, lh, rh, start=start, stop=False)
    pe.matmul(out, lh, rl, start=False, stop=False)
    return pe.matmul(out, ll, rh, start=False, stop=stop)


def decoder_layer(nc, T):
    with ExitStack() as ctx:
        limit = nc.sbuf_usable_end
        cursor = [(nc.sbuf_base + 63) // 64 * 64]

        def place(size):
            at = cursor[0]
            cursor[0] = (at + size + 31) // 32 * 32
            assert cursor[0] <= limit, (cursor[0], limit)
            return at

        def sb(name, shape, dt=F32, at=None):
            size = int(np.prod(shape[1:])) * 4
            return nc.alloc_sbuf_tensor_at(name, shape, dt, offset=place(size) if at is None else at)

        def psum(name, shape):
            return ctx.enter_context(nc.psum_tensor(name, shape, F32))

        def sem(name):
            return ctx.enter_context(nc.semaphore(name))

        KIB = 1024

        consts = sb("consts", [P, N_CONST])

        def const(name, a=0, b=None):
            lo, hi = CONST_AT[name]
            return consts[:, lo + a:(hi if b is None else lo + b)]

        ident = const("ident")
        small = sb("small", [P, 64])
        g1_cols = small[:, 0:8]
        subln_col = small[:, 8:9]
        subln_scaled = small[:, 9:10]
        lam = small[:, 10:11]
        lam_e = small[:, 12:14]
        lam_s = small[:, 14:16]
        x_ss = small[:, 16:24]
        x_rstd = small[:, 24:32]
        x_ms = small[:, 32:40]
        posf = small[:, 40:48]
        posi = sb("posi", [P, 8], I32)

        R_HT, R_A, R_B, R_OT = place(64 * KIB), place(24 * KIB), place(32 * KIB), place(32 * KIB)
        R_WORK = cursor[0]

        hTH = sb("hTH", [P, N_KD, 1024], F32R, at=R_HT)
        hTL = sb("hTL", [P, N_KD, 1024], F32R, at=R_HT + 32 * KIB)
        wA_in = sb("wA_in", [P, N_KD, 384], F32, at=R_A)
        wAL = sb("wAL", [P, N_KD, 384], F32R, at=R_A)
        wAH = sb("wAH", [P, N_KD, 384], F32R, at=R_A + 12 * KIB)
        wB_in = sb("wB_in", [P, N_KD, 512], F32, at=R_B)
        wBL = sb("wBL", [P, N_KD, 512], F32R, at=R_B)
        wBH = sb("wBH", [P, N_KD, 512], F32R, at=R_B + 16 * KIB)
        x_all = sb("x_all", [P, N_TILES, 1024], F32, at=R_B)
        oT = sb("oT", [P, 8, 1024], F32, at=R_OT)
        x_sq = sb("x_sq", [P, 1024], F32, at=R_OT)
        lam_rows = sb("lam_rows", [P, 4, 64], F32, at=R_OT + 4 * KIB)
        lam_prod = sb("lam_prod", [P, 2, 64], F32, at=R_OT + 6 * KIB)
        ang = sb("ang", [P, N_TILES, 72], F32, at=R_OT + 8 * KIB)
        turns = sb("turns", [P, N_TILES, 72], F32, at=R_OT + 12 * KIB)
        turn_part = sb("turn_part", [P, N_TILES, 72], F32, at=R_OT + 16 * KIB)

        sin_t = sb("sin_t", [P, N_TILES, 72])
        cos_t = sb("cos_t", [P, N_TILES, 72])
        gains = sb("gains", [P, 2, 64])
        gn_rows = sb("gn_rows", [P, 2, 128])
        qkTH = sb("qkTH", [P, 1 + N_TILES, 128], F32R)
        qkTL = sb("qkTL", [P, 1 + N_TILES, 128], F32R)
        V = sb("V", [P, N_TILES, 128])
        probs = sb("probs", [P, 2, 1024])
        aT = sb("aT", [P, N_TILES, 128])
        sqA = sb("sqA", [P, 256])
        qkA = sb("qkA", [P, 256])
        rope_cos = sb("rope_cos", [P, 4, 2, 8])
        rope_sin = sb("rope_sin", [P, 4, 2, 8])
        oN = sb("oN", [P, 128])
        stats = sb("stats", [P, 32])
        ss_qk, ms_qk, rstd_qk = stats[:, 0:4], stats[:, 4:8], stats[:, 8:12]
        negmax, rowmax, rowsum, rrow = stats[:, 12:14], stats[:, 14:16], stats[:, 16:18], stats[:, 18:20]
        map2_scale, o_scale, sq_scale = stats[:, 23:24], stats[:, 24:26], stats[:, 26:28]
        ss_o, ms_o, rstd_o = stats[:, 20:21], stats[:, 21:22], stats[:, 22:23]
        qkS = sb("qkS", [P, 4, 64])
        qkCos = sb("qkCos", [P, 4, 64])
        qkSin = sb("qkSin", [P, 4, 64])
        qkR = sb("qkR", [P, 4, 64])
        vg = sb("vg", [P, 2, 256])
        eg = sb("eg", [P, 128])
        sg = sb("sg", [P, 2, 128])
        qkT = sb("qkT", [P, 2, 256])
        sT = sb("sT", [P, 2, 128])
        U = sb("U", [P, 2, 128])
        onR = sb("onR", [P, 128])
        gatedR = sb("gatedR", [P, 128])
        bstat = sb("bstat", [P, 16])
        head_c = sb("head_c", [P, 4])

        wC_at = [R_A, R_B]
        wC_in = [sb(f"wC_in{i}", [P, 24, 128], F32, at=wC_at[i]) for i in range(2)]
        wCL = [sb(f"wCL{i}", [P, 16, 128], F32R, at=wC_at[i]) for i in range(2)]
        wCH = [sb(f"wCH{i}", [P, 16, 128], F32R, at=wC_at[i] + 12 * KIB) for i in range(2)]
        merged = sb("merged", [P, N_KD, 1024], F32, at=R_WORK)
        mergedL = sb("mergedL", [P, N_KD, 1024], F32R, at=R_WORK)
        sig = sb("sig", [P, 2, 512], F32, at=R_WORK + 32 * KIB)
        mergedH = sb("mergedH", [P, N_KD, 1024], F32R, at=R_OT)
        wD_at = [R_A, R_HT]
        wD_in = [sb(f"wD_in{i}", [P, N_KD, 512], F32, at=wD_at[i]) for i in range(2)]
        wDL = [sb(f"wDL{i}", [P, N_KD, 512], F32R, at=wD_at[i]) for i in range(2)]
        wDH_at = [[R_A + 16 * KIB, R_WORK + 36 * KIB], [R_HT + 16 * KIB, R_HT + 24 * KIB]]
        wDH = [[sb(f"wDH{i}_{j}", [P, 4, 512], F32R, at=wDH_at[i][j]) for j in range(2)] for i in range(2)]
        x2 = sb("x2", [P, N_TILES, 1024], F32, at=R_HT + 32 * KIB)
        h2 = sb("h2", [P, 2, 1024], F32, at=R_A)
        h2T = sb("h2T", [P, 2, N_KD, 128], F32, at=R_A + 8 * KIB)
        g2_row = sb("g2_row", [P, 1024], F32, at=R_A + 16 * KIB)

        wr = sb("wr", [P, N_KD, 36], F32, at=R_A + 20 * KIB)
        br = sb("br", [P, 36], F32, at=R_A + 22 * KIB)
        route_at = [max(cursor[0], R_WORK + 37 * KIB)]

        def rt(name, shape, dt=F32):
            at = route_at[0]
            route_at[0] = (at + int(np.prod(shape[1:])) * 4 + 31) // 32 * 32
            assert route_at[0] <= limit, (name, route_at[0], limit)
            return nc.alloc_sbuf_tensor_at(name, shape, dt, offset=at)

        logits = rt("logits", [P, N_TILES, 36])
        stats2 = rt("stats2", [P, 4, 8])
        wsel = rt("wsel", [P, 2, N_TILES])
        q_at = [R_WORK]

        def rq(name, shape, dt=F32):
            at = q_at[0]
            q_at[0] = (at + int(np.prod(shape[1:])) * 4 + 31) // 32 * 32
            return nc.alloc_sbuf_tensor_at(name, shape, dt, offset=at)

        gmax = rq("gmax", [P, 8])
        gdiff = rq("gdiff", [P, 8, 4])
        gexp = rq("gexp", [P, 8, 4])
        gsum = rq("gsum", [P, 8])
        pgrp = rq("pgrp", [P, 8])
        gpen = rq("gpen", [P, 8, 4])
        gidx = rq("gidx", [P, 8])
        goh = rq("goh", [P, 8, 4])
        elsel = rq("elsel", [P, 8, 4, 8])
        el8 = rq("el8", [P, 8, 8])
        vtop = rq("vtop", [P, 2, 8])
        epen = rq("epen", [P, 8, 8])
        eidx = rq("eidx", [P, 2, 8])
        eoh = rq("eoh", [P, 8, 8])
        el8b = rq("el8b", [P, 8, 8])
        vdiff = rq("vdiff", [P, 8])
        vexp = rq("vexp", [P, 8])
        vden = rq("vden", [P, 8])
        eglob = rq("eglob", [P, 2, 8])
        oh = rq("oh", [P, 2, 8, 32])
        mask = rq("mask", [P, 8, 32], F32R)
        before = rq("before", [P, 9, 32], F32R)
        count_masks = rq("count_masks", [P, 256], F32R)
        posm = rq("posm", [P, 2, 8, 32])
        pos = rq("pos", [P, 2, 8])
        pos_i = rq("pos_i", [P, 2, 8], I32)
        slot_i = rq("slot_i", [P, 2, 8], I32)
        blk_i = rq("blk_i", [P, 2, 8], I32)
        slotf = rq("slotf", [P, 2, 8])
        blkf = rq("blkf", [P, 2, 8])
        key = rq("key", [P, 2, 8])
        pick = rq("pick", [P, 16, 128], F32R)
        keyid1f = rq("keyid1f", [P, 16, 32])
        keyid1 = rq("keyid1", [P, 16, 32], F32R)
        keyid = [rq(f"keyid{i}", [P, 256], F32R) for i in range(2)]
        padded = rq("padded", [P, 256])
        zf = rq("zf", [P, 256])
        ids_scatter = rt("ids_scatter", [P, 256], I32)
        ids_gather = rt("ids_gather", [P, 256], I32)
        counts_f = rq("counts_f", [P, 33])
        counts_i = rt("counts_i", [P, 33], I32)
        cur_gather = rt("cur_gather", [P, 1], I32)
        cur_scatter = rt("cur_scatter", [P, 1], I32)

        slot_at = [R_B, R_B + 16 * KIB, R_HT, R_HT + 16 * KIB, R_OT, R_OT + 16 * KIB]
        w_in6 = [sb(f"w_slot{i}", [P, 2048], F32, at=slot_at[i]) for i in range(6)]
        w_low = [sb(f"w_low{i}", [P, 2048], F32R, at=slot_at[i]) for i in range(6)]
        w_high = [sb(f"w_high{i}", [P, 2048], F32R, at=slot_at[i] + 8 * KIB) for i in range(6)]
        xe = sb("xe", [P, 1024], F32, at=R_A)
        xeH = sb("xeH", [P, 8, 128], F32R, at=R_A + 4 * KIB)
        xeL = sb("xeL", [P, 8, 128], F32R, at=R_A + 8 * KIB)
        silu = sb("silu", [P, 512], F32, at=R_A + 12 * KIB)
        hid = sb("hid", [P, 512], F32, at=R_A + 14 * KIB)
        hidH = sb("hidH", [P, 4, 128], F32R, at=R_A + 16 * KIB)
        hidL = sb("hidL", [P, 4, 128], F32R, at=R_A + 18 * KIB)
        y = sb("y", [P, 1024], F32, at=R_A + 20 * KIB)
        comb = sb("comb", [P, 4, 2, 1024], F32, at=R_OT)
        res = sb("res", [P, 4, 1024], F32, at=R_B)

        PROJ = [psum("proj0", [P, 512]), psum("proj1", [P, 512])]
        SC = psum("scores", [P, 2, 1024])
        TB = psum("turned", [P, 512])
        OB = psum("outs", [P, 512])

        h2_dram = nc.dram_tensor("h2_rows", (1024, 1024), F32, kind="Internal").ap()
        y_dram = nc.dram_tensor("y_rows", (2048, 1024), F32, kind="Internal").ap()

        w_in_v = T["w_in"][0].rearrange("(k p) c -> p k c", p=P)
        wa_v = T["w_branch_a"][0].rearrange("(k p) c -> p k c", p=P)
        wb_v = T["w_branch_b"][0].rearrange("(k p) c -> p k c", p=P)
        wo_v = T["w_out"][0].rearrange("(k p) c -> p k c", p=P)
        x_v = T["x"][0].rearrange("(i p) d -> p i d", p=P)
        out_v = T["out"][0].rearrange("(i p) d -> p i d", p=P)
        h2_v = h2_dram.rearrange("(i p) d -> p i d", p=P)
        y_v = y_dram.rearrange("(c i p) d -> p c i d", c=2, p=P)
        wg_v = T["w_gate"][0].rearrange("e (p k) f -> e p (k f)", p=P)
        wu_v = T["w_up"][0].rearrange("e (p k) f -> e p (k f)", p=P)
        wd_v = T["w_down"][0].rearrange("e (p k) n -> e p (k n)", p=P)

        def bank(n):
            if n < 4:
                return SC[:, n // 2, (n % 2) * 512:(n % 2) * 512 + 512]
            return [PROJ[0], PROJ[1], TB, OB][n - 4][:, :]

        names = """pos_in g1_in rows_stored consts_in small_in x_in0 x_in1 x_in2 x_in3 x_sq_done x_ms_done x_rstd_done
            xn_done xT_done hH_done hL_done lam_step lam_expd ang_step angle_done trig_done
            wA_landed wA_high wA_low wB_landed wB_high wB_low gn_landed t_free projA projB sqA_done
            vA_done ssA_done msA_done rstdA_done normA_done ropeA_step ropedA qkTA qkHA scored
            masked maxed negged exped rowsum_inv probs_done aT1 aT2 pv_done o_sq o_ms o_rstd oN_done
            oTA qkS_done vg_done eg_done cosB sinB ropedB eg1 egr sg_done qkTB kv_done U_done
            st_done sT_done oB bn_s bn_a bn_v bn_r onR_done gate_step gated gTB wC_landed0
            wC_landed1 wC_high wC_low gates_done ys_done sig_exp sig_one sig_inv sig_mul merged_step
            wD_landed0 wD_landed1 wD_high wD_low mH mL d_done x2_done g2_in router_in n2_sq n2_ms
            n2_rstd h2_done h2T_done h2T_out lg_done logit_done h2_stored0 h2_stored1 rstep ract pmm
            pick_done pick_used ids_done w_land0 w_land1 w_land2 w_land3 w_land4 w_land5 w_free_gu
            w_free_d idx_copied xe_landed xeT_done xeH_done xeL_done silu_done hid_done hidT_done
            hidH_done hidL_done y_out scattered comb_in0 comb_in1 comb_in2 comb_in3 comb_mid
            res_done out_stored0 out_stored1 out_stored2 out_stored3 head_consts gu_high gu_low
            d_high d_low xe_zero v_w v_hi v_lo""".split()
        S = {n: sem(n) for n in names}

        block = ctx.enter_context(nc.Block())
        FILL, ROUND = range(0, 3), range(3, 19)
        PREP = {3: [0, 1], 4: [2], 5: [3, 4], 6: [5], 7: [6, 7]}
        PREP_C = {3: 0, 5: 1}

        def tile_at(s):
            if s < 0:
                return None, 0, 0
            if s < 2 * N_TILES:
                return "AB"[s // N_TILES], s % N_TILES, s % N_TILES
            return "A", s - 2 * N_TILES, s - N_TILES

        def tiles_of(s, more):
            return [(None, 0, 0) if s - lag >= 2 * N_TILES and not more else tile_at(s - lag) for lag in range(4)]

        def times(eng, h, n):
            return h * n if isinstance(h, int) else eng.snap(h * n)

        def overflow(eng, block_of, first=None):
            most = eng.value_load(counts_i[0:1, 32:33], min_val=0, max_val=1024)
            with eng.If(most > BLOCK):
                if first:
                    first()
                n = eng.alloc_register()
                eng.reg_mov(n, 0)
                with eng.Fori(1, MAX_BLOCKS) as b:
                    with eng.Fori(0, N_EXP) as e:
                        held = eng.value_load(counts_i[0:1, DS(e, 1)], min_val=0, max_val=1024)
                        with eng.If(held > b * BLOCK):
                            block_of(eng.snap(n), e, b)
                            eng.reg_add(n, n, 1)
                        with eng.Else():
                            eng.nop()
                        eng.nop()
                eng.nop()
            with eng.Else():
                eng.nop()
            eng.nop()

        STARTS_FREE = """t_free ssA_done ropedB sg_done qkTA ropedA gated gTB U_done sT_done
            exped eg_done onR_done pv_done projB qkS_done y_out""".split()

        @block.sync
        def _(sp):
            for name in STARTS_FREE:
                sp.sem_inc(S[name], FREE)
            sp.sem_inc(S["sig_mul"], SIG_FREE)
            sp.dma_start(x_all[:, 0:2, :], x_v[:, 0:2, :]).then_inc(S["x_in0"], DMA)
            sp.dma_start(consts[:], T["consts"]).then_inc(S["consts_in"], DMA)
            sp.dma_start(g1_cols, T["norm1_g"][0].rearrange("(k p) -> p k", p=P),
                         allow_slow_non_contiguous=True).then_inc(S["g1_in"], DMA)
            sp.dma_start(posi[:], T["positions"][0].rearrange("(i p) -> p i", p=P),
                         allow_slow_non_contiguous=True).then_inc(S["pos_in"], DMA)
            sp.dma_start(x_all[:, 2:4, :], x_v[:, 2:4, :]).then_inc(S["x_in1"], DMA)

            def load_A(head):
                for j, col in enumerate((QA, KA, VA)):
                    sp.dma_start(wA_in[:, :, 128 * j:128 * j + 128],
                                 w_in_v[:, :, DS(head * 128 + col, 128)]).then_inc(S["wA_landed"], DMA)

            load_A(0)
            for j in (2, 3):
                sp.dma_start(x_all[:, 2 * j:2 * j + 2, :], x_v[:, 2 * j:2 * j + 2, :]).then_inc(S[f"x_in{j}"], DMA)
            sp.dma_start(subln_col, T["diff_subln_g"][0].rearrange("(p o) -> p o", o=1),
                         allow_slow_non_contiguous=True).then_inc(S["small_in"], DMA)
            for j, n in enumerate(("lambda_q1", "lambda_k1", "lambda_q2", "lambda_k2")):
                sp.dma_start(lam_rows[:, j, :], T[n][0].partition_broadcast(P)).then_inc(S["small_in"], DMA)
            for j, n in enumerate(("q_norm_g", "k_norm_g")):
                sp.dma_start(gains[:, j, :], T[n][0].partition_broadcast(P)).then_inc(S["small_in"], DMA)

            sp.wait_ge(S["xT_done"], 16)

            def load_B(h, h8):
                sp.wait_ge(S["projB"], h8 + FREE)
                for j, col in enumerate((QB, KB, VB, GB)):
                    sp.dma_start(wB_in[:, :, 128 * j:128 * j + 128],
                                 w_in_v[:, :, DS(h * 128 + col, 128)]).then_inc(S["wB_landed"], DMA)
                sp.wait_ge(S["xT_done"], 16)
                sp.wait_ge(S["gated"], h8 + FREE)
                for j, n in enumerate(("ret_gn_g", "ret_gn_b")):
                    sp.dma_start(gn_rows[:, j, :],
                                 T[n][0][DS(h * 128, 128)].partition_broadcast(P)).then_inc(S["gn_landed"], DMA)

            with sp.Fori(0, N_HEADS - 1) as h:
                h8 = sp.snap(h * 8)
                load_B(h, h8)
                sp.wait_ge(S["projA"], h8 + 8)
                load_A(h + 1)
            load_B(N_HEADS - 1, 8 * (N_HEADS - 1))

            def load_C(m, slot):
                sp.dma_start(wC_in[slot][:, 0:8, :], w_in_v[:, :, DS(m * 128 + GATE_A, 128)]).then_inc(S[f"wC_landed{slot}"], DMA)
                sp.dma_start(wC_in[slot][:, 8:16, :], w_in_v[:, :, DS(m * 128 + GATE_B, 128)]).then_inc(S[f"wC_landed{slot}"], DMA)
                sp.dma_start(wC_in[slot][:, 16:20, :], wa_v[:, :, DS(m * 128, 128)]).then_inc(S[f"wC_landed{slot}"], DMA)
                sp.dma_start(wC_in[slot][:, 20:24, :], wb_v[:, :, DS(m * 128, 128)]).then_inc(S[f"wC_landed{slot}"], DMA)

            sp.wait_ge(S["projA"], 8 * N_HEADS)
            load_C(0, 0)
            sp.wait_ge(S["projB"], 8 * N_HEADS + FREE)
            load_C(1, 1)
            with sp.Fori(1, 4) as j:
                sp.wait_ge(S["ys_done"], j * 4 - 2)
                load_C(j * 2, 0)
                sp.wait_ge(S["ys_done"], j * 4)
                load_C(j * 2 + 1, 1)
            sp.wait_ge(S["ys_done"], 14)
            sp.dma_start(wD_in[0][:], wo_v[:, :, 0:512]).then_inc(S["wD_landed0"], DMA)
            sp.wait_ge(S["gates_done"], 16)
            for j in range(4):
                sp.dma_start(x2[:, 2 * j:2 * j + 2, :], x_v[:, 2 * j:2 * j + 2, :]).then_inc(S[f"x_in{j}"], DMA)
            sp.dma_start(wD_in[1][:], wo_v[:, :, 512:1024]).then_inc(S["wD_landed1"], DMA)

            def load_gu(e, slots):
                for c in slots:
                    v = (wg_v, wu_v)[c % 2]
                    sp.dma_start(w_in6[c][:], v[e][:, (c // 2) * 2048:(c // 2) * 2048 + 2048]).then_inc(S[f"w_land{c}"], DMA)

            def load_d(e, slots):
                for c in slots:
                    sp.dma_start(w_in6[c][:], wd_v[e][:, (c - 4) * 2048:(c - 4) * 2048 + 2048]).then_inc(S[f"w_land{c}"], DMA)

            load_gu(0, (0, 1))
            sp.wait_ge(S["d_done"], 8)
            sp.dma_start(g2_row[:], T["norm2_g"][0].partition_broadcast(P)).then_inc(S["g2_in"], DMA)
            sp.dma_start(wr[:, :, 0:4], T["w_group_router"][0].rearrange("(k p) c -> p k c", p=P)).then_inc(S["router_in"], DMA)
            sp.dma_start(wr[:, :, 4:36], T["w_expert_router"][0].rearrange("(k p) c -> p k c", p=P)).then_inc(S["router_in"], DMA)
            sp.dma_start(br[:, 0:4], T["b_group_router"][0].partition_broadcast(P)).then_inc(S["router_in"], DMA)
            sp.dma_start(br[:, 4:36], T["b_expert_router"][0].partition_broadcast(P)).then_inc(S["router_in"], DMA)
            for i in range(N_TILES):
                sp.wait_ge(S["h2_done"], i + 1)
                sp.dma_start(h2_v[:, i, :], h2[:, i % 2, :]).then_inc(S[f"h2_stored{i % 2}"], DMA)
            sp.wait_ge(S["d_done"], 16)
            load_gu(0, (2, 3))
            load_d(0, (4, 5))
            for c in range(4):
                sp.wait_ge(S["w_free_gu"], c + 1)
                load_gu(1, (c,))
            for c in (4, 5):
                sp.wait_ge(S["w_free_d"], c - 3)
                load_d(1, (c,))
            for c in range(4):
                sp.wait_ge(S["w_free_gu"], c + 5)
                load_gu(2, (c,))
            with sp.Fori(2, N_EXP - 1) as e:
                for c in range(4):
                    sp.wait_ge(S["w_free_gu"], e * 4 + (c + 1))
                    load_gu(e + 1, (c,))
                for c in (4, 5):
                    sp.wait_ge(S["w_free_d"], e * 2 + (c - 5))
                    load_d(e, (c,))
            for c in range(2):
                sp.wait_ge(S["w_free_gu"], 4 * (N_EXP - 1) + c + 1)
                sp.dma_start(w_in6[c][:], wd_v[N_EXP - 1][:, c * 2048:(c + 1) * 2048]).then_inc(S[f"w_land{c}"], DMA)

            sp.wait_ge(S["ids_done"], 1)

            def loads_again(n, e, b):
                sp.wait_ge(S["scattered"], n * DMA + DMA * N_EXP)
                for c in range(4):
                    sp.dma_start(w_in6[c][:], (wg_v, wu_v)[c % 2][e][:, (c // 2) * 2048:(c // 2) * 2048 + 2048]).then_inc(S["v_w"], DMA)
                for c in (4, 5):
                    sp.dma_start(w_in6[c][:], wd_v[e][:, (c - 4) * 2048:(c - 4) * 2048 + 2048]).then_inc(S["v_w"], DMA)

            overflow(sp, loads_again)
            sp.wait_ge(S["rows_stored"], 1)

            for i in range(N_TILES):
                if i >= 4:
                    sp.wait_ge(S["res_done"], i - 3)
                for c in range(2):
                    sp.dma_start(comb[:, i % 4, c, :], y_v[:, c, i, :]).then_inc(S[f"comb_in{i % 4}"], DMA)
            for b in range(4):
                sp.wait_ge(S[f"out_stored{b}"], DMA * N_TILES // 4)


        def turn_rows(pe, src_rows, dst, step, n):
            for k in range(n):
                last = pe.transpose(dst[:, k * 128:(k + 1) * 128], src_rows[:, DS(k, 128, step=step)], ident)
            return last

        def gate_up(pe, c):
            for k in range(4):
                kk = (c // 2) * 4 + k
                last = split3(pe, PROJ[c % 2][:, :], (xeH[:, kk, :], xeL[:, kk, :]),
                              (w_high[c][:, k * 512:(k + 1) * 512], w_low[c][:, k * 512:(k + 1) * 512]),
                              kk == 0, kk == 7)
            return last

        def down(pe, c, slot=None):
            slot = c if slot is None else slot
            for k in range(2):
                kk = (c - 4) * 2 + k
                for half in range(2):
                    lo = k * 1024 + half * 512
                    last = split3(pe, SC[:, 1, half * 512:(half + 1) * 512], (hidH[:, kk, :], hidL[:, kk, :]),
                                  (w_high[slot][:, lo:lo + 512], w_low[slot][:, lo:lo + 512]), kk == 0, kk == 3)
            return last

        T_FILL, T_ROUND = 3, 28 + 16

        @block.tensor
        def _(pe):
            pe.wait_ge(S["consts_in"], DMA)

            def turn_input(half):
                for n in range(8 * half, 8 * half + 8):
                    pe.wait_ge(S["xn_done"], 4 * half + 4)
                    if n >= 4:
                        pe.wait_ge(S["hL_done"], n - 3)
                    for i in range(4):
                        last = pe.transpose(bank(n % 4)[:, i * 128:(i + 1) * 128],
                                            x_all[:, 4 * half + i, (n % 8) * 128:(n % 8 + 1) * 128], ident)
                    last.then_inc(S["xT_done"], 1)

            turn_input(0)
            pe.wait_ge(S["hL_done"], 8)
            first_pieces = [(g, k) for g in range(2) for k in range(8)]

            def first_gates(n):
                for g, k in first_pieces[:n]:
                    if k == 0:
                        pe.wait_ge(S["wC_low"], 2)
                        pe.wait_ge(S["eg_done"], 8 * N_HEADS - 1 + g + FREE)
                    last = split3(pe, bank(4 + g), (wCH[0][:, g * 8 + k, :], wCL[0][:, g * 8 + k, :]),
                                  (hTH[:, k, 0:512], hTL[:, k, 0:512]), k == 0, k == 7)
                    if (g, k) == (1, 7):
                        last.then_inc(S["gates_done"], 1)
                del first_pieces[:n]

            def head_steps(h, steps, more=True):
                h8, h7, hT = times(pe, h, 8), times(pe, h, 7), times(pe, h, T_ROUND)
                t_used = [0 if steps[0] < 3 else T_FILL]

                def turned_free():
                    pe.wait_ge(S["t_free"], hT + t_used[0] + FREE)

                def take_turned():
                    turned_free()
                    t_used[0] += 1

                def project(s, ks):
                    unit, i, n = tiles_of(s, more)[0]
                    if unit is None:
                        first_gates((len(ks) + 1) // 2)
                        return
                    if ks[0] == 0:
                        last_unit, _, last_n = tile_at(s - 2)
                        if last_unit == "A":
                            pe.wait_ge(S["normA_done"], h8 + (last_n + 1))
                        elif last_unit == "B":
                            pe.wait_ge(S["eg_done"], h8 + (last_n + 1) + FREE)
                    wh, wl, cols = (wAH, wAL, 384) if unit == "A" else (wBH, wBL, 512)
                    for k in ks:
                        if i == 0:
                            pe.wait_ge(S[f"w{unit}_low"], h8 + (n + k + 1))
                        last = split3(pe, PROJ[s % 2][:, 0:cols],
                                      (hTH[:, k, i * 128:(i + 1) * 128], hTL[:, k, i * 128:(i + 1) * 128]),
                                      (wh[:, k, :], wl[:, k, :]), k == 0, k == 7)
                    if ks[-1] == 7:
                        last.then_inc(S["proj" + unit], 1)

                if steps[0] == 0:
                    project(0, range(6))
                for s in steps:
                    (u0, _, _), (u1, i1, n1), (u2, i2, n2), (u3, i3, n3) = tiles_of(s, more)
                    if u1 == "A":
                        pe.wait_ge(S["ropedA"], h8 * 2 + (2 * n1 + 2) + FREE)
                        take_turned()
                        pe.transpose(TB[:, 0:128], qkA[:, 0:128], ident)
                        pe.transpose(TB[:, 128:256], qkA[:, 128:256], ident).then_inc(S["qkTA"], 1)
                    if u1 == "B":
                        pe.wait_ge(S["ropedB"], h8 * 2 + (2 * n1 + 2) + FREE)
                        take_turned()
                        pe.transpose(TB[:, 0:128], qkR[:, 0:2, :].rearrange("p a b -> p (a b)"), ident)
                        pe.transpose(TB[:, 128:256], qkR[:, 2:4, :].rearrange("p a b -> p (a b)"), ident).then_inc(S["qkTB"], 1)
                    project(s, [6, 7])
                    if s == 1:
                        pe.wait_ge(S["hL_done"], 16)
                    if u1 == "A":
                        if i1 == 0:
                            pe.wait_ge(S["sT_done"], h8 + n1 + FREE)
                            pe.wait_ge(S["U_done"], h7 + 7 * (n1 // 8) + FREE)
                        pe.wait_ge(S["exped"], h8 * 2 + 2 * n1 + FREE)
                        turned_free()
                        for c in range(2):
                            r = slice(c * 64, c * 64 + 64)
                            for t0 in range(0, i1 + 1, 4):
                                t1 = min(t0 + 4, i1 + 1)
                                keys = [part[r, 1 + t0:1 + t1, :].rearrange("p a b -> p (a b)") for part in (qkTH, qkTL)]
                                last = split3(pe, SC[:, c, t0 * 128:t1 * 128], (qkTH[r, 0, :], qkTL[r, 0, :]), keys,
                                              True, True)
                        last.then_inc(S["scored"], 1)
                    if u1 == "B":
                        if i1 == 0:
                            pe.wait_ge(S["exped"], h8 * 2 + 16 + FREE)
                        pe.wait_ge(S["sT_done"], h8 + n1 + FREE)
                        turned_free()
                        pe.matmul(bank(0)[:, 0:128], qkT[:, i1 % 2, 128:256], qkT[:, i1 % 2, 0:128],
                                  start=True, stop=True).then_inc(S["st_done"], 1)
                    if u3 == "A":
                        pe.wait_ge(S["oN_done"], h8 + (n3 + 1))
                        take_turned()
                        pe.transpose(TB[:, 0:128], oN[:, :], ident).then_inc(S["oTA"], 1)
                    if u3 == "B":
                        pe.wait_ge(S["gated"], h8 + (n3 + 1) + FREE)
                        take_turned()
                        pe.transpose(TB[:, 0:128], gatedR[:, :], ident).then_inc(S["gTB"], 1)
                    if u2 == "B":
                        pe.wait_ge(S["sT_done"], h8 + (n2 + 1) + FREE)
                        if i2 == 0:
                            pe.wait_ge(S["oN_done"], h8 + 8)
                        else:
                            pe.wait_ge(S["onR_done"], h8 + n2 + FREE)
                            pe.wait_ge(S["U_done"], h7 + n2 + FREE)
                        last = pe.matmul(OB[:, 0:128], sT[:, i2 % 2, :], vg[:, i2 % 2, 0:128], start=True, stop=(i2 == 0))
                        if i2 > 0:
                            last = pe.matmul(OB[:, 0:128], qkT[:, i2 % 2, 0:128], U[:, i2 % 2, :], start=False, stop=True)
                        last.then_inc(S["oB"], 1)
                    if u1 == "B" and i1 < N_TILES - 1:
                        pe.wait_ge(S["U_done"], h7 + n1 + FREE)
                        pe.wait_ge(S["vg_done"], h8 + (n1 + 1))
                        pe.matmul(bank(2)[:, 0:128], qkR[:, 2:4, :].rearrange("p a b -> p (a b)"), vg[:, i1 % 2, 0:128],
                                  start=True, stop=True).then_inc(S["kv_done"], 1)
                    project(s + 1, [0, 1])
                    if u2 == "A":
                        pe.wait_ge(S["probs_done"], h8 + (n2 + 1))
                        take_turned()
                        for j in range(min(4, i2 + 1)):
                            last = pe.transpose(TB[:, j * 128:(j + 1) * 128], probs[:, 0, j * 128:(j + 1) * 128], ident)
                        last.then_inc(S["aT1"], 1)
                    project(s + 1, [2])
                    if u2 == "A" and i2 >= 4:
                        take_turned()
                        for j in range(4, i2 + 1):
                            last = pe.transpose(TB[:, (j - 4) * 128:(j - 3) * 128], probs[:, 0, j * 128:(j + 1) * 128], ident)
                        last.then_inc(S["aT2"], 1)
                    project(s + 1, [3, 4])
                    if u2 == "A":
                        if i2 == 0:
                            pe.wait_ge(S["onR_done"], h8 + n2 + FREE)
                        else:
                            pe.wait_ge(S["oN_done"], h8 + n2)
                        turned_free()
                        for j in range(i2 + 1):
                            last = pe.matmul(OB[:, 0:128], aT[:, j, :], V[:, j, :], start=(j == 0), stop=(j == i2))
                        last.then_inc(S["pv_done"], 1)
                    project(s + 1, [5])
                assert steps[0] == 0 or t_used[0] == (T_FILL if more else 0) + (0 if steps[0] < 3 else T_ROUND), t_used

            head_steps(0, FILL[:1])
            turn_input(1)
            head_steps(0, FILL[1:])
            with pe.Fori(0, N_HEADS - 1) as h:
                head_steps(h, ROUND)
            head_steps(N_HEADS - 1, ROUND, more=False)
            assert not first_pieces

            pe.wait_ge(S["t_free"], N_HEADS * T_ROUND + FREE)
            pe.wait_ge(S["onR_done"], 8 * N_HEADS + FREE)
            pe.wait_ge(S["sT_done"], 8 * N_HEADS + FREE)
            pe.wait_ge(S["U_done"], 7 * N_HEADS + FREE)

            def merge_pair(j, first_pair, last_pair):
                j4, j8 = times(pe, j, 4), times(pe, j, 8)
                for sub in range(2):
                    pe.wait_ge(S["wC_low"], j4 + (2 * sub + 2))
                    for th in range(2):
                        n = 2 * sub + th
                        b0 = 4 if th == 0 else 0
                        pe.wait_ge(S["sig_mul"], j8 + (2 * n - 2) + SIG_FREE)
                        tok = slice(th * 512, th * 512 + 512)

                        def gates():
                            for g in range(2):
                                for k in range(8):
                                    last = split3(pe, bank(b0 + g), (wCH[sub][:, g * 8 + k, :], wCL[sub][:, g * 8 + k, :]),
                                                  (hTH[:, k, tok], hTL[:, k, tok]), k == 0, k == 7)
                            last.then_inc(S["gates_done"], 1)

                        def branches():
                            for g in range(2):
                                for k in range(4):
                                    last = pe.matmul(bank(b0 + 2 + g), wC_in[sub][:, 16 + 4 * g + k, :], oT[:, 4 * g + k, tok],
                                                     start=(k == 0), stop=(k == 3))
                            last.then_inc(S["ys_done"], 1)

                        if last_pair and n == 3:
                            branches()
                            gates()
                        else:
                            if not (first_pair and n == 0):
                                gates()
                            branches()

            merge_pair(0, True, False)
            with pe.Fori(1, 3) as j:
                merge_pair(j, False, False)
            merge_pair(3, False, True)

            pe.wait_ge(S["sig_mul"], 30 + SIG_FREE)

            def out_proj(n, i):
                pe.wait_ge(S["wD_low"], 2 * n + 2)
                pe.wait_ge(S["mL"], i + 1)
                cnt = 8 * n + i
                if cnt >= 3:
                    pe.wait_ge(S["x2_done"], cnt - 2)
                tok = slice(i * 128, i * 128 + 128)
                for k in range(8):
                    last = split3(pe, bank(4 + cnt % 3), (mergedH[:, k, tok], mergedL[:, k, tok]),
                                  (wDH[n][k // 4][:, k % 4, :], wDL[n][:, k, :]), k == 0, k == 7)
                last.then_inc(S["d_done"], 1)

            for i in range(N_TILES):
                out_proj(0, i)
            for i in range(N_TILES + 2):
                if i < N_TILES:
                    out_proj(1, i)
                if i >= 2:
                    t = i - 2
                    pe.wait_ge(S["h2T_out"], t + 1)
                    pe.wait_ge(S["router_in"], 4 * DMA)
                    if t >= 1:
                        pe.wait_ge(S["logit_done"], t)
                    for k in range(8):
                        last = pe.matmul(OB[:, 0:36], h2T[:, t % 2, k, :], wr[:, k, :], start=(k == 0), stop=(k == 7))
                    last.then_inc(S["lg_done"], 1)
                if 1 <= i <= N_TILES:
                    t = i - 1
                    pe.wait_ge(S["h2_done"], t + 1)
                    if t >= 2:
                        pe.wait_ge(S["h2T_out"], t - 1)
                    for k in range(8):
                        last = pe.transpose(SC[:, t % 2, k * 128:(k + 1) * 128], h2[:, t % 2, k * 128:(k + 1) * 128], ident)
                    last.then_inc(S["h2T_done"], 1)

            pe.wait_ge(S["ract"], 1)
            pe.wait_ge(S["rstep"], R_BEFORE)
            pe.matmul(bank(0)[:, 0:256], count_masks[:, 0:128], mask[:].rearrange("p a b -> p (a b)"), start=True, stop=False)
            pe.matmul(bank(0)[:, 0:256], count_masks[:, 128:256], before[:, 0:8, :].rearrange("p a b -> p (a b)"),
                      start=False, stop=True).then_inc(S["pmm"], 1)
            pe.matmul(bank(1)[:, 0:32], count_masks[:, 128:256], before[:, 8, :], start=True, stop=True).then_inc(S["pmm"], 1)
            for q in range(16):
                if q % 8 == 0:
                    pe.wait_ge(S["pick_done"], q // 8 + 1)
                last = pe.matmul(bank(2)[:, 0:32], pick[:, q, :], keyid1[:, q, :], start=(q == 0), stop=(q == 15))
            last.then_inc(S["pmm"], 1)

            def all_tables():
                for q in range(16):
                    pe.wait_ge(S["pick_done"], q + 3)
                    pe.matmul(bank(2)[:, 0:256], pick[:, q, :], keyid[q % 2][:, :], start=(q == 0), stop=(q == 15)
                              ).then_inc(S["pick_used"], 1)

            def turn_x():
                turn_rows(pe, xe, SC[:, 0, :], 8, 8).then_inc(S["xeT_done"], 1)

            def run_gate_up(e4):
                for c in range(4):
                    pe.wait_ge(S["gu_low"], e4 + (c + 1))
                    last = gate_up(pe, c)
                    last.then_inc(S["w_free_gu"], 1)

            def run_down(e2):
                for c in (4, 5):
                    pe.wait_ge(S["d_low"], e2 + (c - 3))
                    down(pe, c).then_inc(S["w_free_d"], 1)

            pe.wait_ge(S["xe_landed"], DMA)
            turn_x()
            pe.wait_ge(S["xeL_done"], 1)
            run_gate_up(0)
            pe.wait_ge(S["xe_landed"], 2 * DMA)
            turn_x()
            pe.wait_ge(S["hid_done"], 1)
            turn_rows(pe, hid, TB, 4, 4).then_inc(S["hidT_done"], 1)
            pe.wait_ge(S["hidL_done"], 1)
            run_down(0)

            def expert_step(e, more):
                e2, e4, e16 = (e * 2, e * 4, e * 16) if isinstance(e, int) else (pe.snap(e * 2), pe.snap(e * 4), pe.snap(e * 16))
                pe.wait_ge(S["xeL_done"], e + 1)
                pe.wait_ge(S["hid_done"], e)
                run_gate_up(e4)
                if more:
                    pe.wait_ge(S["xe_landed"], e16 + 2 * DMA)
                    turn_x()
                if not isinstance(e, int) or e > 1:
                    pe.wait_ge(S["hidL_done"], e)
                    pe.wait_ge(S["y_out"], e - 1 + FREE)
                    run_down(e2 - 2)
                pe.wait_ge(S["hid_done"], e + 1)
                turn_rows(pe, hid, TB, 4, 4).then_inc(S["hidT_done"], 1)

            expert_step(1, True)
            with pe.Fori(2, N_EXP - 1) as e:
                expert_step(e, True)
            expert_step(N_EXP - 1, False)
            pe.wait_ge(S["hidL_done"], N_EXP)
            pe.wait_ge(S["y_out"], N_EXP - 1 + FREE)
            for c in range(2):
                pe.wait_ge(S["gu_low"], 4 * N_EXP + c + 1)
                down(pe, 4 + c, slot=c).then_inc(S["w_free_d"], 1)
            pe.wait_ge(S["y_out"], N_EXP + FREE)

            def block_products(n, e, b):
                pe.wait_ge(S["xe_landed"], n * DMA + DMA * (N_EXP + 1))
                turn_x()
                pe.wait_ge(S["xeL_done"], n + (N_EXP + 1))
                pe.wait_ge(S["v_lo"], n * 6 + 6)
                for c in range(4):
                    gate_up(pe, c).then_inc(S["w_free_gu"], 1)
                pe.wait_ge(S["hid_done"], n + (N_EXP + 1))
                turn_rows(pe, hid, TB, 4, 4).then_inc(S["hidT_done"], 1)
                pe.wait_ge(S["hidL_done"], n + (N_EXP + 1))
                for c in (4, 5):
                    down(pe, c).then_inc(S["w_free_d"], 1)
                pe.wait_ge(S["y_out"], n + (N_EXP + 1) + FREE)

            overflow(pe, block_products, all_tables)

        @block.scalar
        def _(act):
            def high(dst, src_, landed, value, done, n=1):
                act.wait_ge(landed, value)
                act.activation(dst, src_, ACT.Copy).then_inc(done, n)

            def high_C(m_value, sub, piece):
                act.wait_ge(S[f"wC_landed{sub}"], m_value)
                act.activation(wCH[sub][:, piece * 8:piece * 8 + 8, :], wC_in[sub][:, piece * 8:piece * 8 + 8, :],
                               ACT.Copy).then_inc(S["wC_high"], 1)

            def head_steps(h, steps, more=True):
                h8, h48, h64 = times(act, h, 8), times(act, h, 48), times(act, h, 64)
                for s in steps:
                    (u0, i0, n0), (u1, i1, n1), (u2, i2, n2), (u3, i3, n3) = tiles_of(s, more)
                    src_bank = PROJ[s % 2]
                    if u1 == "A":
                        act.wait_ge(S["qkTA"], h8 + (n1 + 1) + FREE)
                        act.activation(qkTH[:, 0:i1 + 2:i1 + 1, :], TB[:, 0:256].rearrange("p (a b) -> p a b", a=2), ACT.Copy
                                       ).then_inc(S["qkHA"], 1)
                    if u1 == "B":
                        act.wait_ge(S["qkTB"], h8 + (n1 + 1))
                        act.activation(qkT[:, i1 % 2, :], TB[:, 0:256], ACT.Copy).then_inc(S["t_free"], 1)
                    if u3 == "A":
                        act.wait_ge(S["pv_done"], h8 + (n3 + 1) + FREE)
                        act.activation(oN[:], OB[:, 0:128], ACT.Square, accum_out=ss_o).then_inc(S["o_sq"], 1)
                    if u0 == "A":
                        act.wait_ge(S["projA"], h8 + (n0 + 1))
                        act.wait_ge(S["ssA_done"], h8 + n0 + FREE)
                        act.activation(sqA[:], src_bank[:, 0:256], ACT.Square).then_inc(S["sqA_done"], 1)
                        act.activation(V[:, i0, :], src_bank[:, 256:384], ACT.Copy).then_inc(S["vA_done"], 1)
                    if u0 == "B":
                        par = i0 % 2
                        act.wait_ge(S["projB"], h8 + (n0 + 1) + FREE)
                        if i0 == 0:
                            act.wait_ge(S["head_consts"], h + 1)
                        act.wait_ge(S["ropedB"], h8 * 2 + 2 * n0 + FREE)
                        if i0 >= 2:
                            act.wait_ge(S["oB"], h8 + (n0 - 1))
                            act.wait_ge(S["sg_done"], h8 + (n0 - 1) + FREE)
                        act.activation(qkS[:, 0:2, :], src_bank[:, 0:128].rearrange("p (a b) -> p a b", a=2), ACT.Copy,
                                       scale=head_c[:, 0:1]).then_inc(S["qkS_done"], 1)
                        act.activation(qkS[:, 2:4, :], src_bank[:, 128:256].rearrange("p (a b) -> p a b", a=2), ACT.Copy,
                                       scale=head_c[:, 1:2]).then_inc(S["qkS_done"], 1)
                        act.activation(vg[:, par, :], src_bank[:, 256:512], ACT.Copy).then_inc(S["vg_done"], 1)
                        act.wait_ge(S["sg_done"], h8 + n0 + FREE)
                        act.activation(eg[:], src_bank[:, 384:512], ACT.Exp, scale=-1.0).then_inc(S["eg_done"], 1)
                    if u0 == "B" and not more:
                        if s % 8 in PREP_C:
                            high_C(4 * DMA, 0, PREP_C[s % 8])
                    elif s % 8 in PREP:
                        ks = PREP[s % 8]
                        if u0 == "A":
                            high(wBH[:, ks[0]:ks[-1] + 1, :], wB_in[:, ks[0]:ks[-1] + 1, :],
                                 S["wB_landed"], h64 + 4 * DMA, S["wB_high"], len(ks))
                        else:
                            high(wAH[:, ks[0]:ks[-1] + 1, :], wA_in[:, ks[0]:ks[-1] + 1, :],
                                 S["wA_landed"], h48 + 6 * DMA, S["wA_high"], len(ks))
                    if u3 == "A":
                        act.wait_ge(S["oTA"], h8 + (n3 + 1))
                        act.activation(oT[:, DS(h, 1), i3 * 128:(i3 + 1) * 128].rearrange("p a b -> p (a b)"), TB[:, 0:128],
                                       ACT.Copy, scale=subln_scaled).then_inc(S["t_free"], 1)
                    if u3 == "B":
                        act.wait_ge(S["gTB"], h8 + (n3 + 1) + FREE)
                        act.activation(oT[:, DS(h + 4, 1), i3 * 128:(i3 + 1) * 128].rearrange("p a b -> p (a b)"), TB[:, 0:128],
                                       ACT.Copy).then_inc(S["t_free"], 1)
                    L = (i1 + 1) * 128
                    def exponentials(c):
                        act.activation(probs[:, c, 0:L], SC[:, c, 0:L], ACT.Exp, bias=negmax[:, c:c + 1], scale=0.125,
                                       accum_out=rowsum[:, c:c + 1]).then_inc(S["exped"], 1)
                    if u2 == "A":
                        nb = min(4, i2 + 1)
                        act.wait_ge(S["aT1"], h8 + (n2 + 1))
                        act.activation(aT[:, 0:nb, :].rearrange("p a b -> p (a b)"), TB[:, 0:nb * 128], ACT.Copy
                                       ).then_inc(S["t_free"], 1)
                    if u1 == "A":
                        act.wait_ge(S["negged"], h8 + (n1 + 1))
                        exponentials(1)
                        if u2 == "A" and i2 >= 4:
                            act.wait_ge(S["aT2"], h * 4 + (i2 - 3))
                        exponentials(0)

            for half in range(2):
                for i in range(4 * half, 4 * half + 4):
                    act.wait_ge(S[f"x_in{i // 2}"], DMA)
                    if i:
                        act.wait_ge(S["x_sq_done"], i)
                    act.activation(x_sq[:], x_all[:, i, :], ACT.Square, accum_out=x_ss[:, i:i + 1]).then_inc(S["x_sq_done"], 1)
                if half == 1:
                    act.wait_ge(S["angle_done"], 1)
                    act.activation(sin_t[:], ang[:], ACT.Sin).then_inc(S["trig_done"], 1)
                    act.activation(cos_t[:], turns[:], ACT.Sin, scale=-1.0, bias=const("half_pi")).then_inc(S["trig_done"], 1)
                    head_steps(0, FILL[:1])
                act.wait_ge(S["g1_in"], DMA)
                for n in range(8 * half, 8 * half + 8):
                    act.wait_ge(S["xT_done"], n + 1)
                    act.activation(hTH[:, n % 8, half * 512:(half + 1) * 512], bank(n % 4), ACT.Copy,
                                   scale=g1_cols[:, n % 8:n % 8 + 1]).then_inc(S["hH_done"], 1)
                if half == 0:
                    for k in range(8):
                        high(wAH[:, k, :], wA_in[:, k, :], S["wA_landed"], 3 * DMA, S["wA_high"])
            act.wait_ge(S["lam_step"], 2)
            act.activation(lam_e, lam_s, ACT.Exp).then_inc(S["lam_expd"], 1)

            head_steps(0, FILL[1:])
            with act.Fori(0, N_HEADS - 1) as h:
                head_steps(h, ROUND)
            head_steps(N_HEADS - 1, ROUND, more=False)

            act.wait_ge(S["gated"], 8 * N_HEADS + FREE)

            def merge_pair(j, last):
                j4, j8 = (j * 4, j * 8) if isinstance(j, int) else (act.snap(j * 4), act.snap(j * 8))
                j64 = j * 64 if isinstance(j, int) else act.snap(j * 64)
                for sub in range(2):
                    for th in range(2):
                        n = 2 * sub + th
                        if last and n == 3:
                            high_merged(0)
                        act.wait_ge(S["gates_done"], j4 + (n + 1))
                        act.wait_ge(S["sig_mul"], j8 + 2 * n + SIG_FREE)
                        for g in range(2):
                            act.activation(sig[:, g, :], bank((4 if th == 0 else 0) + g), ACT.Exp, scale=-1.0
                                           ).then_inc(S["sig_exp"], 1)
                        for piece in range(2):
                            if n == 0:
                                high_C(j64 + 4 * DMA, 1, piece)
                            if n == 2 and not last:
                                high_C(j64 + 8 * DMA, 0, piece)
                            if n == 2 and last:
                                high(wDH[0][piece][:], wD_in[0][:, piece * 4:piece * 4 + 4, :],
                                     S["wD_landed0"], DMA, S["wD_high"])

            def high_merged(th):
                if th == 0:
                    act.wait_ge(S["ys_done"], 16)
                act.wait_ge(S["sig_mul"], 30 + 2 * th + SIG_FREE)
                for i in range(4 * th, 4 * th + 4):
                    act.activation(mergedH[:, :, i * 128:(i + 1) * 128], merged[:, :, i * 128:(i + 1) * 128], ACT.Copy
                                   ).then_inc(S["mH"], 1)

            with act.Fori(0, 3) as j:
                merge_pair(j, False)
            merge_pair(3, True)
            high_merged(1)
            for piece in range(2):
                high(wDH[1][piece][:], wD_in[1][:, piece * 4:piece * 4 + 4, :], S["wD_landed1"], DMA, S["wD_high"])
            for i in range(N_TILES + 1):
                if i < N_TILES:
                    act.wait_ge(S["x2_done"], 9 + i)
                    if i >= 2:
                        act.wait_ge(S[f"h2_stored{i % 2}"], DMA * (i // 2))
                        act.wait_ge(S["h2T_done"], i - 1)
                    act.activation(h2[:, i % 2, :], x2[:, i, :], ACT.Square, accum_out=stats2[:, 0, i:i + 1]).then_inc(S["n2_sq"], 1)
                if i >= 1:
                    t = i - 1
                    act.wait_ge(S["h2T_done"], t + 1)
                    if t >= 2:
                        act.wait_ge(S["lg_done"], t - 1)
                    act.activation(h2T[:, t % 2, :, :].rearrange("p a b -> p (a b)"), SC[:, t % 2, :], ACT.Copy).then_inc(S["h2T_out"], 1)
            lo = CONST_AT["strict"][0]
            act.activation(count_masks[:], consts[:, lo:lo + 256], ACT.Copy).then_inc(S["ract"], 1)
            act.wait_ge(S["rstep"], R_GDIFF)
            act.activation(gexp[:], gdiff[:], ACT.Exp).then_inc(S["ract"], 1)
            act.wait_ge(S["rstep"], R_VDIFF)
            act.activation(vexp[:], vdiff[:], ACT.Exp).then_inc(S["ract"], 1)

            def high_slot(c, value):
                act.wait_ge(S[f"w_land{c}"], value)
                act.activation(w_high[c][:], w_in6[c][:], ACT.Copy).then_inc(S["gu_high" if c < 4 else "d_high"], 1)

            def x_high(value):
                act.wait_ge(S["xeT_done"], value)
                act.activation(xeH[:].rearrange("p a b -> p (a b)"), SC[:, 0, :], ACT.Copy).then_inc(S["xeH_done"], 1)

            def hid_high(value):
                act.wait_ge(S["hidT_done"], value)
                act.activation(hidH[:].rearrange("p a b -> p (a b)"), TB[:, :], ACT.Copy).then_inc(S["hidH_done"], 1)

            def gate_silu(e):
                act.wait_ge(S["w_free_gu"], e * 4 + 4)
                act.wait_ge(S["hid_done"], e)
                act.activation(silu[:], PROJ[0][:, :], ACT.Silu).then_inc(S["silu_done"], 1)

            for c in range(6):
                high_slot(c, DMA)
            x_high(1)
            high_slot(0, 2 * DMA)
            gate_silu(0)
            x_high(2)
            hid_high(1)
            for c in range(1, 4):
                high_slot(c, 2 * DMA)
            act.wait_ge(S["w_free_d"], 2)
            act.activation(y[:], SC[:, 1, :], ACT.Copy).then_inc(S["y_out"], 1)

            def expert_step(e, more):
                e16 = times(act, e, 16)
                if not isinstance(e, int) or e > 1:
                    high_slot(4, e16)
                    high_slot(5, e16)
                if more:
                    high_slot(0, e16 + 2 * DMA)
                gate_silu(e)
                if more:
                    x_high(e + 2)
                    for c in (1, 2, 3):
                        high_slot(c, e16 + 2 * DMA)
                else:
                    for c in (0, 1):
                        high_slot(c, e16 + 2 * DMA)
                if not isinstance(e, int) or e > 1:
                    act.wait_ge(S["w_free_d"], e * 2)
                    act.wait_ge(S["scattered"], e16 - DMA)
                    act.activation(y[:], SC[:, 1, :], ACT.Copy).then_inc(S["y_out"], 1)
                hid_high(e + 1)

            expert_step(1, True)
            with act.Fori(2, N_EXP - 1) as e:
                expert_step(e, True)
            expert_step(N_EXP - 1, False)
            act.wait_ge(S["w_free_d"], 2 * N_EXP)
            act.wait_ge(S["scattered"], DMA * (N_EXP - 1))
            act.activation(y[:], SC[:, 1, :], ACT.Copy).then_inc(S["y_out"], 1)

            def block_steps(n, e, b):
                act.wait_ge(S["v_w"], n * (6 * DMA) + 6 * DMA)
                for c in range(6):
                    act.activation(w_high[c][:], w_in6[c][:], ACT.Copy).then_inc(S["v_hi"], 1)
                x_high(n + (N_EXP + 1))
                act.wait_ge(S["w_free_gu"], n * 4 + 4 * (N_EXP + 1))
                act.activation(silu[:], PROJ[0][:, :], ACT.Silu).then_inc(S["silu_done"], 1)
                hid_high(n + (N_EXP + 1))
                act.wait_ge(S["w_free_d"], n * 2 + 2 * (N_EXP + 1))
                act.activation(y[:], SC[:, 1, :], ACT.Copy).then_inc(S["y_out"], 1)

            act.wait_ge(S["scattered"], DMA * N_EXP)
            overflow(act, block_steps)
            for i in range(N_TILES):
                act.wait_ge(S["res_done"], i + 1)
                act.dma_start(out_v[:, i, :], res[:, i % 4, :]).then_inc(S[f"out_stored{i % 4}"], DMA)

        @block.gpsimd
        def _(pool):
            mhalf = const("minus_half")
            pool.wait_ge(S["consts_in"], DMA)
            def x_powers(tiles):
                for i in tiles:
                    pool.wait_ge(S["x_ms_done"], i + 1)
                    pool.tensor_tensor(x_rstd[:, i:i + 1], x_ms[:, i:i + 1], mhalf[:, 0:1], ALU.pow).then_inc(S["x_rstd_done"], 1)

            x_powers(range(4))
            steps = [0]

            def step(ins):
                steps[0] += 1
                ins.then_inc(S["ang_step"], 1)
                pool.wait_ge(S["ang_step"], steps[0])

            pool.wait_ge(S["pos_in"], DMA)
            step(pool.tensor_copy(posf, posi[:]))
            step(pool.tensor_tensor(ang[:], posf.unsqueeze(2).to_broadcast([P, 8, 72]),
                                    const("freq").unsqueeze(1).to_broadcast([P, 8, 72]), ALU.mult))
            step(pool.tensor_scalar(turns[:], ang[:], 1.0 / (2 * math.pi), MAGIC, ALU.mult, ALU.add))
            step(pool.tensor_scalar(turns[:], turns[:], -MAGIC, None, ALU.add))
            for part in TWO_PI:
                step(pool.tensor_scalar(turn_part[:], turns[:], -part, None, ALU.mult))
                step(pool.tensor_tensor(ang[:], ang[:], turn_part[:], ALU.add))
            x_powers(range(4, 8))
            pool.wait_ge(S["trig_done"], 2)
            def head_steps(h, steps, more=True):
                h8 = times(pool, h, 8)
                for s in steps:
                    (u0, i0, n0), (u1, i1, n1), (u2, i2, n2), (u3, i3, n3) = tiles_of(s, more)
                    if s == 3:
                        pool.wait_ge(S["qkS_done"], h8 * 2 + FREE)
                        pool.wait_ge(S["sT_done"], h8 + FREE)
                        lo = CONST_AT["ret_q"][0]
                        pool.tensor_copy(head_c[:], consts[:, lo:lo + 16].rearrange("p (a b) -> p b a", b=4)[:, DS(h, 1), :]
                                         .rearrange("p a b -> p (a b)")).then_inc(S["head_consts"], 1)
                    if u3 == "A":
                        pool.wait_ge(S["o_ms"], h8 + (n3 + 1))
                        pool.tensor_tensor(rstd_o, ms_o, mhalf[:, 0:1], ALU.pow).then_inc(S["o_rstd"], 1)
                    if u3 == "B":
                        if i3 == 0:
                            pool.wait_ge(S["gn_landed"], h * 32 + 32)
                        pool.wait_ge(S["onR_done"], h8 + (n3 + 1) + FREE)
                        pool.tensor_tensor(onR[:], onR[:], gn_rows[:, 0, :], ALU.mult).then_inc(S["gate_step"], 1)
                        pool.wait_ge(S["gate_step"], h8 * 2 + (2 * n3 + 1))
                        pool.tensor_tensor(onR[:], onR[:], gn_rows[:, 1, :], ALU.add).then_inc(S["gate_step"], 1)
                        pool.wait_ge(S["gate_step"], h8 * 2 + (2 * n3 + 2))
                        pool.wait_ge(S["gTB"], h8 + n3 + FREE)
                        pool.tensor_tensor(gatedR[:], onR[:], sg[:, i3 % 2, :], ALU.mult).then_inc(S["gated"], 1)
                    if u1 == "B":
                        pool.wait_ge(S["egr"], h8 + (n1 + 1))
                        pool.wait_ge(S["gated"], h8 + max(n1 - 1, 0) + FREE)
                        pool.tensor_tensor(sg[:, i1 % 2, :], vg[:, i1 % 2, 128:256], eg[:], ALU.mult).then_inc(S["sg_done"], 1)
                    if u0 == "A":
                        pool.wait_ge(S["msA_done"], h8 + (n0 + 1))
                        pool.tensor_tensor(rstd_qk, ms_qk, mhalf[:, 0:4], ALU.pow).then_inc(S["rstdA_done"], 1)
                    if u0 == "B":
                        sin = sin_t[:, i0, 8:72].unsqueeze(1).to_broadcast([P, 2, 64])
                        pool.wait_ge(S["qkS_done"], h8 * 2 + (2 * n0 + 2) + FREE)
                        pool.wait_ge(S["ropedB"], h8 * 2 + 2 * n0 + FREE)
                        pool.tensor_tensor(qkSin[:, 0:4:2, :], qkS[:, 1:4:2, :], sin, ALU.mult).then_inc(S["sinB"], 1)
                        pool.tensor_tensor(qkSin[:, 1:4:2, :], qkS[:, 0:4:2, :], sin, ALU.mult).then_inc(S["sinB"], 1)
                    if u2 == "B":
                        pool.wait_ge(S["bn_v"], h8 + (n2 + 1))
                        pool.tensor_tensor(bstat[:, 9:10], bstat[:, 8:9], mhalf[:, 0:1], ALU.pow).then_inc(S["bn_r"], 1)

            head_steps(0, FILL)
            with pool.Fori(0, N_HEADS - 1) as h:
                head_steps(h, ROUND)
            head_steps(N_HEADS - 1, ROUND, more=False)
            for i in range(N_TILES):
                pool.wait_ge(S["n2_ms"], i + 1)
                pool.tensor_tensor(stats2[:, 2, i:i + 1], stats2[:, 1, i:i + 1], mhalf[:, 0:1], ALU.pow).then_inc(S["n2_rstd"], 1)

            def gather(col, chain, done):
                pool.tensor_copy(cur_gather[:], ids_gather[:, col]).then_inc(S["idx_copied"], 1)
                pool.wait_ge(S["idx_copied"], chain)
                pool.indirect_dma_start(out=xe[:], out_offset=None, in_=h2_dram,
                                        in_offset=bass.IndirectOffsetOnAxis(ap=cur_gather[:, 0:1], axis=0),
                                        bounds_check=1023, oob_is_err=False).then_inc(S[done], DMA)

            def scatter(col, chain, done):
                pool.tensor_copy(cur_scatter[:], ids_scatter[:, col]).then_inc(S["idx_copied"], 1)
                pool.wait_ge(S["idx_copied"], chain)
                pool.indirect_dma_start(out=y_dram, out_offset=bass.IndirectOffsetOnAxis(ap=cur_scatter[:, 0:1], axis=0),
                                        in_=y[:], in_offset=None,
                                        bounds_check=2047, oob_is_err=False).then_inc(S[done], DMA)

            for i in range(2):
                pool.wait_ge(S[f"h2_stored{i}"], 4 * DMA)
            pool.wait_ge(S["h2T_out"], 8)
            pool.memset(xe[:], 0.0).then_inc(S["xe_zero"], 1)
            pool.wait_ge(S["xe_zero"], 1)
            pool.wait_ge(S["ids_done"], 1)
            gather(slice(0, 1), 1, "xe_landed")
            pool.wait_ge(S["xeT_done"], 1)
            gather(slice(1, 2), 2, "xe_landed")
            pool.wait_ge(S["xeT_done"], 2)
            gather(slice(2, 3), 3, "xe_landed")

            def expert_step(e, more):
                pool.sem_clear(S["idx_copied"])
                n = 0
                if more:
                    pool.wait_ge(S["xeT_done"], e + 2)
                    gather(DS(e + 2, 1), 1, "xe_landed")
                    n = 1
                pool.wait_ge(S["y_out"], e + FREE)
                scatter(DS(e - 1, 1), n + 1, "scattered")

            with pool.Fori(1, N_EXP - 2) as e:
                expert_step(e, True)
            expert_step(N_EXP - 2, False)
            expert_step(N_EXP - 1, False)
            pool.wait_ge(S["y_out"], N_EXP + FREE)
            pool.wait_ge(S["scattered"], DMA * (N_EXP - 1))
            scatter(slice(N_EXP - 1, N_EXP), 2, "scattered")
            pool.wait_ge(S["scattered"], DMA * N_EXP)

            def block_moves(n, e, b):
                pool.sem_clear(S["idx_copied"])
                col = pool.snap(b * N_EXP + e)
                gather(DS(col, 1), 1, "xe_landed")
                pool.wait_ge(S["y_out"], n + (N_EXP + 1) + FREE)
                scatter(DS(col, 1), 2, "scattered")
                pool.wait_ge(S["scattered"], n * DMA + DMA * (N_EXP + 1))

            def tables_ready():
                pool.wait_ge(S["ids_done"], 2)

            overflow(pool, block_moves, tables_ready)
            pool.memset(cur_gather[:], 0).then_inc(S["rows_stored"], 1)

        @block.vector
        def _(dve):
            def low(dst, src_, high_, ready, value, done, n=1):
                dve.wait_ge(ready, value)
                dve.tensor_tensor(dst, src_, high_.bitcast(F32), ALU.subtract).then_inc(done, n)

            def low_C(value, sub, piece):
                dve.wait_ge(S["wC_high"], value)
                r = slice(piece * 8, piece * 8 + 8)
                dve.tensor_tensor(wCL[sub][:, r, :], wC_in[sub][:, r, :], wCH[sub][:, r, :].bitcast(F32), ALU.subtract
                                  ).then_inc(S["wC_low"], 1)

            def head_steps(h, steps, more=True):
                h8, h7, h24 = times(dve, h, 8), times(dve, h, 7), times(dve, h, 24)

                def split_weights(s):
                    ks = PREP[s % 8]
                    kk = slice(ks[0], ks[-1] + 1)
                    if tile_at(s)[0] == "A":
                        low(wBL[:, kk, :], wB_in[:, kk, :], wBH[:, kk, :], S["wB_high"], h8 + kk.stop, S["wB_low"], len(ks))
                    else:
                        low(wAL[:, kk, :], wA_in[:, kk, :], wAH[:, kk, :], S["wA_high"], h8 + (8 + kk.stop), S["wA_low"], len(ks))

                for s in steps:
                    (u0, i0, n0), (u1, i1, n1), (u2, i2, n2), (u3, i3, n3) = tiles_of(s, more)
                    src_bank = PROJ[s % 2]
                    if u1 == "A":
                        dve.wait_ge(S["qkHA"], h8 + (n1 + 1))
                        dve.tensor_tensor(qkTL[:, 0:i1 + 2:i1 + 1, :], TB[:, 0:256].rearrange("p (a b) -> p a b", a=2),
                                          qkTH[:, 0:i1 + 2:i1 + 1, :].bitcast(F32), ALU.subtract
                                          ).then_inc(S["t_free"], 1)
                    if u3 == "A":
                        dve.wait_ge(S["o_sq"], h8 + (n3 + 1))
                        dve.tensor_scalar(ms_o, ss_o, sq_scale[:, i3 % 2:i3 % 2 + 1], EPS, ALU.mult, ALU.add).then_inc(S["o_ms"], 1)
                    if u2 == "A":
                        L = (i2 + 1) * 128
                        dve.wait_ge(S["rowsum_inv"], h8 * 4 + (4 * n2 + 4))
                        dve.scalar_tensor_tensor(probs[:, 0, 0:L], probs[:, 1, 0:L], map2_scale, probs[:, 0, 0:L],
                                                 ALU.mult, ALU.subtract).then_inc(S["probs_done"], 1)
                    if u3 == "A":
                        dve.wait_ge(S["o_rstd"], h8 + (n3 + 1))
                        dve.tensor_scalar(oN[:], OB[:, 0:128], rstd_o, o_scale[:, i3 % 2:i3 % 2 + 1], ALU.mult, ALU.mult).then_inc(S["oN_done"], 1)
                    if u0 == "A":
                        dve.wait_ge(S["sqA_done"], h8 + (n0 + 1))
                        dve.tensor_reduce(ss_qk, sqA[:].rearrange("p (g d) -> p g d", g=4), AX_X, ALU.add).then_inc(S["ssA_done"], 1)
                        dve.wait_ge(S["ssA_done"], h8 + (n0 + 1) + FREE)
                        dve.tensor_scalar(ms_qk, ss_qk, 1.0 / 64, EPS, ALU.mult, ALU.add).then_inc(S["msA_done"], 1)
                    if u1 == "A":
                        L = (i1 + 1) * 128
                        dve.wait_ge(S["scored"], h8 + (n1 + 1))
                        dve.tensor_tensor(SC[:, :, L - 128:L], SC[:, :, L - 128:L],
                                          const("causal").unsqueeze(1).to_broadcast([P, 2, 128]), ALU.add).then_inc(S["masked"], 1)
                        dve.wait_ge(S["masked"], h8 + (n1 + 1))
                        dve.tensor_reduce(rowmax, SC[:, :, 0:L], AX_X, ALU.max).then_inc(S["maxed"], 1)
                        dve.wait_ge(S["maxed"], h8 + (n1 + 1))
                        dve.tensor_scalar(negmax, rowmax, -0.125, None, ALU.mult).then_inc(S["negged"], 1)
                    if u1 == "B":
                        dve.wait_ge(S["st_done"], h8 + (n1 + 1))
                        dve.scalar_tensor_tensor(sT[:, i1 % 2, :], bank(0)[:, 0:128], head_c[:, 3:4], const("tri"), ALU.mult, ALU.mult
                                                 ).then_inc(S["sT_done"], 1)
                    if u0 == "B":
                        cos = cos_t[:, i0, 8:72].unsqueeze(1).to_broadcast([P, 4, 64])
                        dve.wait_ge(S["qkS_done"], h8 * 2 + (2 * n0 + 2) + FREE)
                        dve.tensor_tensor(qkCos[:], qkS[:], cos, ALU.mult).then_inc(S["cosB"], 1)
                    if u2 == "B":
                        dve.wait_ge(S["oB"], h8 + (n2 + 1))
                        dve.bn_stats(bstat[:, 0:6], OB[:, 0:128]).then_inc(S["bn_s"], 1)
                        dve.wait_ge(S["bn_s"], 1)
                        dve.wait_ge(S["bn_s"], h8 + (n2 + 1))
                        dve.bn_aggr(bstat[:, 6:8], bstat[:, 0:6]).then_inc(S["bn_a"], 1)
                        dve.wait_ge(S["bn_a"], h8 + (n2 + 1))
                        dve.tensor_scalar(bstat[:, 8:9], bstat[:, 7:8], EPS, None, ALU.add).then_inc(S["bn_v"], 1)
                    if u1 == "B" and i1 < N_TILES - 1:
                        dve.wait_ge(S["kv_done"], h7 + (n1 + 1))
                        if i1 == 0:
                            dve.tensor_copy(U[:, 1, :], bank(2)[:, 0:128]).then_inc(S["U_done"], 1)
                        else:
                            dve.wait_ge(S["U_done"], h7 + n1 + FREE)
                            dve.scalar_tensor_tensor(U[:, (i1 + 1) % 2, :], U[:, i1 % 2, :], head_c[:, 2:3], bank(2)[:, 0:128],
                                                     ALU.mult, ALU.add).then_inc(S["U_done"], 1)
                    if u2 == "B":
                        dve.wait_ge(S["bn_r"], h8 + (n2 + 1))
                        dve.wait_ge(S["gated"], h8 + n2 + FREE)
                        dve.tensor_scalar(onR[:], OB[:, 0:128], bstat[:, 6:7], bstat[:, 9:10], ALU.subtract, ALU.mult
                                          ).then_inc(S["onR_done"], 1)
                    if u2 == "A" and i2 >= 4:
                        dve.wait_ge(S["aT2"], h * 4 + (i2 - 3))
                        dve.tensor_copy(aT[:, 4:i2 + 1, :].rearrange("p a b -> p (a b)"), TB[:, 0:(i2 - 3) * 128]
                                        ).then_inc(S["t_free"], 1)
                    if u0 == "A":
                        dve.wait_ge(S["rstdA_done"], h8 + (n0 + 1))
                        dve.wait_ge(S["vA_done"], h8 + (n0 + 1))
                        dve.wait_ge(S["qkTA"], h8 + n0 + FREE)
                        for g in range(4):
                            last = dve.scalar_tensor_tensor(qkA[:, g * 64:(g + 1) * 64], src_bank[:, g * 64:(g + 1) * 64],
                                                            rstd_qk[:, g:g + 1], gains[:, g // 2, :], ALU.mult, ALU.mult)
                        last.then_inc(S["normA_done"], 1)
                        if steps[0] == 0:
                            dve.wait_ge(S["trig_done"], 2)
                        dve.wait_ge(S["normA_done"], h8 + (n0 + 1))
                        x4 = qkA[:].rearrange("p (g d) -> p g d", g=4)[:, :, 0:16].rearrange("p g (a b) -> p g a b", a=2)
                        cos = cos_t[:, i0, 0:8].unsqueeze(1).unsqueeze(1).to_broadcast([P, 4, 2, 8])
                        sin = sin_t[:, i0, 0:8].unsqueeze(1).to_broadcast([P, 4, 8])
                        dve.wait_ge(S["ropedA"], h8 * 2 + 2 * n0 + FREE)
                        dve.tensor_tensor(rope_cos[:], x4, cos, ALU.mult).then_inc(S["ropeA_step"], 1)
                        dve.tensor_tensor(rope_sin[:, :, 0, :], x4[:, :, 1, :], sin, ALU.mult).then_inc(S["ropeA_step"], 1)
                        dve.tensor_tensor(rope_sin[:, :, 1, :], x4[:, :, 0, :], sin, ALU.mult).then_inc(S["ropeA_step"], 1)
                        dve.wait_ge(S["ropeA_step"], h24 + (3 * n0 + 3))
                        dve.tensor_tensor(x4[:, :, 0, :], rope_cos[:, :, 0, :], rope_sin[:, :, 0, :], ALU.subtract).then_inc(S["ropedA"], 1)
                        dve.tensor_tensor(x4[:, :, 1, :], rope_cos[:, :, 1, :], rope_sin[:, :, 1, :], ALU.add).then_inc(S["ropedA"], 1)
                    if u0 == "B":
                        dve.wait_ge(S["cosB"], h8 + (n0 + 1))
                        dve.wait_ge(S["sinB"], h8 * 2 + (2 * n0 + 2))
                        if i0:
                            dve.wait_ge(S["kv_done"], h7 + n0)
                        dve.tensor_tensor(qkR[:, 0:4:2, :], qkCos[:, 0:4:2, :], qkSin[:, 0:4:2, :], ALU.subtract).then_inc(S["ropedB"], 1)
                        dve.tensor_tensor(qkR[:, 1:4:2, :], qkCos[:, 1:4:2, :], qkSin[:, 1:4:2, :], ALU.add).then_inc(S["ropedB"], 1)
                    if u0 == "B" and not more:
                        if s % 8 in PREP_C:
                            low_C(PREP_C[s % 8] + 1, 0, PREP_C[s % 8])
                    elif s % 8 in PREP and u0 is not None:
                        split_weights(s)
                    if u0 == "B":
                        dve.wait_ge(S["eg_done"], h8 + (n0 + 1) + FREE)
                        dve.tensor_scalar(eg[:], eg[:], 1.0, None, ALU.add).then_inc(S["eg1"], 1)
                        dve.wait_ge(S["eg1"], h8 + (n0 + 1))
                        dve.reciprocal(eg[:], eg[:]).then_inc(S["egr"], 1)
                    if u1 == "A":
                        dve.wait_ge(S["exped"], h8 * 2 + (2 * n1 + 2) + FREE)
                        b = slice(i1 % 2, i1 % 2 + 1)
                        dve.reciprocal(rrow, rowsum).then_inc(S["rowsum_inv"], 1)
                        dve.wait_ge(S["rowsum_inv"], h8 * 4 + (4 * n1 + 1))
                        dve.scalar_tensor_tensor(map2_scale, rrow[:, 1:2], lam, rowsum[:, 0:1], ALU.mult, ALU.mult
                                                 ).then_inc(S["rowsum_inv"], 1)
                        dve.tensor_scalar(o_scale[:, b], rrow[:, 0:1], -1.0, None, ALU.mult).then_inc(S["rowsum_inv"], 1)
                        dve.scalar_tensor_tensor(sq_scale[:, b], rrow[:, 0:1], 1.0 / 128, rrow[:, 0:1], ALU.mult, ALU.mult
                                                 ).then_inc(S["rowsum_inv"], 1)

            for half in range(2):
                for pair in (2 * half, 2 * half + 1):
                    for i in (2 * pair, 2 * pair + 1):
                        dve.wait_ge(S["x_sq_done"], i + 1)
                        dve.tensor_scalar(x_ms[:, i:i + 1], x_ss[:, i:i + 1], 1.0 / 1024, EPS, ALU.mult, ALU.add
                                          ).then_inc(S["x_ms_done"], 1)
                    for i in (2 * pair, 2 * pair + 1):
                        dve.wait_ge(S["x_rstd_done"], i + 1)
                        dve.tensor_scalar(x_all[:, i, :], x_all[:, i, :], x_rstd[:, i:i + 1], None, ALU.mult
                                          ).then_inc(S["xn_done"], 1)
                if half == 1:
                    dve.wait_ge(S["small_in"], 7 * DMA)
                    head_steps(0, FILL[:1])
                for n in range(8 * half, 8 * half + 8):
                    dve.wait_ge(S["hH_done"], n + 1)
                    dst = (slice(None), n % 8, slice(half * 512, (half + 1) * 512))
                    dve.scalar_tensor_tensor(hTL[dst], bank(n % 4), g1_cols[:, n % 8:n % 8 + 1], hTH[dst].bitcast(F32),
                                             ALU.mult, ALU.subtract).then_inc(S["hL_done"], 1)
                if half == 0:
                    for k in range(8):
                        low(wAL[:, k, :], wA_in[:, k, :], wAH[:, k, :], S["wA_high"], k + 1, S["wA_low"])
                    dve.wait_ge(S["ang_step"], 10)
                    dve.tensor_scalar(ang[:], ang[:], PI_BELOW, -PI_BELOW, ALU.min, ALU.max).then_inc(S["ang_step"], 1)
                    dve.wait_ge(S["ang_step"], 11)
                    dve.scalar_tensor_tensor(turns[:], ang[:], -1.0, ang[:], ALU.mult, ALU.max).then_inc(S["angle_done"], 1)
            dve.tensor_tensor(lam_prod[:], lam_rows[:, 0:4:2, :], lam_rows[:, 1:4:2, :], ALU.mult).then_inc(S["lam_step"], 1)
            dve.wait_ge(S["lam_step"], 1)
            dve.tensor_reduce(lam_s, lam_prod[:], AX_X, ALU.add).then_inc(S["lam_step"], 1)
            dve.wait_ge(S["lam_expd"], 1)
            dve.scalar_tensor_tensor(lam, lam_e[:, 0:1], LAM_INIT, lam_e[:, 1:2], ALU.add, ALU.subtract).then_inc(S["lam_step"], 1)
            dve.tensor_scalar(subln_scaled, subln_col, 1.0 - LAM_INIT, None, ALU.mult).then_inc(S["lam_step"], 1)

            head_steps(0, FILL[1:])
            with dve.Fori(0, N_HEADS - 1) as h:
                head_steps(h, ROUND)
            head_steps(N_HEADS - 1, ROUND, more=False)

            dve.wait_ge(S["gated"], 8 * N_HEADS + FREE)

            def merge_pair(j, last):
                j4, j8 = (j * 4, j * 8) if isinstance(j, int) else (dve.snap(j * 4), dve.snap(j * 8))
                for sub in range(2):
                    for th in range(2):
                        n = 2 * sub + th
                        b0 = 4 if th == 0 else 0
                        dve.wait_ge(S["sig_exp"], j8 + (2 * n + 2))
                        dve.tensor_scalar(sig[:], sig[:], 1.0, None, ALU.add).then_inc(S["sig_one"], 1)
                        dve.wait_ge(S["sig_one"], j4 + (n + 1))
                        dve.reciprocal(sig[:], sig[:]).then_inc(S["sig_inv"], 1)
                        dve.wait_ge(S["sig_inv"], j4 + (n + 1))
                        dve.wait_ge(S["ys_done"], j4 + (n + 1))
                        for g in range(2):
                            dve.tensor_tensor(sig[:, g, :], sig[:, g, :], bank(b0 + 2 + g), ALU.mult).then_inc(S["merged_step"], 1)
                        dve.wait_ge(S["merged_step"], j8 + (2 * n + 2))
                        m = 2 * j + sub
                        dve.tensor_tensor(merged[:, DS(m, 1), th * 512:(th + 1) * 512].rearrange("p a b -> p (a b)"),
                                          sig[:, 0, :], sig[:, 1, :], ALU.add).then_inc(S["sig_mul"], 2)
                        for piece in range(2):
                            r = slice(piece * 4, piece * 4 + 4)
                            if n == 0:
                                low_C(j4 + (3 + piece), 1, piece)
                            if n == 2 and not last:
                                low_C(j4 + (5 + piece), 0, piece)
                            if n == 2 and last:
                                low(wDL[0][:, r, :], wD_in[0][:, r, :], wDH[0][piece][:], S["wD_high"], piece + 1, S["wD_low"])
                        if n == 2 and last:
                            for i in range(4):
                                low_merged(i)

            def low_merged(i):
                dve.wait_ge(S["mH"], i + 1)
                tok = slice(i * 128, i * 128 + 128)
                dve.tensor_tensor(mergedL[:, :, tok], merged[:, :, tok], mergedH[:, :, tok].bitcast(F32), ALU.subtract
                                  ).then_inc(S["mL"], 1)

            with dve.Fori(0, 3) as j:
                merge_pair(j, False)
            merge_pair(3, True)

            def add_residual(n, i):
                cnt = 8 * n + i
                cols = slice(n * 512, n * 512 + 512)
                if n == 0 and i % 2 == 0:
                    dve.wait_ge(S[f"x_in{i // 2}"], 2 * DMA)
                dve.wait_ge(S["d_done"], cnt + 1)
                dve.tensor_tensor(x2[:, i, cols], bank(4 + cnt % 3), x2[:, i, cols], ALU.add).then_inc(S["x2_done"], 1)

            for i in range(4, N_TILES):
                add_residual(0, i - 4)
                low_merged(i)
            add_residual(0, 4)
            add_residual(0, 5)
            for piece in range(2):
                r = slice(piece * 4, piece * 4 + 4)
                low(wDL[1][:, r, :], wD_in[1][:, r, :], wDH[1][piece][:], S["wD_high"], piece + 3, S["wD_low"])
            add_residual(0, 6)
            add_residual(0, 7)

            dve.wait_ge(S["g2_in"], DMA)
            dve.wait_ge(S["router_in"], 4 * DMA)
            for i in range(N_TILES + 2):
                if i < N_TILES:
                    add_residual(1, i)
                    dve.wait_ge(S["n2_sq"], i + 1)
                    dve.tensor_scalar(stats2[:, 1, i:i + 1], stats2[:, 0, i:i + 1], 1.0 / 1024, EPS, ALU.mult, ALU.add
                                      ).then_inc(S["n2_ms"], 1)
                    dve.wait_ge(S["n2_rstd"], i + 1)
                    if i >= 2:
                        dve.wait_ge(S[f"h2_stored{i % 2}"], DMA * (i // 2))
                        dve.wait_ge(S["h2T_done"], i - 1)
                    dve.scalar_tensor_tensor(h2[:, i % 2, :], x2[:, i, :], stats2[:, 2, i:i + 1], g2_row[:], ALU.mult, ALU.mult
                                             ).then_inc(S["h2_done"], 1)
                if i >= 2:
                    dve.wait_ge(S["lg_done"], i - 1)
                    dve.tensor_tensor(logits[:, i - 2, :], OB[:, 0:36], br[:], ALU.add).then_inc(S["logit_done"], 1)

            steps = [0]

            def rstep(ins):
                steps[0] += 1
                ins.then_inc(S["rstep"], 1)
                dve.wait_ge(S["rstep"], steps[0])

            iota8 = const("iota_exp8").unsqueeze(1).to_broadcast([P, 8, 8])
            iota4 = const("iota_grp").unsqueeze(1).to_broadcast([P, 8, 4])
            dve.wait_ge(S["logit_done"], 8)
            gl = logits[:, :, 0:4]
            rstep(dve.tensor_reduce(gmax[:], gl, AX_X, ALU.max))
            rstep(dve.tensor_tensor(gdiff[:], gl, gmax[:].unsqueeze(2).to_broadcast([P, 8, 4]), ALU.subtract))
            assert steps[0] == R_GDIFF
            rstep(dve.tensor_scalar(gpen[:], gdiff[:], 0.0, 8.0, ALU.is_lt, ALU.mult))
            rstep(dve.tensor_tensor(gpen[:], gpen[:], iota4, ALU.add))
            rstep(dve.tensor_reduce(gidx[:], gpen[:], AX_X, ALU.min))
            rstep(dve.tensor_tensor(goh[:], gidx[:].unsqueeze(2).to_broadcast([P, 8, 4]), iota4, ALU.is_equal))
            rstep(dve.tensor_tensor(elsel[:], logits[:, :, 4:36].rearrange("p t (g e) -> p t g e", g=4),
                                    goh[:].unsqueeze(3).to_broadcast([P, 8, 4, 8]), ALU.mult))
            rstep(dve.tensor_reduce(el8[:], elsel[:].rearrange("p t g e -> p t e g"), AX_X, ALU.add))

            def best(values, c):
                rstep(dve.tensor_reduce(vtop[:, c, :], values[:], AX_X, ALU.max))
                rstep(dve.tensor_tensor(epen[:], values[:], vtop[:, c, :].unsqueeze(2).to_broadcast([P, 8, 8]), ALU.is_lt))
                rstep(dve.scalar_tensor_tensor(epen[:], epen[:], 16.0, iota8, ALU.mult, ALU.add))
                rstep(dve.tensor_reduce(eidx[:, c, :], epen[:], AX_X, ALU.min))

            best(el8, 0)
            rstep(dve.tensor_tensor(eoh[:], eidx[:, 0, :].unsqueeze(2).to_broadcast([P, 8, 8]), iota8, ALU.is_equal))
            rstep(dve.scalar_tensor_tensor(el8b[:], eoh[:], BIG_NEG, el8[:], ALU.mult, ALU.add))
            best(el8b, 1)
            rstep(dve.tensor_tensor(vdiff[:], vtop[:, 1, :], vtop[:, 0, :], ALU.subtract))
            assert steps[0] == R_VDIFF, steps[0]
            for c in range(2):
                rstep(dve.scalar_tensor_tensor(eglob[:, c, :], gidx[:], 8.0, eidx[:, c, :], ALU.mult, ALU.add))
            for c in range(2):
                rstep(dve.tensor_tensor(oh[:, c, :, :], eglob[:, c, :].unsqueeze(2).to_broadcast([P, 8, 32]),
                                        const("iota", 0, 32).unsqueeze(1).to_broadcast([P, 8, 32]), ALU.is_equal))
            rstep(dve.tensor_tensor(mask[:], oh[:, 0, :, :], oh[:, 1, :, :], ALU.add))
            rstep(dve.tensor_scalar(before[:, 0, :], mask[:, 0, :].bitcast(F32), 0.0, None, ALU.mult))
            for i in range(8):
                rstep(dve.tensor_tensor(before[:, i + 1, :], before[:, i, :].bitcast(F32), mask[:, i, :].bitcast(F32), ALU.add))
            assert steps[0] == R_BEFORE, steps[0]
            dve.wait_ge(S["ract"], 3)
            rstep(dve.tensor_reduce(gsum[:], gexp[:], AX_X, ALU.add))
            rstep(dve.reciprocal(pgrp[:], gsum[:]))
            rstep(dve.tensor_scalar(vden[:], vexp[:], 1.0, None, ALU.add))
            rstep(dve.reciprocal(vden[:], vden[:]))
            rstep(dve.tensor_tensor(wsel[:, 0, :], pgrp[:], vden[:], ALU.mult))
            rstep(dve.tensor_tensor(wsel[:, 1, :], wsel[:, 0, :], vexp[:], ALU.mult))
            dve.wait_ge(S["pmm"], 2)
            for c in range(2):
                rstep(dve.tensor_tensor(posm[:, c, :, :], oh[:, c, :, :],
                                        bank(0)[:, 0:256].rearrange("p (a b) -> p a b", a=8), ALU.mult))
            rstep(dve.tensor_reduce(pos[:].rearrange("p a b -> p (a b)"), posm[:].rearrange("p a b c -> p (a b) c"), AX_X, ALU.add))
            rstep(dve.tensor_copy(pos_i[:], pos[:]))
            rstep(dve.tensor_scalar(slot_i[:], pos_i[:], BLOCK - 1, None, ALU.bitwise_and))
            rstep(dve.tensor_scalar(blk_i[:], pos_i[:], BLOCK_BITS, None, ALU.logical_shift_right))
            rstep(dve.tensor_copy(slotf[:], slot_i[:]))
            rstep(dve.tensor_copy(blkf[:], blk_i[:]))
            rstep(dve.scalar_tensor_tensor(key[:], blkf[:], 32.0, eglob[:], ALU.mult, ALU.add))
            key16 = key[:].rearrange("p a b -> p (a b)").unsqueeze(2)
            rstep(dve.tensor_tensor(keyid1f[:], key16.to_broadcast([P, 16, 32]),
                                    const("iota", 0, 32).unsqueeze(1).to_broadcast([P, 16, 32]), ALU.is_equal))
            rstep(dve.tensor_tensor(keyid1[:], keyid1f[:], const("token1").unsqueeze(2).to_broadcast([P, 16, 32]), ALU.mult))
            for c in range(2):
                dve.tensor_tensor(pick[:, 8 * c:8 * c + 8, :], slotf[:, c, :].unsqueeze(2).to_broadcast([P, 8, 128]),
                                  const("iota", 0, 128).unsqueeze(1).to_broadcast([P, 8, 128]), ALU.is_equal
                                  ).then_inc(S["pick_done"], 1)
            rstep(dve.tensor_copy(counts_f[:, 0:32], bank(1)[:, 0:32]))
            rstep(dve.tensor_reduce(counts_f[:, 32:33], counts_f[:, 0:32], AX_X, ALU.max))
            rstep(dve.tensor_copy(counts_i[:], counts_f[:]))

            def row_ids(n_keys):
                rstep(dve.tensor_scalar(padded[:, 0:n_keys], bank(2)[:, 0:n_keys], 0.0, 4096.0, ALU.is_equal, ALU.mult))
                rstep(dve.scalar_tensor_tensor(zf[:, 0:n_keys], bank(2)[:, 0:n_keys], -1.0, padded[:, 0:n_keys], ALU.add, ALU.add))
                rstep(dve.tensor_copy(ids_scatter[:, 0:n_keys], zf[:, 0:n_keys]))
                dve.tensor_scalar(ids_gather[:, 0:n_keys], ids_scatter[:, 0:n_keys], 3071, None, ALU.bitwise_and
                                  ).then_inc(S["ids_done"], 1)

            def low_slot(c, value):
                dve.wait_ge(S["gu_high" if c < 4 else "d_high"], value)
                dve.tensor_tensor(w_low[c][:], w_in6[c][:], w_high[c][:].bitcast(F32), ALU.subtract
                                  ).then_inc(S["gu_low" if c < 4 else "d_low"], 1)

            low_slot(0, 1)
            dve.wait_ge(S["pmm"], 3)
            row_ids(32)

            def all_tables():
                for q in range(16):
                    c, i = q // 8, q % 8
                    if q >= 2:
                        dve.wait_ge(S["pick_used"], q - 1)
                    dve.tensor_scalar(keyid[q % 2][:], const("iota"), key[:, c, i:i + 1], const("token1", q, q + 1),
                                      ALU.is_equal, ALU.mult).then_inc(S["pick_done"], 1)
                dve.wait_ge(S["pick_used"], 16)
                row_ids(32 * MAX_BLOCKS)

            def x_low(value):
                dve.wait_ge(S["xeH_done"], value)
                dve.tensor_tensor(xeL[:].rearrange("p a b -> p (a b)"), SC[:, 0, :],
                                  xeH[:].rearrange("p a b -> p (a b)").bitcast(F32), ALU.subtract).then_inc(S["xeL_done"], 1)

            def hidden(value):
                dve.wait_ge(S["silu_done"], value)
                dve.tensor_tensor(hid[:], silu[:], PROJ[1][:, :], ALU.mult).then_inc(S["hid_done"], 1)

            def hid_low(value):
                dve.wait_ge(S["hidH_done"], value)
                dve.tensor_tensor(hidL[:].rearrange("p a b -> p (a b)"), TB[:, :],
                                  hidH[:].rearrange("p a b -> p (a b)").bitcast(F32), ALU.subtract).then_inc(S["hidL_done"], 1)

            for c in (1, 2):
                low_slot(c, c + 1)
            x_low(1)
            low_slot(3, 4)
            low_slot(4, 1)
            low_slot(5, 2)
            low_slot(0, 5)
            hidden(1)
            x_low(2)
            hid_low(1)
            for c in range(1, 4):
                low_slot(c, 4 + c + 1)

            def expert_step(e, more):
                e4, e2 = times(dve, e, 4), times(dve, e, 2)
                if not isinstance(e, int) or e > 1:
                    low_slot(4, e2 - 1)
                    low_slot(5, e2)
                if more:
                    low_slot(0, e4 + 5)
                hidden(e + 1)
                if more:
                    x_low(e + 2)
                    for c in (1, 2, 3):
                        low_slot(c, e4 + (5 + c))
                else:
                    for c in (0, 1):
                        low_slot(c, e4 + (5 + c))
                hid_low(e + 1)

            expert_step(1, True)
            with dve.Fori(2, N_EXP - 1) as e:
                expert_step(e, True)
            expert_step(N_EXP - 1, False)

            def block_lows(n, e, b):
                for c in range(6):
                    dve.wait_ge(S["v_hi"], n * 6 + (c + 1))
                    dve.tensor_tensor(w_low[c][:], w_in6[c][:], w_high[c][:].bitcast(F32), ALU.subtract).then_inc(S["v_lo"], 1)
                x_low(n + (N_EXP + 1))
                hidden(n + (N_EXP + 1))
                hid_low(n + (N_EXP + 1))

            dve.wait_ge(S["scattered"], DMA * N_EXP)
            overflow(dve, block_lows, all_tables)
            for i in range(N_TILES):
                b = i % 4
                dve.wait_ge(S[f"comb_in{b}"], 2 * DMA * (i // 4 + 1))
                if i >= 4:
                    dve.wait_ge(S[f"out_stored{b}"], DMA * (i // 4))
                dve.scalar_tensor_tensor(res[:, b, :], comb[:, b, 0, :], wsel[:, 0, i:i + 1], x2[:, i, :], ALU.mult, ALU.add
                                         ).then_inc(S["comb_mid"], 1)
                dve.wait_ge(S["comb_mid"], i + 1)
                dve.scalar_tensor_tensor(res[:, b, :], comb[:, b, 1, :], wsel[:, 1, i:i + 1], res[:, b, :], ALU.mult, ALU.add
                                         ).then_inc(S["res_done"], 1)


_INS = ["x", "positions", "norm1_g", "w_in", "q_norm_g", "k_norm_g", "lambda_q1", "lambda_k1", "lambda_q2", "lambda_k2",
        "diff_subln_g", "ret_gn_g", "ret_gn_b", "w_branch_a", "w_branch_b", "w_out", "norm2_g",
        "w_group_router", "b_group_router", "w_expert_router", "b_expert_router", "w_gate", "w_up", "w_down"]


def kernel(**inputs):
    import concourse.bacc as bacc
    from concourse.bass_utils import run_bass_kernel_spmd

    nc = bacc.Bacc("TRN2", target_bir_lowering=False, num_devices=1)
    arrays, tensors = {}, {}
    for name in _INS:
        arrays[f"in_{name}"] = np.ascontiguousarray(inputs[name])
    arrays["in_consts"] = constants()
    for full, a in arrays.items():
        tensors[full[3:]] = nc.dram_tensor(full, a.shape, mybir.dt.from_np(a.dtype), kind="ExternalInput").ap()
    tensors["out"] = nc.dram_tensor("out_0", (1, 1024, 1024), F32, kind="ExternalOutput").ap()
    decoder_layer(nc, tensors)
    r = run_bass_kernel_spmd(nc, [arrays], core_ids=[0])
    return r.results[0]["out_0"]
```
